# Optimizing a Trainium2 kernel written in Bass

```python
import math
import jax, jax.numpy as jnp
from jax import lax
import numpy as np

D_MODEL = 2048
BATCH = 1
SEQ = 256
DEPTH = 1
DEC_BATCH = 8
DEC_SEQ = 8
PAST_LEN = 2048
PAGE_SIZE = 128

A_WIDTH = D_MODEL // 4
A_GROUPS = 4
A_DIM = A_WIDTH // A_GROUPS
CHUNK = 128
B_WIDTH = D_MODEL // 2
B_HEAD_DIM = 64
B_HEADS = B_WIDTH // B_HEAD_DIM
M_WIDTH = D_MODEL // 4
M_HEADS = 4
M_HEAD_DIM = M_WIDTH // M_HEADS
N_MEM = 256
DILATIONS = ((128, 1), (512, 4), (2048, 16))
WINDOW_MAX = 2048
N_BUCKETS = 32
MAX_DISTANCE = 2048
N_GROUPS = 4
EXPERTS_PER_GROUP = 8
N_EXPERTS = N_GROUPS * EXPERTS_PER_GROUP
TOP_K = 2
EXPERT_FF = D_MODEL // 8
IN_COLS = 2 * A_WIDTH + 3 * B_WIDTH + M_WIDTH
EPS = 1e-6

kernel_name = "hybrid_gmlp_dilated_memory_hmoe_step"

def rms_norm(x, g):
    xf = x.astype(jnp.float32)
    y = xf * lax.rsqrt(jnp.mean(xf * xf, axis=-1, keepdims=True) + EPS)
    return (y * g.astype(jnp.float32)).astype(x.dtype)

def t5_bucket(dist):
    max_exact = N_BUCKETS // 2
    d = jnp.maximum(dist, 0)
    df = jnp.maximum(d, 1).astype(jnp.float32)
    large = max_exact + (jnp.log(df / max_exact) / math.log(MAX_DISTANCE / max_exact)
                         * (N_BUCKETS - max_exact)).astype(jnp.int32)
    large = jnp.minimum(large, N_BUCKETS - 1)
    return jnp.where(d < max_exact, d, large)

def mixer_inputs(x, g_mix, w_in, g_av, g_qb, g_kb, g_qm):
    bt, s, _ = x.shape
    z = jnp.einsum("bsd,dc->bsc", rms_norm(x, g_mix), w_in)
    o_b = 2 * A_WIDTH
    o_m = o_b + 3 * B_WIDTH
    uv = jax.nn.gelu(z[..., :o_b], approximate=False)
    u = uv[..., :A_WIDTH].reshape(bt, s, A_GROUPS, A_DIM)
    va = rms_norm(uv[..., A_WIDTH:].reshape(bt, s, A_GROUPS, A_DIM), g_av)
    qkv = z[..., o_b:o_m].reshape(bt, s, 3, B_HEADS, B_HEAD_DIM)
    qb = rms_norm(qkv[:, :, 0], g_qb)
    kb = rms_norm(qkv[:, :, 1], g_kb)
    vb = qkv[:, :, 2]
    qm = rms_norm(z[..., o_m:].reshape(bt, s, M_HEADS, M_HEAD_DIM), g_qm)
    return u, va, qb, kb, vb, qm

def spatial_gate(u, v, w_s, b_s, c):
    bt, s, g, ch = v.shape
    vc = v.reshape(bt, s // c, c, g, ch)
    w = jnp.where(jnp.tril(jnp.ones((c, c), dtype=bool)), w_s[:, :c, :c], 0)
    mixed = jnp.einsum("gts,bnsgc->bntgc", w, vc) + b_s[:, :c].T[None, None, :, :, None]
    return u * mixed.reshape(bt, s, g, ch)

def combine_by_denominator(outs, lses):
    wts = jax.nn.softmax(jnp.stack(lses, axis=0), axis=0)
    return jnp.sum(wts[..., None] * jnp.stack(outs, axis=0), axis=0)

def dilated_attend_prompt(q, k, v, rel_bias):
    dtype = q.dtype
    q, k, v = q.astype(jnp.float32), k.astype(jnp.float32), v.astype(jnp.float32)
    bsz, s, h, dh = q.shape
    scale = B_HEAD_DIM ** -0.5
    outs, lses = [], []
    for window, dil in DILATIONS:
        blk = window // dil
        unit = blk * dil
        sp = -(-s // unit) * unit
        nb = sp // unit

        def to_sub(t):
            t = jnp.pad(t, ((0, 0), (0, sp - s), (0, 0), (0, 0)))
            t = t.reshape(bsz, sp // dil, dil, h, dh).transpose(0, 2, 1, 3, 4)
            return t.reshape(bsz, dil, nb, blk, h, dh)

        def with_prev(t):
            prev = jnp.pad(t, ((0, 0), (0, 0), (1, 0), (0, 0), (0, 0), (0, 0)))[:, :, :nb]
            return jnp.concatenate([prev, t], axis=3)

        qs = to_sub(q)
        kk, vv = with_prev(to_sub(k)), with_prev(to_sub(v))
        qi = jnp.arange(blk)[:, None] + blk
        kj = jnp.arange(2 * blk)[None, :]
        delta = qi - kj
        bias = jnp.transpose(rel_bias[t5_bucket(delta * dil)].astype(jnp.float32), (2, 0, 1))
        mk = jnp.arange(nb)[:, None, None] * blk + kj[None] - blk
        valid = (delta >= 0)[None] & (delta <= blk)[None] & (mk >= 0)
        sc = jnp.einsum("brnqhe,brnkhe->brnhqk", qs, kk) * scale + bias
        sc = jnp.where(valid[None, None, :, None], sc, -jnp.inf)
        m = jnp.max(sc, axis=-1, keepdims=True)
        p = jnp.exp(sc - m)
        l = jnp.sum(p, axis=-1, keepdims=True)
        o = jnp.einsum("brnhqk,brnkhe->brnqhe", p / l, vv)
        lse = (m + jnp.log(l))[..., 0]
        o = o.reshape(bsz, dil, sp // dil, h, dh).transpose(0, 2, 1, 3, 4).reshape(bsz, sp, h, dh)[:, :s]
        lse = lse.transpose(0, 1, 2, 4, 3).reshape(bsz, dil, sp // dil, h).transpose(0, 2, 1, 3)
        outs.append(o)
        lses.append(lse.reshape(bsz, sp, h)[:, :s])
    return combine_by_denominator(outs, lses).astype(dtype)

def dilated_attend_sample(q, k_all, v_all, rel_bias):
    dtype = q.dtype
    q, k_all, v_all = q.astype(jnp.float32), k_all.astype(jnp.float32), v_all.astype(jnp.float32)
    ds = q.shape[1]
    base = k_all.shape[1] - ds
    scale = B_HEAD_DIM ** -0.5
    outs, lses = [], []
    for window, dil in DILATIONS:
        n = jnp.arange(window // dil + 1)
        idx = base + jnp.arange(ds)[:, None] - n[None, :] * dil
        valid = idx >= 0
        idc = jnp.maximum(idx, 0)
        kg = k_all[:, idc]
        vg = v_all[:, idc]
        bias = rel_bias[t5_bucket(n * dil)].astype(jnp.float32).T
        sc = jnp.einsum("bqhe,bqkhe->bhqk", q, kg) * scale + bias[None, :, None, :]
        sc = jnp.where(valid[None, None], sc, -jnp.inf)
        m = jnp.max(sc, axis=-1, keepdims=True)
        p = jnp.exp(sc - m)
        l = jnp.sum(p, axis=-1, keepdims=True)
        outs.append(jnp.einsum("bhqk,bqkhe->bqhe", p / l, vg))
        lses.append(jnp.transpose((m + jnp.log(l))[..., 0], (0, 2, 1)))
    return combine_by_denominator(outs, lses).astype(dtype)

def memory_attend(q, mk, mv):
    dtype = q.dtype
    sc = jnp.einsum("bshe,bmhe->bhsm", q.astype(jnp.float32), mk.astype(jnp.float32)) * (M_HEAD_DIM ** -0.5)
    p = jax.nn.softmax(sc, axis=-1)
    return jnp.einsum("bhsm,bmhe->bshe", p, mv.astype(jnp.float32)).astype(dtype)

def memory_kv(mem, g_mem, w_mem_kv, g_km):
    bt = mem.shape[0]
    kv = jnp.einsum("bmd,dc->bmc", rms_norm(mem, g_mem), w_mem_kv)
    mk = rms_norm(kv[..., :M_WIDTH].reshape(bt, N_MEM, M_HEADS, M_HEAD_DIM), g_km)
    mv = kv[..., M_WIDTH:].reshape(bt, N_MEM, M_HEADS, M_HEAD_DIM)
    return mk, mv

def hier_moe(n, w_rg, w_re, w_gate, w_up, w_down):
    bt, s, d = n.shape
    t = n.reshape(bt * s, d)
    g_logits = jnp.einsum("nd,dg->ng", t, w_rg).astype(jnp.float32)
    grp = jnp.argmax(g_logits, axis=-1)
    e_logits = jnp.einsum("nd,gde->nge", t, w_re).astype(jnp.float32)
    e_sel = jnp.take_along_axis(e_logits, grp[:, None, None], axis=1)[:, 0]
    top_v, top_i = lax.top_k(e_sel, TOP_K)
    top_w = jax.nn.softmax(top_v, axis=-1)
    expert_id = grp[:, None] * EXPERTS_PER_GROUP + top_i
    gates = jnp.sum(jax.nn.one_hot(expert_id, N_EXPERTS, dtype=jnp.float32) * top_w[..., None], axis=1)
    hg = jnp.einsum("nd,edf->nef", t, w_gate)
    hu = jnp.einsum("nd,edf->nef", t, w_up)
    act = jax.nn.silu(hg) * hu * gates[..., None].astype(t.dtype)
    return jnp.einsum("nef,efd->nd", act, w_down).reshape(bt, s, d)

def mixer_output_and_ffn(x, ya, yb, ym, w_out, g_ffn, w_rg, w_re, w_gate, w_up, w_down):
    bt, s, _ = x.shape
    mixed = jnp.concatenate([ya.reshape(bt, s, A_WIDTH), yb.reshape(bt, s, B_WIDTH),
                             ym.reshape(bt, s, M_WIDTH)], axis=-1)
    h = x + jnp.einsum("bsc,cd->bsd", mixed, w_out)
    return h + hier_moe(rms_norm(h, g_ffn), w_rg, w_re, w_gate, w_up, w_down)

def setup_inputs(seed: int = 0) -> dict:
    key = jax.random.key(seed)
    ks = jax.random.split(key, 32)
    f32 = jnp.float32

    def nrm(k, shape, scale=1.0):
        return jax.random.normal(k, shape, f32) * scale

    def gain(k, shape):
        return 1.0 + 0.01 * jax.random.normal(k, shape, f32)

    wb = min(WINDOW_MAX, PAST_LEN)
    dsc = D_MODEL ** -0.5
    return {
        "x_prompt": nrm(ks[0], (BATCH, SEQ, D_MODEL)),
        "x_sample": nrm(ks[1], (DEC_BATCH, DEC_SEQ, D_MODEL)),
        "mem_prompt": nrm(ks[2], (BATCH, N_MEM, D_MODEL)),
        "cache_win_k": nrm(ks[3], (DEPTH, DEC_BATCH, wb, B_HEADS, B_HEAD_DIM)),
        "cache_win_v": nrm(ks[4], (DEPTH, DEC_BATCH, wb, B_HEADS, B_HEAD_DIM)),
        "cache_mem_k": nrm(ks[5], (DEPTH, DEC_BATCH, N_MEM, M_HEADS, M_HEAD_DIM)),
        "cache_mem_v": nrm(ks[6], (DEPTH, DEC_BATCH, N_MEM, M_HEADS, M_HEAD_DIM)),
        "rel_bias": nrm(ks[7], (N_BUCKETS, B_HEADS), 0.2),
        "g_mix": gain(ks[8], (DEPTH, D_MODEL)),
        "w_in": nrm(ks[9], (DEPTH, D_MODEL, IN_COLS), dsc),
        "g_av": gain(ks[10], (DEPTH, A_GROUPS, A_DIM)),
        "w_s": nrm(ks[11], (DEPTH, A_GROUPS, CHUNK, CHUNK), CHUNK ** -0.5),
        "b_s": nrm(ks[12], (DEPTH, A_GROUPS, CHUNK), 0.1),
        "g_qb": gain(ks[13], (DEPTH, B_HEAD_DIM)),
        "g_kb": gain(ks[14], (DEPTH, B_HEAD_DIM)),
        "g_qm": gain(ks[15], (DEPTH, M_HEAD_DIM)),
        "g_km": gain(ks[16], (DEPTH, M_HEAD_DIM)),
        "g_mem": gain(ks[17], (DEPTH, D_MODEL)),
        "w_mem_kv": nrm(ks[18], (DEPTH, D_MODEL, 2 * M_WIDTH), dsc),
        "w_out": nrm(ks[19], (DEPTH, D_MODEL, D_MODEL), dsc),
        "g_ffn": gain(ks[20], (DEPTH, D_MODEL)),
        "w_router_group": nrm(ks[21], (DEPTH, D_MODEL, N_GROUPS), dsc),
        "w_router_expert": nrm(ks[22], (DEPTH, N_GROUPS, D_MODEL, EXPERTS_PER_GROUP), dsc),
        "w_gate": nrm(ks[23], (DEPTH, N_EXPERTS, D_MODEL, EXPERT_FF), dsc),
        "w_up": nrm(ks[24], (DEPTH, N_EXPERTS, D_MODEL, EXPERT_FF), dsc),
        "w_down": nrm(ks[25], (DEPTH, N_EXPERTS, EXPERT_FF, D_MODEL), EXPERT_FF ** -0.5),
    }

def reference(x_prompt, x_sample, mem_prompt, cache_win_k, cache_win_v, cache_mem_k, cache_mem_v,
              rel_bias, g_mix, w_in, g_av, w_s, b_s, g_qb, g_kb, g_qm, g_km, g_mem, w_mem_kv, w_out,
              g_ffn, w_router_group, w_router_expert, w_gate, w_up, w_down):
    xp, xs = x_prompt, x_sample
    s = xp.shape[1]
    ds = xs.shape[1]
    wp = min(WINDOW_MAX, s)
    pk, pv, pc, pmk, pmv, sk, sv, sc_ = [], [], [], [], [], [], [], []
    for l in range(DEPTH):
        u, va, qb, kb, vb, qm = mixer_inputs(xp, g_mix[l], w_in[l], g_av[l], g_qb[l], g_kb[l], g_qm[l])
        ya = spatial_gate(u, va, w_s[l], b_s[l], CHUNK)
        yb = dilated_attend_prompt(qb, kb, vb, rel_bias)
        mk, mv = memory_kv(mem_prompt, g_mem[l], w_mem_kv[l], g_km[l])
        ym = memory_attend(qm, mk, mv)
        xp = mixer_output_and_ffn(xp, ya, yb, ym, w_out[l], g_ffn[l], w_router_group[l],
                                  w_router_expert[l], w_gate[l], w_up[l], w_down[l])
        pk.append(kb[:, s - wp:])
        pv.append(vb[:, s - wp:])
        pc.append(va[:, s - CHUNK:])
        pmk.append(mk)
        pmv.append(mv)
        u, va, qb, kb, vb, qm = mixer_inputs(xs, g_mix[l], w_in[l], g_av[l], g_qb[l], g_kb[l], g_qm[l])
        ya = spatial_gate(u, va, w_s[l], b_s[l], ds)
        k_all = jnp.concatenate([cache_win_k[l].astype(kb.dtype), kb], axis=1)
        v_all = jnp.concatenate([cache_win_v[l].astype(vb.dtype), vb], axis=1)
        yb = dilated_attend_sample(qb, k_all, v_all, rel_bias)
        ym = memory_attend(qm, cache_mem_k[l], cache_mem_v[l])
        xs = mixer_output_and_ffn(xs, ya, yb, ym, w_out[l], g_ffn[l], w_router_group[l],
                                  w_router_expert[l], w_gate[l], w_up[l], w_down[l])
        sk.append(kb)
        sv.append(vb)
        sc_.append(va)
    win_k_prompt = jnp.stack(pk, axis=0)
    win_v_prompt = jnp.stack(pv, axis=0)
    chunk_v_prompt = jnp.stack(pc, axis=0)
    mem_k_prompt = jnp.stack(pmk, axis=0)
    mem_v_prompt = jnp.stack(pmv, axis=0)
    win_k_sample = jnp.stack(sk, axis=0)
    win_v_sample = jnp.stack(sv, axis=0)
    chunk_v_sample = jnp.stack(sc_, axis=0)
    return (xp, xs, win_k_prompt, win_v_prompt, chunk_v_prompt, mem_k_prompt, mem_v_prompt,
            win_k_sample, win_v_sample, chunk_v_sample)


_drawn_inputs = setup_inputs


def setup_inputs(seed=0):
    import zlib

    import numpy as np

    out = dict(_drawn_inputs(seed))
    spreads = {}
    factors = {'g_mix': 3.21,
     'g_av': 4.063,
     'g_qb': 8.0,
     'g_kb': 5.852,
     'g_qm': 8.0,
     'g_km': 5.476,
     'g_mem': 5.628}
    for name, (base, spread) in spreads.items():
        noise = np.random.default_rng([zlib.crc32(name.encode()), seed]).standard_normal(out[name].shape)
        drawn = base * np.exp(spread * noise) if base else spread * noise
        out[name] = __import__('jax').numpy.asarray(drawn.astype(out[name].dtype))
    for name, factor in factors.items():
        out[name] = (out[name] * factor).astype(out[name].dtype)
    return out
```

```python
import math
from contextlib import ExitStack

import numpy as np

import concourse.bass as bass
from concourse import mybir

F32 = mybir.dt.float32
U32 = mybir.dt.uint32
I32 = mybir.dt.int32
ALU = mybir.AluOpType
ACT = mybir.ActivationFunctionType
X = mybir.AxisListType.X
ds = bass.ds

P = 128
D = 2048
KT = D // P
NPROMPT, NBATCH, NQ = 256, 8, 8
NSAMPLE = NBATCH * NQ
NT = NPROMPT + NSAMPLE
ROWS = [(0, 128), (128, 128), (256, 64)]
H, DH = 16, 64
HP = H // 2
G, DG = 4, 128
NMEM = 256
PAST = 2048
EPS = 1e-6
NEG = -1e30
COLS = 512
QTR = 4
K4 = KT // QTR
NCHUNK = 9
C_Q, C_K, C_QM, C_V, C_U, C_VA = 0, 2, 4, 5, 7, 8
KEYS_A, KEYS_B = 512, 768
KEYS = KEYS_A + KEYS_B
VT = KEYS // P
NKEY = KEYS + NSAMPLE
DIST0 = PAST + NQ - 1
TABLE = 2560
NEXP, NGRP, EPG, FF = 32, 4, 8, 256
BLOCK = 64
NBLK = (2 * NT - NEXP) // BLOCK + NEXP + 1
NBLK += NBLK % 2
NTAB = NBLK + 2
S_WIN = DH ** -0.5
S_MEM = DG ** -0.5

CST = {}
_at = 0
for _n, _w in (("ident", 128), ("flip", 128), ("ones", 128), ("ltri", 128), ("iota", 64), ("thr", 8), ("pairs", 12),
               ("gmix", 16), ("gmem", 16), ("bs", 4), ("bss", 4), ("wr", KT * 36), ("wst", 4 * 128), ("wsbd", 4 * 64)):
    CST[_n] = (_at, _w)
    _at += _w
NCST = _at
GV = {"qb": (0, 64), "kb": (64, 64), "qm": (128, 128), "km": (256, 128), "av": (384, 512)}


class Steps:

    def __init__(self, eng, sem):
        self.eng, self.sem, self.base, self.n = eng, sem, 0, 0

    def __call__(self, ins):
        self.n += 1
        ins.then_inc(self.sem, 1)
        self.eng.wait_ge(self.sem, self.base + self.n)


def hybrid_step(nc, x_rows, mem_rows, x_t, mem_t, w_proj, w_o, kc, vc, mkc, mvc, cst_d, gv_d, gffn_d,
                relb_d, onehot_d, w_gu, w_dn, empty_d, o_y, o_k, o_v, o_va, o_mk, o_mv,
                bias_d, n2_d, tab_d, y_d):
    with ExitStack() as ctx:
        def sb(name, shape, dt=F32):
            return ctx.enter_context(nc.sbuf_tensor(name, shape, dt))

        def sem(name):
            return ctx.enter_context(nc.semaphore(name))

        cst = sb("cst", [P, NCST])
        gv = sb("gv", [P, 896])
        stat = sb("stat", [P, 256])
        nhalf = sb("nhalf", [P, 96])
        idx = sb("idx", [P, 24], U32)
        ARENA = 48300
        arena = sb("arena", [P, ARENA])
        ps = ctx.enter_context(nc.psum_tensor("ps", [P, 8, 512], F32))

        def c(name, rows=P):
            a, w = CST[name]
            return cst[0:rows, a:a + w]

        def area(at, *dims):
            n = int(np.prod(dims))
            ap = arena[:, at:at + n]
            if len(dims) == 1:
                return ap
            names = "abcdef"[:len(dims)]
            return ap.rearrange(f"p ({' '.join(names)}) -> p {' '.join(names)}",
                                **{k: v for k, v in zip(names, dims)})

        ident = c("ident")
        wr = c("wr").rearrange("p (k n) -> p k n", k=KT)
        wst = c("wst").rearrange("p (g n) -> p g n", g=G)
        wsbd = c("wsbd").rearrange("p (g n) -> p g n", g=G)
        A_W, A_XT = 0, 8192
        A_Z = A_XT + KT * NT
        A_BP = A_Z + NCHUNK * 3 * COLS
        A_KV = A_BP + H * 256
        A_QT = A_KV + 2048
        A_KT = A_QT + HP * NT
        A_QMT = A_KT + HP * NT
        A_MKT = A_QMT + G * NT
        A_Y = A_MKT + G * NMEM
        A_BS = A_Y + KT * NT
        A_END = A_BS + 2176
        assert A_END <= ARENA, A_END
        wring = area(A_W, QTR, K4, COLS)
        xT = area(A_XT, KT, NT)
        z = area(A_Z, NCHUNK, 3, COLS)
        bias_p = area(A_BP, H, 256)
        mk = area(A_KV, 2, COLS)
        mv = area(A_KV + 1024, 2, COLS)
        qT = area(A_QT, HP, NT)
        kT = area(A_KT, HP, NT)
        qmT = area(A_QMT, G, NT)
        mkT = area(A_MKT, G, NMEM)
        memT = area(A_Y, KT, NMEM)
        yT = area(A_Y, KT, NT)
        bias_s = area(A_BS, 2168)
        xst = area(A_QT, 2, D)
        bias_r = area(A_Z + C_V * 3 * COLS, H, 256)
        onehot = area(A_QT + 2 * D, TABLE)[0:33, :]
        relb = area(A_QT + 2 * D + TABLE, H)[0:33, :]
        table = area(A_BP, TABLE)[0:H, :]
        sc_p = area(A_BS, 2, 512)
        pt_p = area(A_BS + 1024, 2, 512)
        kbuf = area(0, HP * KEYS)
        kA = area(0, HP, 512)
        kB1 = area(4096, HP, 512)
        kB2 = area(8192, HP, 256)
        vbuf = area(HP * KEYS, VT, 1024)
        assert 2 * HP * KEYS <= A_Z + C_V * 3 * COLS
        mkb = area(0, 2, 16, NMEM)
        mvb = area(10240, 2, 4, 2, COLS)
        A_RB = A_Z + C_U * 3 * COLS
        sc_s = area(A_RB, NKEY)
        pt_s = area(A_RB + 1344, 11, P)
        qpad = area(A_RB + 1344 + 1408, HP * 144)
        qmpad = area(A_RB + 3904, 2176)
        p_m = area(A_RB + 6080, 256)
        pt_m = area(A_RB + 6336, 2, P)
        assert 6336 + 256 <= 2 * 3 * COLS + 4096
        A_H = A_RB + 512
        hres = area(A_H, 3, D)
        n2 = area(10240, 3, D)
        n2T = area(16384, KT, NT)
        gff = area(21504, D)
        wgu = area(0, 2, 2, KT, FF)
        wdn = area(16384, 2, 2, D)
        assert 24576 <= A_H and A_H + 3 * D <= A_KV
        A_E = A_H + 3 * D
        xg = area(A_E, D)
        xgT = area(A_E + D, KT, BLOCK)
        E0 = A_E + D + KT * BLOCK
        gu_sb = area(E0, FF)
        sg = area(E0 + 256, 2, BLOCK)
        actT = area(E0 + 384, 2, BLOCK)
        y_sb = area(E0 + 512, 2, 1024)
        eblk_i = area(E0 + 2560, NBLK).bitcast(I32)
        cnt_i = area(E0 + 2624, 8).bitcast(I32)
        idx_all = area(E0 + 2640, 2 * NTAB).bitcast(U32).rearrange("p (n f) -> p n f", f=2)
        R0 = E0 + 2730
        g8 = area(R0, 3, 8)
        el = area(R0 + 24, 3, 32)
        mx = area(R0 + 120, 3, 8)
        mi = area(R0 + 144, 3, 8).bitcast(U32)
        grp = area(R0 + 168, 3, 1)
        goh = area(R0 + 171, 3, 4)
        prod = area(R0 + 183, 3, 4, 8)
        esel = area(R0 + 279, 3, 8)
        top = area(R0 + 303, 3, 8)
        ti = area(R0 + 327, 3, 8).bitcast(U32)
        tif = area(R0 + 351, 3, 2)
        eid = area(R0 + 357, 3, 2)
        moh = area(R0 + 363, 2, 3, 32)
        asum = area(R0 + 555, 3, 32)
        cmp5 = area(R0 + 651, 32, 5)
        nb = area(R0 + 811, 32)
        zer = area(R0 + 843, 32)
        incl = area(R0 + 875, 32)
        base = area(R0 + 907, 32)
        ge4 = area(R0 + 939, 2, 3, 4)
        rankf = area(R0 + 963, 2, 3)
        basef = area(R0 + 969, 2, 3)
        fullf = area(R0 + 975, 2, 3)
        pick = area(R0 + 1035, 3, 32)
        slotf = area(R0 + 1131, 2, 3)
        dd = area(R0 + 1137, 3, 1)
        w1p = area(R0 + 1140, 3, 1)
        wk = area(R0 + 1143, 2, 3, 1)
        cmpb = area(R0 + 1149, NBLK, 32)
        ebf = area(R0 + 1149 + NBLK * 32, NBLK)
        cntf = area(R0 + 1149 + NBLK * 33, 8)
        assert R0 + 1149 + NBLK * 33 + 8 <= ARENA
        yg = area(0, 2, 3, D)
        slot_u = idx[:, 0:6].rearrange("p (k t) -> p k t", k=2)
        pair_u = idx[:, 8:20].rearrange("p (k t f) -> p k t f", k=2, t=3)
        row_cur = idx[0:BLOCK, 20:21]
        dst_cur = idx[:, 21:22]

        s_cst, s_gv, s_relb = sem("s_cst"), sem("s_gv"), sem("s_relb")
        s_xst = [sem(f"s_xst{i}") for i in range(2)]
        s_xt, s_memt = sem("s_xt"), sem("s_memt")
        w_loaded = [sem(f"w_loaded{i}") for i in range(QTR)]
        w_used, gemm_done, z_ready = sem("w_used"), sem("gemm_done"), sem("z_ready")
        dv, ac, po = sem("dv"), sem("ac"), sem("po")
        pe_seen, pool_seen = sem("pe_seen"), sem("pool_seen")
        flip_mm, flip_used = sem("flip_mm"), sem("flip_used")
        dset, xt_scaled, sumsq, ms_ready, rs_ready = sem("dset"), sem("xt_scaled"), sem("sumsq"), sem("ms_ready"), sem("rs_ready")
        tab_mm, tab_cp, tab_out, bp_loaded, bs_loaded = sem("tab_mm"), sem("tab_cp"), sem("tab_out"), sem("bp_loaded"), sem("bs_loaded")
        normed, gelu_done, tr_done, tr_used = sem("normed"), sem("gelu_done"), sem("tr_done"), sem("tr_used")
        st_mem, st_k, st_v, st_va, st_y = (sem(n) for n in ("st_mem", "st_k", "st_v", "st_va", "st_y"))
        sc_read, sy_free, y_free, srec, route_d, route_e = (sem(n) for n in (
            "sc_read", "sy_free", "y_free", "srec", "route_d", "route_e"))
        sc_mm, mx_ready, exp_done, p_ready, pt_mm, pt_ready, pv_mm, y_used = (sem(n) for n in (
            "sc_mm", "mx_ready", "exp_done", "p_ready", "pt_mm", "pt_ready", "pv_mm", "y_used"))
        gate_mm, gated, gate_tr, gate_y = sem("gate_mm"), sem("gated"), sem("gate_tr"), sem("gate_y")
        pad_ready, mem_loaded, msc_mm, mmx, mexp, mp_ready, mpt_mm, mpt_ready, mpv_mm, my_ready = (sem(n) for n in (
            "pad_ready", "mem_loaded", "msc_mm", "mmx", "mexp", "mp_ready", "mpt_mm", "mpt_ready", "mpv_mm", "my_ready"))
        k_loaded = [sem(f"k_loaded{i}") for i in range(3)]
        v_loaded, qpad_ready, s_mm, s_used, smx, sexp, sp_ready, spt_mm, spt_ready, spv_mm, sy_used = (sem(n) for n in (
            "v_loaded", "qpad_ready", "s_mm", "s_used", "smx", "sexp", "sp_ready", "spt_mm", "spt_ready", "spv_mm", "sy_used"))
        wo_loaded = [sem(f"wo_loaded{i}") for i in range(QTR)]
        wo_used, wo_done, x_again, h_ready = sem("wo_used"), sem("wo_done"), sem("x_again"), sem("h_ready")
        n2_ready, n2_tr, n2T_ready, logits, routed, n2_stored, tab_zero, slots_out, idx_in = (sem(n) for n in (
            "n2_ready", "n2_tr", "n2T_ready", "logits", "routed", "n2_stored", "tab_zero", "slots_out", "idx_in"))
        onehots, ranks = sem("onehots"), sem("ranks")
        gu_loaded = [sem(f"gu_loaded{i}") for i in range(2)]
        dn_loaded = [sem(f"dn_loaded{i}") for i in range(2)]
        gathered, xg_tr, xgT_ready, gu_mm, gu_copied, at_mm, silu_done, act_ready, dn_mm, y_ready, y_stored = (sem(n) for n in (
            "gathered", "xg_tr", "xgT_ready", "gu_mm", "gu_copied", "at_mm", "silu_done", "act_ready", "dn_mm", "y_ready", "y_stored"))
        back = [sem(f"back{t}") for t in range(3)]
        final, moe_dv, idx_cp = sem("final"), sem("moe_dv"), sem("idx_cp")

        NORM_X, NORM_MEM = 0, 3
        st_rs = stat[:, 8:16]
        st_n = stat[:, 16:64]
        st_nr = stat[:, 64:112]
        st_m = stat[:, 112:120]
        st_l = stat[:, 120:128]
        st_r = stat[:, 128:136]
        st_h = stat[:, 136:139]
        st_hr = stat[:, 140:143]

        block = ctx.enter_context(nc.Block())

        @block.sync
        def _(sp):
            sp.dma_start(cst[:, :], cst_d).then_inc(s_cst, 16)
            sp.dma_start(memT, mem_t).then_inc(s_memt, 16)
            for q in range(QTR):
                sp.dma_start(wring[:, q], w_proj[0, q]).then_inc(w_loaded[q], 16)
            for n in range(2):
                sp.dma_start(xst[:, n], mem_rows[n * P:(n + 1) * P, :]).then_inc(s_xst[n], 16)
            sp.dma_start(xT, x_t).then_inc(s_xt, 16)
            sp.dma_start(gv[:, :], gv_d.partition_broadcast(P)).then_inc(s_gv, 16)
            for n, (r0, m) in enumerate(ROWS):
                sp.wait_ge(sumsq, n + 1)
                sp.dma_start(xst[0:m, n % 2], x_rows[r0:r0 + m, :]).then_inc(s_xst[n % 2], 16)
            sp.wait_ge(tab_out, 16)
            sp.dma_start(bias_r, bass.AP(tensor=bias_d.tensor, offset=DIST0 - 255, ap=[[1, P], [TABLE, H], [1, 256]])
                         ).then_inc(bp_loaded, 16)

            def next_chunk(ch, before):
                for q in range(QTR):
                    if q < QTR - 1:
                        sp.wait_ge(w_used, (ch - 1) * (QTR - 1) + q + 1)
                    else:
                        sp.wait_ge(gemm_done, before)
                    sp.dma_start(wring[:, q], w_proj[ds(ch, 1), q]).then_inc(w_loaded[q], 16)
            next_chunk(1, 2)
            with sp.Fori(2, NCHUNK + 2) as ch:
                next_chunk(ch, ch * 3 - 2)
            sp.wait_ge(gemm_done, 4 + 3 * NCHUNK)
            sp.dma_start(mkb, mkc).then_inc(mem_loaded, 16)
            sp.wait_ge(tr_done, 24)
            sp.wait_ge(st_k, 48)
            sp.dma_start(mvb, mvc).then_inc(mem_loaded, 16)
            sp.wait_ge(pv_mm, 20)
            sp.wait_ge(dset, 2)
            for q in range(NQ):
                sp.dma_start(bias_s[q:P:NQ, 0:PAST], bias_d[:, DIST0 - PAST - q:DIST0 - q]).then_inc(bs_loaded, 16)
                sp.dma_start(bias_s[q:P:NQ, PAST + 56:PAST + 64], bias_d[:, DIST0 - q:DIST0 - q + NQ]).then_inc(bs_loaded, 16)
            sp.wait_ge(msc_mm, 2)
            sp.wait_ge(mpv_mm, 2)
            for n, (kp, a, b) in enumerate(((kA, 0, 4096), (kB1, 4096, 8192), (kB2, 8192, 10240))):
                sp.dma_start(kp, kc[0, :, a:b]).then_inc(k_loaded[n], 16)
            sp.dma_start(vbuf, vc[0]).then_inc(v_loaded, 16)
            with sp.Fori(1, NBATCH) as b:
                for n, (kp, a, e) in enumerate(((kA, 0, 4096), (kB1, 4096, 8192), (kB2, 8192, 10240))):
                    sp.wait_ge(s_mm, (b - 1) * 3 + n + 1)
                    sp.dma_start(kp, kc[ds(b, 1), :, a:e]).then_inc(k_loaded[n], 16)
                sp.wait_ge(spv_mm, b)
                sp.dma_start(vbuf, vc[ds(b, 1)]).then_inc(v_loaded, 16)
            sp.wait_ge(s_mm, 3 * NBATCH)
            for q in range(QTR):
                sp.dma_start(wring[:, q], w_o[0, q]).then_inc(wo_loaded[q], 16)
            sp.wait_ge(spv_mm, NBATCH)
            sp.wait_ge(st_v, 48)
            for n, (r0, m) in enumerate(ROWS):
                sp.dma_start(hres[0:m, n], x_rows[r0:r0 + m, :]).then_inc(x_again, 16)
            with sp.Fori(1, 4) as ch:
                for q in range(QTR):
                    if q < QTR - 1:
                        sp.wait_ge(wo_used, (ch - 1) * (QTR - 1) + q + 1)
                    else:
                        sp.wait_ge(wo_done, ch * 3)
                    sp.dma_start(wring[:, q], w_o[ds(ch, 1), q]).then_inc(wo_loaded[q], 16)
            sp.dma_start(gff, gffn_d.partition_broadcast(P)).then_inc(x_again, 16)
            for n, (r0, m) in enumerate(ROWS):
                sp.wait_ge(n2_ready, n + 1)
                sp.dma_start(n2_d[r0:r0 + m, :], n2[0:m, n]).then_inc(n2_stored, 16)
            sp.wait_ge(routed, 1)
            sp.wait_ge(n2_stored, 48)
            pairs = sp.value_load(cnt_i[0:1, 0:1], min_val=1, max_val=NBLK // 2)
            for s in range(2):
                e = sp.value_load(eblk_i[0:1, s:s + 1], min_val=0, max_val=NEXP - 1)
                sp.dma_start(wgu[:, s], w_gu[ds(e, 1)]).then_inc(gu_loaded[s], 16)
                sp.dma_start(wdn[:, s], w_dn[ds(e, 1)]).then_inc(dn_loaded[s], 16)
            with sp.Fori(1, pairs) as i:
                for s in range(2):
                    e = sp.value_load(eblk_i[0:1, ds(i * 2 + s, 1)], min_val=0, max_val=NEXP - 1)
                    sp.wait_ge(gu_mm, i * 2 + (s - 1))
                    sp.dma_start(wgu[:, s], w_gu[ds(e, 1)]).then_inc(gu_loaded[s], 16)
                    sp.wait_ge(dn_mm, i * 2 + (s - 1))
                    sp.dma_start(wdn[:, s], w_dn[ds(e, 1)]).then_inc(dn_loaded[s], 16)

        @block.tensor
        def _(pe):
            mm, tr = nc.tensor.matmul, nc.tensor.transpose
            pe.wait_ge(s_relb, 32)
            for n in range(TABLE // 512):
                if n >= 2:
                    pe.wait_ge(tab_cp, n - 1)
                mm(ps[0:H, 6 + n % 2, :], relb[:, :], onehot[:, n * 512:(n + 1) * 512], start=True, stop=True).then_inc(tab_mm, 1)

            def chunk(bank, src, rows, load_value):
                for q in range(QTR):
                    pe.wait_ge(w_loaded[q], load_value)
                    for t, (r0, m) in enumerate(rows):
                        for k in range(K4):
                            kt = q * K4 + k
                            last = mm(ps[0:m, bank + t, :], src[:, kt, r0:r0 + m], wring[:, q, k, :],
                                      start=kt == 0, stop=kt == KT - 1)
                        if q == QTR - 1:
                            last.then_inc(gemm_done, 1)
                    if q < QTR - 1:
                        last.then_inc(w_used, 1)

            pe.wait_ge(xt_scaled, 1)
            for ch in range(2):
                chunk(3 * ch, memT, ROWS[:2], 16 * (ch + 1))
            pe.wait_ge(bp_loaded, 16)
            pe.wait_ge(tab_cp, TABLE // 512)
            for n in range(H // 2):
                if n >= 2:
                    pe.wait_ge(flip_used, n - 1)
                mm(ps[:, 6 + n % 2, :], c("flip"), bias_r[:, 2 * n:2 * n + 2, :], start=True, stop=True).then_inc(flip_mm, 1)
            pe.wait_ge(xt_scaled, 2)
            pe.wait_ge(z_ready, 4)
            with pe.Fori(0, NCHUNK // 2) as i:
                for s in range(2):
                    pe.wait_ge(z_ready, i * 6 + (4 + 3 * (s - 1)))
                    chunk(3 * s, xT, ROWS, i * 32 + 16 * (s + 3))
            pe.wait_ge(z_ready, 4 + 3 * (NCHUNK - 2))
            chunk(0, xT, ROWS, 16 * (NCHUNK + 2))

            def turn(n, src, rows):
                if n >= 2:
                    pe.wait_ge(tr_used, n - 1)
                for t, (r0, m) in enumerate(rows):
                    last = tr(ps[:, 6 + n % 2, r0:r0 + m], src(t)[0:m, :], ident[0:m, 0:m])
                last.then_inc(tr_done, 1)
            pe.wait_ge(flip_used, H // 2)
            n = 0
            pe.wait_ge(normed, 1)
            for g in range(G):
                turn(n, lambda t: mk[:, t, g * DG:(g + 1) * DG], ROWS[:2])
                n += 1
            pe.wait_ge(normed, 4)
            for ch, pairs in ((C_Q, HP), (C_K, HP), (C_QM, G)):
                for hp in range(pairs):
                    turn(n, lambda t: z[:, ch + hp // 4, t, (hp % 4) * P:(hp % 4 + 1) * P], ROWS)
                    n += 1
            pe.wait_ge(tr_used, n)
            pe.wait_ge(z_ready, 4 + 3 * NCHUNK)

            def scores(h):
                if h >= 2:
                    pe.wait_ge(sc_read, h - 1)
                b = h % 2
                if h < H:
                    r = slice(64 * (h % 2), 64 * (h % 2) + 64)
                    mm(ps[:, b, 0:128], qT[r, h // 2, 0:128], kT[r, h // 2, 0:128], start=True, stop=True)
                    mm(ps[:, b, 128:384], qT[r, h // 2, 128:256], kT[r, h // 2, 0:256], start=True, stop=True).then_inc(sc_mm, 1)
                else:
                    g = h - H
                    mm(ps[:, b, 0:256], qmT[:, g, 0:128], mkT[:, g, :], start=True, stop=True)
                    mm(ps[:, b, 256:512], qmT[:, g, 128:256], mkT[:, g, :], start=True, stop=True).then_inc(sc_mm, 1)

            def turn_p(h):
                b = 2 + h % 2
                pe.wait_ge(p_ready, h + 1)
                if h >= 2:
                    pe.wait_ge(pt_ready, h - 1)
                p = sc_p[:, h % 2]
                if h < H:
                    tr(ps[:, b, 0:128], p[:, 0:128], ident)
                    tr(ps[:, b, 128:256], p[:, 128:256], ident)
                    tr(ps[:, b, 256:384], p[:, 256:384], ident).then_inc(pt_mm, 1)
                else:
                    tr(ps[:, b, 0:128], p[:, 0:128], ident)
                    tr(ps[:, b, 128:256], p[:, 256:384], ident)
                    tr(ps[:, b, 256:384], p[:, 128:256], ident)
                    tr(ps[:, b, 384:512], p[:, 384:512], ident).then_inc(pt_mm, 1)

            def values(h):
                pe.wait_ge(pt_ready, h + 1)
                pt = pt_p[:, h % 2]
                if h < H:
                    hp, r = h // 2, slice(64 * (h % 2), 64 * (h % 2) + 64)
                    b = 4 + hp % 2
                    if h % 2 == 0 and hp >= 2:
                        pe.wait_ge(y_used, hp - 1)
                    v = [z[:, C_V + h // 8, t, (h % 8) * DH:(h % 8 + 1) * DH] for t in range(2)]
                    mm(ps[r, b, 0:256], v[0], pt[:, 0:256], start=True, stop=False, skip_group_check=True)
                    mm(ps[r, b, 128:256], v[1], pt[:, 256:384], start=False, stop=True, skip_group_check=True).then_inc(pv_mm, 1)
                else:
                    g = h - H
                    b = 4 + g % 2
                    pe.wait_ge(y_used, HP + g - 1)
                    mm(ps[:, b, 0:256], mv[:, 0, g * DG:(g + 1) * DG], pt[:, 0:256], start=True, stop=False)
                    mm(ps[:, b, 0:256], mv[:, 1, g * DG:(g + 1) * DG], pt[:, 256:512], start=False, stop=True).then_inc(pv_mm, 1)

            for i in range(20 + 2):
                if i < 20:
                    scores(i)
                if 1 <= i <= 20:
                    turn_p(i - 1)
                if i >= 2:
                    values(i - 2)

            pe.wait_ge(y_used, HP + G)
            pe.wait_ge(sc_read, 20)
            pe.wait_ge(normed, 5)
            for g in range(G):
                cols = slice(g * DG, (g + 1) * DG)
                for t in range(2):
                    mm(ps[:, g, t * 128:(t + 1) * 128], wst[:, g, :], z[:, C_VA, t, cols], start=True, stop=True)
                mm(ps[0:64, g, 256:384], wsbd[0:64, g, :], z[0:64, C_VA, 2, cols], start=True, stop=True).then_inc(gate_mm, 1)
            for g in range(G):
                pe.wait_ge(gated, g + 1)
                for t, (r0, m) in enumerate(ROWS):
                    last = tr(ps[:, 4 + g, r0:r0 + m], z[0:m, C_U, t, g * DG:(g + 1) * DG], ident[0:m, 0:m])
                last.then_inc(gate_tr, 1)

            for r in range(2):
                pe.wait_ge(pad_ready, r + 1)
                if r == 0:
                    pe.wait_ge(mem_loaded, 32)
                for i in range(16):
                    last = mm(ps[:, r, 0:256], qmpad[:, i * 128:(i + 1) * 128], mkb[:, r, i, :], start=i == 0, stop=i == 15)
                last.then_inc(msc_mm, 1)
                pe.wait_ge(mp_ready, r + 1)
                for t in range(2):
                    last = tr(ps[:, 2 + r, t * 128:(t + 1) * 128], p_m[:, t * 128:(t + 1) * 128], ident)
                last.then_inc(mpt_mm, 1)
                pe.wait_ge(mpt_ready, r + 1)
                if r == 0:
                    pe.wait_ge(gate_y, G)
                for i in range(16):
                    for t in range(2):
                        last = mm(ps[:, 4 + r, i * 8:(i + 1) * 8], mvb[:, r, i // 4, t, (i % 4) * DG:(i % 4 + 1) * DG],
                                  pt_m[:, t, i * 8:(i + 1) * 8], start=t == 0, stop=t == 1)
                last.then_inc(mpv_mm, 1)
            pe.wait_ge(my_ready, 2)

            def qk(b):
                pe.wait_ge(qpad_ready, b + 1)
                for n, (kp, w) in enumerate(((kA, 512), (kB1, 512), (kB2, 256))):
                    pe.wait_ge(k_loaded[n], b * 16 + 16)
                    if type(b) is not int:
                        pe.wait_ge(s_used, (b - 1) * 3 + n + 1)
                    for half in range(2):
                        for g in range(4):
                            hp = 2 * g + half
                            last = mm(ps[32 * g:32 * g + 32, n, 0:w], qpad[:, hp * 128 + 32 * g:hp * 128 + 32 * g + 32],
                                      kp[:, hp, :], start=half == 0, stop=half == 1)
                    if n == 2:
                        for half in range(2):
                            for g in range(4):
                                hp = 2 * g + half
                                last = mm(ps[32 * g:32 * g + 32, n, w:w + NSAMPLE],
                                          qpad[:, hp * 128 + 32 * g:hp * 128 + 32 * g + 32],
                                          kT[:, hp, NPROMPT:NT], start=half == 0, stop=half == 1)
                    last.then_inc(s_mm, 1)

            def turn_s(b):
                pe.wait_ge(sp_ready, b + 1)
                if type(b) is not int:
                    pe.wait_ge(spt_ready, b * 3)
                for t in range(11):
                    w = 128 if t < VT else NSAMPLE
                    last = tr(ps[0:w, 3 + t // 4, (t % 4) * 128:(t % 4) * 128 + 128], sc_s[:, t * 128:t * 128 + w], ident)
                    if t in (3, 7, 10):
                        last.then_inc(spt_mm, 1)

            def pv(turned, loaded, free):
                pe.wait_ge(spt_ready, turned)
                pe.wait_ge(v_loaded, loaded)
                pe.wait_ge(sy_free, free)
                for hp in range(HP):
                    for t in range(VT):
                        mm(ps[:, 6, hp * 16:hp * 16 + 16], vbuf[:, t, hp * 128:(hp + 1) * 128],
                           pt_s[:, t, hp * 16:hp * 16 + 16], start=t == 0, stop=False)
                    last = mm(ps[:, 6, hp * 16:hp * 16 + 16],
                              z[0:NSAMPLE, C_V + hp // 4, 2, (hp % 4) * 128:(hp % 4 + 1) * 128],
                              pt_s[0:NSAMPLE, VT, hp * 16:hp * 16 + 16], start=False, stop=True)
                last.then_inc(spv_mm, 1)

            qk(0)
            turn_s(0)
            with pe.Fori(1, NBATCH) as b:
                qk(b)
                pv(b * 3, b * 16, b)
                turn_s(b)
            pv(3 * NBATCH, 16 * NBATCH, NBATCH)
            pe.wait_ge(sy_free, NBATCH + 1)

            def out_chunk(bank, load_value):
                for q in range(QTR):
                    pe.wait_ge(wo_loaded[q], load_value)
                    for t, (r0, m) in enumerate(ROWS):
                        for k in range(K4):
                            kt = q * K4 + k
                            last = mm(ps[0:m, bank + t, :], yT[:, kt, r0:r0 + m], wring[:, q, k, :],
                                      start=kt == 0, stop=kt == KT - 1)
                        if q == QTR - 1:
                            last.then_inc(wo_done, 1)
                    if q < QTR - 1:
                        last.then_inc(wo_used, 1)
            out_chunk(0, 16)
            out_chunk(3, 32)
            pe.wait_ge(h_ready, 3)
            out_chunk(0, 48)
            pe.wait_ge(h_ready, 6)
            out_chunk(3, 64)

            pe.wait_ge(h_ready, 12)
            for t, (r0, m) in enumerate(ROWS):
                pe.wait_ge(n2_ready, t + 1)
                for k4 in range(4):
                    j = t * 4 + k4
                    if j >= 2:
                        pe.wait_ge(n2T_ready, j - 1)
                    for k in range(4):
                        kt = k4 * 4 + k
                        last = tr(ps[:, j % 2, k * 128:k * 128 + m], n2[0:m, t, kt * 128:(kt + 1) * 128], ident[0:m, 0:m])
                    last.then_inc(n2_tr, 1)
            pe.wait_ge(n2T_ready, 12)
            for t, (r0, m) in enumerate(ROWS):
                for kt in range(KT):
                    last = mm(ps[0:m, 2, t * 36:(t + 1) * 36], n2T[:, kt, r0:r0 + m], wr[:, kt, :], start=kt == 0, stop=kt == KT - 1)
            last.then_inc(logits, 1)
            pe.wait_ge(onehots, 1)
            for t in range(3):
                mm(ps[:, 3, t * 32:(t + 1) * 32], c("ltri"), asum[:, t, :], start=True, stop=t == 0)
                for u in range(t):
                    mm(ps[:, 3, t * 32:(t + 1) * 32], c("ones"), asum[:, u, :], start=False, stop=u == t - 1)
            for t in range(3):
                last = mm(ps[:, 3, 96:128], c("ones"), asum[:, t, :], start=t == 0, stop=t == 2)
            last.then_inc(ranks, 1)

            def turn_x(value):
                pe.wait_ge(gathered, value)
                pe.sem_inc(pe_seen, 1)
                for kt in range(KT):
                    last = tr(ps[:, 1 + kt // 8, (kt % 8) * 64:(kt % 8) * 64 + 64], xg[0:BLOCK, kt * 128:(kt + 1) * 128],
                              ident[0:BLOCK, 0:BLOCK])
                last.then_inc(xg_tr, 1)

            pe.wait_ge(routed, 1)
            pairs = pe.value_load(cnt_i[0:1, 0:1], min_val=1, max_val=NBLK // 2)
            turn_x(16)
            with pe.Fori(0, pairs) as i:
                for s in range(2):
                    pe.wait_ge(xgT_ready, i * 4 + 2 * (s + 1))
                    pe.wait_ge(gu_loaded[s], i * 16 + 16)
                    for kt in range(KT):
                        for u in range(2):
                            last = mm(ps[64 * u:64 * u + 64, 0, 0:FF], xgT[:, kt, :], wgu[:, s, u, kt, :],
                                      start=kt == 0, stop=kt == KT - 1)
                    last.then_inc(gu_mm, 1)
                    turn_x(i * 32 + 16 * (s + 2))
                    pe.wait_ge(gu_copied, i * 2 + s + 1)
                    for j in range(2):
                        last = tr(ps[:, 3, j * 128:(j + 1) * 128], gu_sb[:, j * 128:(j + 1) * 128], ident)
                    last.then_inc(at_mm, 1)
                    pe.wait_ge(act_ready, i * 2 + s + 1)
                    pe.wait_ge(dn_loaded[s], i * 16 + 16)
                    for j in range(2):
                        for b in range(2):
                            for half in range(2):
                                n = 2 * half + b
                                last = mm(ps[64 * half:64 * half + 64, 4 + 2 * s + b, :], actT[:, j, :],
                                          wdn[:, s, j, n * 512:(n + 1) * 512], start=j == 0, stop=j == 1)
                    last.then_inc(dn_mm, 1)

        @block.scalar
        def _(act):
            copy = nc.scalar.copy
            tiles = [(P, NORM_MEM), (P, NORM_MEM + 1)] + [(m, NORM_X + t) for t, (_, m) in enumerate(ROWS)]
            act.wait_ge(dset, 1)
            for n, (m, col) in enumerate(tiles):
                act.wait_ge(s_xst[n % 2], 16 * (n // 2 + 1))
                nc.scalar.activation(xst[0:m, n % 2], xst[0:m, n % 2], ACT.Square, accum_out=stat[0:m, col:col + 1]).then_inc(sumsq, 1)
            act.wait_ge(rs_ready, 1)
            for ch in range(2):
                for t in range(2):
                    act.wait_ge(gemm_done, ch * 2 + t + 1)
                    nc.scalar.activation((mk, mv)[ch][:, t], ps[:, 3 * ch + t, :], ACT.Copy,
                                         scale=st_rs[:, NORM_MEM + t:NORM_MEM + t + 1]).then_inc(z_ready, 1)

            def out(ch, s, done):
                for t, (_, m) in enumerate(ROWS):
                    act.wait_ge(gemm_done, done + t + 1)
                    nc.scalar.activation(z[0:m, ds(ch, 1), t, :], ps[0:m, 3 * s + t, :], ACT.Copy,
                                         scale=st_rs[0:m, NORM_X + t:NORM_X + t + 1]).then_inc(z_ready, 1)
            with act.Fori(0, NCHUNK // 2) as i:
                for s in range(2):
                    out(i * 2 + s, s, i * 6 + (4 + 3 * s))
            out(NCHUNK - 1, 0, 4 + 3 * (NCHUNK - 1))
            act.wait_ge(z_ready, 4 + 3 * NCHUNK)
            act.wait_ge(po, 2)
            nc.scalar.activation(z[:, C_U:C_VA + 1], z[:, C_U:C_VA + 1], ACT.Gelu).then_inc(gelu_done, 1)
            act.wait_ge(tab_cp, TABLE // 512)
            dst = [(mkT[:, g, :], NMEM) for g in range(G)] + [(qT[:, n, :], NT) for n in range(HP)] \
                + [(kT[:, n, :], NT) for n in range(HP)] + [(qmT[:, g, :], NT) for g in range(G)]
            for n, (d, w) in enumerate(dst):
                act.wait_ge(tr_done, n + 1)
                copy(d, ps[:, 6 + n % 2, 0:w]).then_inc(tr_used, 1)

            for i in range(21):
                if i < 20:
                    act.wait_ge(mx_ready, i + 1)
                    b, w = i % 2, (128 if i < H else 256)
                    m = st_m[:, 2 * b:2 * b + 2]
                    l = st_l[:, 2 * b:2 * b + 2]
                    if i < H:
                        nc.scalar.activation(sc_p[:, b, 0:128], sc_p[:, b, 0:128], ACT.Exp, bias=m[:, 0:1], accum_out=l[:, 0:1])
                        nc.scalar.activation(sc_p[:, b, 128:384], sc_p[:, b, 128:384], ACT.Exp, bias=m[:, 1:2],
                                             accum_out=l[:, 1:2]).then_inc(exp_done, 1)
                    else:
                        nc.scalar.activation(sc_p[:, b, 0:256], sc_p[:, b, 0:256], ACT.Exp, bias=m[:, 0:1], accum_out=l[:, 0:1])
                        nc.scalar.activation(sc_p[:, b, 256:512], sc_p[:, b, 256:512], ACT.Exp, bias=m[:, 1:2],
                                             accum_out=l[:, 1:2]).then_inc(exp_done, 1)
                if i >= 1:
                    h = i - 1
                    w = 384 if h < H else 512
                    act.wait_ge(pt_mm, h + 1)
                    if h >= 2:
                        act.wait_ge(pv_mm, h - 1)
                    copy(pt_p[:, h % 2, 0:w], ps[:, 2 + h % 2, 0:w]).then_inc(pt_ready, 1)
            for g in range(G):
                act.wait_ge(gate_tr, g + 1)
                copy(yT[:, g, :], ps[:, 4 + g, 0:NT]).then_inc(gate_y, 1)
            for r in range(2):
                act.wait_ge(mmx, r + 1)
                nc.scalar.activation(p_m, ps[:, r, 0:256], ACT.Exp, bias=st_m[:, 4:5], scale=S_MEM,
                                     accum_out=st_l[:, 4:5]).then_inc(mexp, 1)
                act.wait_ge(mpt_mm, r + 1)
                copy(pt_m, ps[:, 2 + r, 0:256].rearrange("p (t n) -> p t n", t=2)).then_inc(mpt_ready, 1)
            with act.Fori(0, NBATCH) as b:
                act.wait_ge(smx, b + 1)
                nc.scalar.activation(sc_s, sc_s, ACT.Exp, bias=st_m[:, 5:6], accum_out=st_l[:, 5:6]).then_inc(sexp, 1)
                for n in range(3):
                    act.wait_ge(spt_mm, b * 3 + n + 1)
                    if n < 2:
                        copy(pt_s[:, 4 * n:4 * n + 4], ps[:, 3 + n, :].rearrange("p (t n) -> p t n", t=4)).then_inc(spt_ready, 1)
                    else:
                        copy(pt_s[:, 8:10], ps[:, 5, 0:256].rearrange("p (t n) -> p t n", t=2))
                        copy(pt_s[0:64, 10], ps[0:64, 5, 256:384]).then_inc(spt_ready, 1)
            act.wait_ge(spv_mm, NBATCH)
            for t, (_, m) in enumerate(ROWS):
                act.wait_ge(h_ready, 10 + t)
                nc.scalar.activation(n2[0:m, t], hres[0:m, t], ACT.Square, accum_out=st_h[0:m, t:t + 1]).then_inc(sumsq, 1)
            for j in range(12):
                t, k4 = j // 4, j % 4
                r0, m = ROWS[t]
                act.wait_ge(n2_tr, j + 1)
                copy(n2T[:, 4 * k4:4 * k4 + 4, r0:r0 + m],
                     ps[:, j % 2, :].rearrange("p (k n) -> p k n", k=4)[:, :, 0:m]).then_inc(n2T_ready, 1)
            act.wait_ge(route_d, 1)
            nc.scalar.activation(dd, dd, ACT.Exp).then_inc(route_e, 1)

            act.wait_ge(routed, 1)
            pairs = act.value_load(cnt_i[0:1, 0:1], min_val=1, max_val=NBLK // 2)
            act.wait_ge(xg_tr, 1)
            copy(xgT[:, 8:16], ps[:, 2, :].rearrange("p (k n) -> p k n", k=8)).then_inc(xgT_ready, 1)
            with act.Fori(0, pairs) as i:
                for s in range(2):
                    act.wait_ge(xg_tr, i * 2 + s + 2)
                    copy(xgT[:, 8:16], ps[:, 2, :].rearrange("p (k n) -> p k n", k=8)).then_inc(xgT_ready, 1)
                    act.wait_ge(at_mm, i * 2 + s + 1)
                    nc.scalar.activation(sg, ps[:, 3, 0:256].rearrange("p (j n) -> p j n", j=2)[:, :, 0:BLOCK],
                                         ACT.Silu).then_inc(silu_done, 1)
                    act.wait_ge(dn_mm, i * 2 + s + 1)
                    act.wait_ge(y_free, i * 2 + s + 1)
                    copy(y_sb[:, s, 512:1024], ps[:, 5 + 2 * s, :]).then_inc(y_ready, 1)

        @block.vector
        def _(dve):
            link = Steps(dve, dv)
            V = nc.vector
            V.memset(stat[:, :], 1.0).then_inc(dset, 1)
            dve.wait_ge(s_cst, 16)
            dve.wait_ge(s_memt, 16)
            V.tensor_tensor(memT, memT, c("gmem").unsqueeze(2).to_broadcast([P, KT, NMEM]), ALU.mult).then_inc(xt_scaled, 1)
            for n in range(TABLE // 512):
                dve.wait_ge(tab_mm, n + 1)
                V.tensor_copy(table[:, n * 512:(n + 1) * 512], ps[0:H, 6 + n % 2, :]).then_inc(tab_cp, 1)
            dve.wait_ge(s_xt, 16)
            V.tensor_tensor(xT, xT, c("gmix").unsqueeze(2).to_broadcast([P, KT, NT]), ALU.mult).then_inc(xt_scaled, 1)
            dve.wait_ge(sumsq, 5)
            V.tensor_scalar(stat[:, 0:5], stat[:, 0:5], 1.0 / D, EPS, ALU.mult, ALU.add).then_inc(ms_ready, 1)
            for n in range(H // 2):
                dve.wait_ge(flip_mm, n + 1)
                V.tensor_copy(bias_p[:, 2 * n:2 * n + 2, :], ps[:, 6 + n % 2, :].rearrange("p (h n) -> p h n", h=2)).then_inc(flip_used, 1)

            state = {"n": 1}

            def norm(src, groups, e, gain, scratch, need):
                dve.wait_ge(z_ready, need)
                link(V.tensor_tensor(scratch, src, src, ALU.mult))
                link(V.tensor_reduce(st_n[:, 0:groups], scratch.rearrange("p n (h e) -> p (n h) e", e=e), X, ALU.add))
                V.tensor_scalar(st_n[:, 0:groups], st_n[:, 0:groups], 1.0 / e, EPS, ALU.mult, ALU.add).then_inc(ms_ready, 1)
                state["n"] += 1
                dve.wait_ge(rs_ready, state["n"])
                n = src.shape[1]
                for k in range(n):
                    v = src[:, k].rearrange("p (h e) -> p h e", e=e)
                    hh = COLS // e
                    rb = st_nr[:, k * hh:(k + 1) * hh].unsqueeze(2).to_broadcast([P, hh, e])
                    last = V.tensor_tensor(v, v, rb, ALU.mult)
                link(last)
                for k in range(n):
                    v = src[:, k].rearrange("p (h e) -> p h e", e=e)
                    hh = COLS // e
                    if gain[1] == COLS:
                        gb = gv[:, gain[0]:gain[0] + gain[1]].rearrange("p (h e) -> p h e", e=e)
                    else:
                        gb = gv[:, gain[0]:gain[0] + gain[1]].unsqueeze(1).to_broadcast([P, hh, e])
                    last = V.tensor_tensor(v, v, gb, ALU.mult)
                last.then_inc(normed, 1)

            def flat(ap):
                return ap.rearrange("p a t e -> p (a t) e")

            dve.wait_ge(s_gv, 16)
            dve.wait_ge(po, 2)
            dve.wait_ge(gemm_done, 4)
            norm(mk, 8, DG, GV["km"], area(A_Y, 2, COLS), 4)
            norm(flat(z[:, C_Q:C_Q + 2]), 48, DH, GV["qb"], area(A_Y, 6, COLS), 4 + 3 * 2)
            norm(flat(z[:, C_K:C_K + 2]), 48, DH, GV["kb"], area(A_Y, 6, COLS), 4 + 3 * 4)
            norm(flat(z[:, C_QM:C_QM + 1]), 12, DG, GV["qm"], area(A_Y, 3, COLS), 4 + 3 * 5)
            dve.wait_ge(gelu_done, 1)
            norm(flat(z[:, C_VA:C_VA + 1]), 12, DG, GV["av"], area(A_Y, 3, COLS), 4 + 3 * 9)

            for i in range(23):
                if i < 20:
                    b = i % 2
                    dve.wait_ge(sc_mm, i + 1)
                    w0, w = (128, 384) if i < H else (256, 512)
                    if i < H:
                        V.scalar_tensor_tensor(sc_p[:, b, 0:128], ps[:, b, 0:128], S_WIN, bias_p[:, i, 128:256], ALU.mult, ALU.add)
                        last = V.scalar_tensor_tensor(sc_p[:, b, 128:384], ps[:, b, 128:384], S_WIN, bias_p[:, i, :], ALU.mult, ALU.add)
                    else:
                        last = V.tensor_scalar(sc_p[:, b, :], ps[:, b, :], S_MEM, None, ALU.mult)
                    link(last)
                    dve.sem_inc(sc_read, 1)
                    V.tensor_reduce(st_m[:, 2 * b:2 * b + 1], sc_p[:, b, 0:w0], X, ALU.max, negate=True)
                    V.tensor_reduce(st_m[:, 2 * b + 1:2 * b + 2], sc_p[:, b, w0:w], X, ALU.max, negate=True).then_inc(mx_ready, 1)
                if 1 <= i <= 20:
                    h = i - 1
                    b = h % 2
                    w0, w = (128, 384) if h < H else (256, 512)
                    dve.wait_ge(exp_done, h + 1)
                    link(V.reciprocal(st_r[:, 2 * b:2 * b + 2], st_l[:, 2 * b:2 * b + 2]))
                    V.tensor_scalar(sc_p[:, b, 0:w0], sc_p[:, b, 0:w0], st_r[:, 2 * b:2 * b + 1], None, ALU.mult)
                    V.tensor_scalar(sc_p[:, b, w0:w], sc_p[:, b, w0:w], st_r[:, 2 * b + 1:2 * b + 2], None, ALU.mult).then_inc(p_ready, 1)
                if i >= 3:
                    h = i - 3
                    dve.wait_ge(pv_mm, h + 1)
                    if h < H and h % 2 == 1:
                        V.tensor_copy(yT[:, 4 + h // 2, 0:256], ps[:, 4 + (h // 2) % 2, 0:256]).then_inc(y_used, 1)
                    if h >= H:
                        V.tensor_copy(yT[:, 12 + h - H, 0:256], ps[:, 4 + (h - H) % 2, 0:256]).then_inc(y_used, 1)
            V.memset(bias_s[:, PAST:PAST + 120], NEG).then_inc(dset, 1)
            for g in range(G):
                cols = slice(g * DG, (g + 1) * DG)
                dve.wait_ge(gate_mm, g + 1)
                V.scalar_tensor_tensor(z[:, C_U, 0:2, cols], ps[:, g, 0:256].rearrange("p (t n) -> p t n", t=2),
                                       c("bs")[:, g:g + 1], z[:, C_U, 0:2, cols], ALU.add, ALU.mult)
                V.scalar_tensor_tensor(z[0:64, C_U, 2, cols], ps[0:64, g, 256:384],
                                       c("bss", 64)[:, g:g + 1], z[0:64, C_U, 2, cols], ALU.add, ALU.mult).then_inc(gated, 1)
            dve.wait_ge(gate_tr, G)
            dve.wait_ge(st_va, 32)
            link(V.memset(qmpad, 0.0))
            link(V.memset(qpad, 0.0))
            for r in range(2):
                if r:
                    dve.wait_ge(msc_mm, r)
                V.tensor_copy(qmpad.rearrange("p (b h s) -> p b h s", b=4, h=4)[:, :, :, 0:8],
                              qmT[:, :, NPROMPT + 32 * r:NPROMPT + 32 * r + 32].rearrange("p h (b q) -> p b h q", b=4)
                              ).then_inc(pad_ready, 1)
                dve.wait_ge(msc_mm, r + 1)
                link(V.tensor_reduce(st_m[:, 6:7], ps[:, r, 0:256], X, ALU.max))
                V.tensor_scalar(st_m[:, 4:5], st_m[:, 6:7], -S_MEM, None, ALU.mult).then_inc(mmx, 1)
                dve.wait_ge(mexp, r + 1)
                link(V.reciprocal(st_r[:, 4:5], st_l[:, 4:5]))
                V.tensor_scalar(p_m, p_m, st_r[:, 4:5], None, ALU.mult).then_inc(mp_ready, 1)
                dve.wait_ge(mpv_mm, r + 1)
                V.tensor_copy(yT[:, 12:16, NPROMPT + 32 * r:NPROMPT + 32 * r + 32].rearrange("p h (b q) -> p b h q", b=4),
                              ps[:, 4 + r, 0:128].rearrange("p (b h q) -> p b h q", b=4, h=4)).then_inc(my_ready, 1)
            dve.wait_ge(bs_loaded, 16 * 16)

            def pad_q(b):
                for j in range(2):
                    r = slice(64 * j, 64 * j + 64)
                    last = V.tensor_copy(qpad.rearrange("p (h s) -> p h s", s=144)[r, :, 8 * j:8 * j + 8],
                                         qT[r, :, ds(b * 8 + NPROMPT, 8)])
                last.then_inc(qpad_ready, 1)

            def y_out(b):
                for j in range(2):
                    r = slice(64 * j, 64 * j + 64)
                    last = V.tensor_copy(yT[r, 4:12, ds(b * 8 + NPROMPT, 8)],
                                         ps[r, 6, 0:128].rearrange("p (h s) -> p h s", s=16)[:, :, 8 * j:8 * j + 8])
                last.then_inc(sy_free, 1)

            bB = bias_s[:, 0:1536].rearrange("p (m s) -> p m s", s=16)[:, :, 0:8]

            def soften(b, smx_done):
                dve.wait_ge(s_mm, b * 3 + 1)
                V.scalar_tensor_tensor(sc_s[:, 0:512], ps[:, 0, :], S_WIN, bias_s[:, 1536:2048], ALU.mult, ALU.add).then_inc(s_used, 1)
                dve.wait_ge(s_mm, b * 3 + 2)
                V.scalar_tensor_tensor(sc_s[:, 512:1024].rearrange("p (m s) -> p m s", s=8), ps[:, 1, :].rearrange("p (m s) -> p m s", s=8),
                                       S_WIN, bB[:, 0:64], ALU.mult, ALU.add).then_inc(s_used, 1)
                dve.wait_ge(s_mm, b * 3 + 3)
                V.scalar_tensor_tensor(sc_s[:, 1024:1280].rearrange("p (m s) -> p m s", s=8), ps[:, 2, 0:256].rearrange("p (m s) -> p m s", s=8),
                                       S_WIN, bB[:, 64:96], ALU.mult, ALU.add)
                V.scalar_tensor_tensor(sc_s[:, 1280:1344], ps[:, 2, 256:320], S_WIN, bias_s[:, ds(b * -8 + (PAST + 56), NSAMPLE)],
                                       ALU.mult, ALU.add).then_inc(s_used, 1)
                dve.wait_ge(s_used, b * 3 + 3)
                V.tensor_reduce(st_m[:, 5:6], sc_s, X, ALU.max, negate=True).then_inc(smx, 1)
                dve.wait_ge(sexp, b + 1)
                V.reciprocal(st_r[:, 5:6], st_l[:, 5:6]).then_inc(srec, 1)
                dve.wait_ge(srec, b + 1)
                V.tensor_scalar(sc_s, sc_s, st_r[:, 5:6], None, ALU.mult).then_inc(sp_ready, 1)

            dve.sem_inc(sy_free, 1)
            pad_q(0)
            soften(0, None)
            with dve.Fori(1, NBATCH) as b:
                dve.wait_ge(s_mm, b * 3)
                pad_q(b)
                soften(b, None)
                dve.wait_ge(spv_mm, b)
                y_out(b - 1)
            dve.wait_ge(spv_mm, NBATCH)
            y_out(NBATCH - 1)
            dve.wait_ge(x_again, 48)
            V.memset(st_h, 1.0)
            for ch in range(4):
                for t, (_, m) in enumerate(ROWS):
                    dve.wait_ge(wo_done, 3 * ch + t + 1)
                    hh = hres[0:m, t, ch * 512:(ch + 1) * 512]
                    V.tensor_tensor(hh, ps[0:m, 3 * (ch % 2) + t, :], hh, ALU.add).then_inc(h_ready, 1)
            dve.wait_ge(sumsq, 8)
            V.tensor_scalar(st_h, st_h, 1.0 / D, EPS, ALU.mult, ALU.add).then_inc(ms_ready, 1)
            state["n"] += 1
            dve.wait_ge(rs_ready, state["n"])
            dve.wait_ge(x_again, 64)
            for t, (_, m) in enumerate(ROWS):
                V.scalar_tensor_tensor(n2[0:m, t], hres[0:m, t], st_hr[0:m, t:t + 1], gff[0:m, :], ALU.mult, ALU.mult).then_inc(n2_ready, 1)

            link(V.memset(area(R0, 120), -3e38))
            dve.wait_ge(logits, 1)
            lg = ps[:, 2, 0:108].rearrange("p (t n) -> p t n", t=3)
            for t, m in ((slice(0, 2), P), (slice(2, 3), 64)):
                V.tensor_copy(g8[0:m, t, 0:4], lg[0:m, t, 0:4])
                last = V.tensor_copy(el[0:m, t, :], lg[0:m, t, 4:36])
            link(last)
            for t in range(3):
                link(V.max(mx[:, t, :], g8[:, t, :]))
                link(V.max_index(mi[:, t, :], mx[:, t, :], g8[:, t, :]))
            link(V.tensor_copy(grp, mi[:, :, 0:1]))
            iota = c("iota")
            link(V.tensor_tensor(goh, iota[:, 0:4].unsqueeze(1).to_broadcast([P, 3, 4]), grp.to_broadcast([P, 3, 4]), ALU.is_equal))
            link(V.tensor_tensor(prod, el.rearrange("p t (g e) -> p t g e", g=4), goh.unsqueeze(3).to_broadcast([P, 3, 4, 8]), ALU.mult))
            link(V.tensor_reduce(esel, prod.rearrange("p t g e -> p t e g"), X, ALU.add))
            for t in range(3):
                link(V.max(top[:, t, :], esel[:, t, :]))
                link(V.max_index(ti[:, t, :], top[:, t, :], esel[:, t, :]))
            link(V.tensor_copy(tif, ti[:, :, 0:2]))
            link(V.scalar_tensor_tensor(eid, grp.to_broadcast([P, 3, 2]), float(EPG), tif, ALU.mult, ALU.add))
            for k in range(2):
                link(V.tensor_tensor(moh[:, k], iota[:, 0:32].unsqueeze(1).to_broadcast([P, 3, 32]),
                                     eid[:, :, k:k + 1].to_broadcast([P, 3, 32]), ALU.is_equal))
            link(V.memset(moh[64:128, :, 2, :], 0.0))
            V.tensor_tensor(asum, moh[:, 0], moh[:, 1], ALU.add).then_inc(onehots, 1)
            V.tensor_tensor(dd, top[:, :, 1:2], top[:, :, 0:1], ALU.subtract).then_inc(route_d, 1)
            dve.wait_ge(route_e, 1)
            link(V.tensor_scalar(w1p, dd, 1.0, None, ALU.add))
            link(V.reciprocal(wk[:, 0], w1p))
            link(V.tensor_tensor(wk[:, 1], dd, wk[:, 0], ALU.mult))
            dve.wait_ge(ranks, 1)
            link(V.tensor_copy(nb, ps[:, 3, 96:128]))
            link(V.tensor_tensor(cmp5, nb.unsqueeze(2).to_broadcast([P, 32, 5]),
                                 c("thr")[:, 0:5].unsqueeze(1).to_broadcast([P, 32, 5]), ALU.is_gt))
            link(V.tensor_reduce(nb, cmp5, X, ALU.add))
            link(V.memset(zer, 0.0))
            link(V.tensor_tensor_scan(incl, nb, zer, 0.0, ALU.add, ALU.add))
            link(V.tensor_tensor(base, incl, nb, ALU.subtract))
            for k in range(2):
                link(V.tensor_tensor(pick, moh[:, k], ps[:, 3, 0:96].rearrange("p (t e) -> p t e", t=3), ALU.mult))
                link(V.tensor_reduce(rankf[:, k], pick, X, ALU.add))
                link(V.tensor_tensor(pick, moh[:, k], base.unsqueeze(1).to_broadcast([P, 3, 32]), ALU.mult))
                link(V.tensor_reduce(basef[:, k], pick, X, ALU.add))
            link(V.tensor_tensor(ge4, rankf.unsqueeze(3).to_broadcast([P, 2, 3, 4]),
                                 c("thr")[:, 1:5].unsqueeze(1).unsqueeze(1).to_broadcast([P, 2, 3, 4]), ALU.is_ge))
            link(V.tensor_reduce(fullf, ge4, X, ALU.add))
            link(V.scalar_tensor_tensor(slotf, rankf, float(NTAB), basef, ALU.mult, ALU.add))
            link(V.scalar_tensor_tensor(slotf, fullf, float(1 - BLOCK * NTAB), slotf, ALU.mult, ALU.add))
            link(V.tensor_copy(slot_u, slotf))
            link(V.tensor_copy(pair_u, c("pairs").rearrange("p (k t f) -> p k t f", k=2, t=3)))
            link(V.tensor_tensor(cmpb, incl.unsqueeze(1).to_broadcast([P, NBLK, 32]),
                                 iota[:, 0:NBLK].unsqueeze(2).to_broadcast([P, NBLK, 32]), ALU.is_le))
            link(V.tensor_reduce(ebf, cmpb, X, ALU.add))
            link(V.tensor_scalar(ebf, ebf, float(NEXP - 1), None, ALU.min))
            link(V.tensor_copy(eblk_i, ebf))
            link(V.tensor_scalar(cntf[:, 0:1], incl[:, 31:32], 0.5, 0.25, ALU.mult, ALU.add))
            V.tensor_copy(cnt_i[:, 0:1], cntf[:, 0:1]).then_inc(routed, 1)
            dve.wait_ge(routed, 1)

            pairs = dve.value_load(cnt_i[0:1, 0:1], min_val=1, max_val=NBLK // 2)
            dve.wait_ge(xg_tr, 1)
            V.tensor_copy(xgT[:, 0:8], ps[:, 1, :].rearrange("p (k n) -> p k n", k=8)).then_inc(xgT_ready, 1)
            with dve.Fori(0, pairs) as i:
                for s in range(2):
                    dve.wait_ge(gu_mm, i * 2 + s + 1)
                    V.tensor_copy(gu_sb, ps[:, 0, 0:FF]).then_inc(gu_copied, 1)
                    dve.wait_ge(xg_tr, i * 2 + s + 2)
                    V.tensor_copy(xgT[:, 0:8], ps[:, 1, :].rearrange("p (k n) -> p k n", k=8)).then_inc(xgT_ready, 1)
                    dve.wait_ge(silu_done, i * 2 + s + 1)
                    V.tensor_tensor(actT, sg, ps[:, 3, 0:256].rearrange("p (j n) -> p j n", j=2)[:, :, BLOCK:2 * BLOCK],
                                    ALU.mult).then_inc(act_ready, 1)
                    dve.wait_ge(dn_mm, i * 2 + s + 1)
                    dve.wait_ge(y_free, i * 2 + s + 1)
                    V.tensor_copy(y_sb[:, s, 0:512], ps[:, 4 + 2 * s, :]).then_inc(y_ready, 1)
            for t, (_, m) in enumerate(ROWS):
                dve.wait_ge(back[t], 32)
                for k in range(2):
                    last = V.scalar_tensor_tensor(hres[0:m, t], yg[0:m, k, t], wk[0:m, k, t], hres[0:m, t], ALU.mult, ALU.add)
                    if k == 0:
                        last.then_inc(moe_dv, 1)
                        dve.wait_ge(moe_dv, t + 1)
                last.then_inc(final, 1)

        @block.gpsimd
        def _(pool):
            g = nc.gpsimd
            pool.dma_start(relb[:, :], relb_d).then_inc(s_relb, 16)
            pool.dma_start(onehot[:, :], onehot_d).then_inc(s_relb, 16)
            g.memset(nhalf[:, :], -0.5).then_inc(po, 1)
            pool.dma_start(tab_d, empty_d).then_inc(tab_zero, 16)
            pool.wait_ge(tab_cp, TABLE // 512)
            pool.dma_start(bias_d, table[:, :]).then_inc(tab_out, 16)
            def rsqrt(n, out, in_):
                pool.wait_ge(ms_ready, n)
                g.tensor_tensor(out, in_, nhalf[:, 0:in_.shape[1]], ALU.pow).then_inc(rs_ready, 1)
            pool.wait_ge(po, 1)
            rsqrt(1, st_rs[:, 0:5], stat[:, 0:5])
            pool.wait_ge(rs_ready, 1)
            pool.wait_ge(flip_mm, H // 2)
            g.memset(z[64:128, :, 2, :], 0.0).then_inc(po, 1)
            pool.wait_ge(z_ready, 4)
            pool.dma_start(o_mv.rearrange("(t p) n -> p t n", p=P), mv).then_inc(st_mem, 16)
            rsqrt(2, st_nr[:, 0:8], st_n[:, 0:8])
            pool.wait_ge(normed, 1)
            pool.dma_start(o_mk.rearrange("(t p) n -> p t n", p=P), mk).then_inc(st_mem, 16)
            rsqrt(3, st_nr[:, 0:48], st_n[:, 0:48])
            rsqrt(4, st_nr[:, 0:48], st_n[:, 0:48])
            pool.wait_ge(normed, 3)

            for a in range(2):
                pool.dma_start(o_k[0:256, a * 512:(a + 1) * 512].rearrange("(t p) n -> p t n", p=P), z[:, C_K + a, 0:2, :]).then_inc(st_k, 16)
            pool.dma_start(o_k[256:320, :].rearrange("p (a n) -> p a n", a=2), z[0:64, C_K:C_K + 2, 2, :]).then_inc(st_k, 16)
            rsqrt(5, st_nr[:, 0:12], st_n[:, 0:12])
            pool.wait_ge(z_ready, 4 + 3 * 7)
            for a in range(2):
                pool.dma_start(o_v[0:256, a * 512:(a + 1) * 512].rearrange("(t p) n -> p t n", p=P), z[:, C_V + a, 0:2, :]).then_inc(st_v, 16)
            pool.dma_start(o_v[256:320, :].rearrange("p (a n) -> p a n", a=2), z[0:64, C_V:C_V + 2, 2, :]).then_inc(st_v, 16)
            rsqrt(6, st_nr[:, 0:12], st_n[:, 0:12])
            pool.wait_ge(normed, 5)
            pool.dma_start(o_va[0:128, :], z[:, C_VA, 1, :]).then_inc(st_va, 16)
            pool.dma_start(o_va[128:192, :], z[0:64, C_VA, 2, :]).then_inc(st_va, 16)
            rsqrt(7, st_hr[:, 0:3], st_h[:, 0:3])
            pool.wait_ge(routed, 1)
            pool.wait_ge(tab_zero, 16)
            for k in range(2):
                for t, (_, m) in enumerate(ROWS):
                    pool.indirect_dma_start(tab_d, bass.IndirectOffsetOnAxis(ap=slot_u[0:m, k, t:t + 1], axis=0),
                                            pair_u[0:m, k, t, :], None).then_inc(slots_out, 16)
            pool.wait_ge(slots_out, 16 * 6)
            pool.wait_ge(n2_stored, 48)
            pool.wait_ge(st_mem, 32)
            pool.wait_ge(st_k, 48)
            pool.wait_ge(st_v, 48)
            pool.wait_ge(st_va, 32)
            for half in range(2):
                pool.dma_start(idx_all[64 * half:64 * half + 64], tab_d.rearrange("(p n) f -> p n f", p=BLOCK)).then_inc(idx_in, 16)
            pool.wait_ge(idx_in, 32)
            g.tensor_copy(row_cur, idx_all[0:BLOCK, 0, 0:1]).then_inc(idx_cp, 1)
            g.tensor_scalar(idx_all[64:128, :, 1], idx_all[64:128, :, 1], 1.0, None, ALU.add).then_inc(idx_cp, 1)
            pool.wait_ge(idx_cp, 2)
            pool.indirect_dma_start(xg[0:BLOCK, :], None, n2_d, bass.IndirectOffsetOnAxis(ap=row_cur, axis=0)).then_inc(gathered, 16)
            pairs = pool.value_load(cnt_i[0:1, 0:1], min_val=1, max_val=NBLK // 2)
            g.sem_inc(y_free, 1)
            g.sem_inc(y_free, 1)
            with pool.Fori(0, pairs) as i:
                for s in range(2):
                    pool.wait_ge(xg_tr, i * 2 + s + 1)
                    pool.wait_ge(gathered, i * 32 + 16 * (s + 1))
                    g.tensor_copy(row_cur, idx_all[0:BLOCK, ds(i * 2 + s + 1, 1), 0]).then_inc(idx_cp, 1)
                    g.tensor_copy(dst_cur, idx_all[:, ds(i * 2 + s, 1), 1]).then_inc(idx_cp, 1)
                    pool.wait_ge(idx_cp, i * 4 + 2 * (s + 2))
                    g.sem_inc(pool_seen, 1)
                    pool.indirect_dma_start(xg[0:BLOCK, :], None, n2_d, bass.IndirectOffsetOnAxis(ap=row_cur, axis=0)).then_inc(gathered, 16)
                    pool.wait_ge(y_ready, i * 4 + 2 * (s + 1))
                    g.sem_inc(pool_seen, 1)
                    pool.indirect_dma_start(y_d, bass.IndirectOffsetOnAxis(ap=dst_cur, axis=0), y_sb[:, s, :], None,
                                            bounds_check=4 * NT - 1, oob_is_err=False).then_inc(y_stored, 16)
                    pool.wait_ge(y_stored, i * 32 + 16 * (s + 1))
                    g.sem_inc(y_free, 1)
            pool.wait_ge(y_stored, pairs * 32)
            pool.wait_ge(gathered, pairs * 32 + 16)
            pool.wait_ge(dn_mm, pairs * 2)
            g.sem_inc(pool_seen, 1)
            for t, (r0, m) in enumerate(ROWS):
                for k in range(2):
                    pool.dma_start(yg[0:m, k, t, :].rearrange("p (a n) -> p a n", a=2),
                                   y_d[2 * (k * NT + r0):2 * (k * NT + r0 + m), :].rearrange("(p a) n -> p a n", a=2)).then_inc(back[t], 16)
            for t, (r0, m) in enumerate(ROWS):
                pool.wait_ge(final, t + 1)
                pool.dma_start(o_y[r0:r0 + m, :], hres[0:m, t]).then_inc(st_y, 16)
            pool.wait_ge(st_y, 48)


def distance_bucket(dist):
    d = np.maximum(dist, 0)
    exact = 16
    df = np.maximum(d, 1).astype(np.float32)
    large = exact + (np.log(df / np.float32(exact)) / np.float32(math.log(2048 / exact)) * np.float32(16)).astype(np.int32)
    return np.where(d < exact, d, np.minimum(large, 31))


def constants():
    dist = DIST0 - np.arange(TABLE)
    count = sum(((dist >= 0) & (dist <= w) & (dist % dl == 0)).astype(int) for w, dl in ((128, 1), (512, 4), (2048, 16)))
    onehot = np.zeros((33, TABLE), np.float32)
    onehot[distance_bucket(dist), np.arange(TABLE)] = 1
    onehot[32] = np.where(count > 0, np.log(np.maximum(count, 1)), NEG)
    c = {n: np.zeros((P, w), np.float32) for n, (_, w) in CST.items()}
    c["ident"][:] = np.eye(P)
    c["flip"][:] = np.eye(P)[::-1]
    c["ones"][:] = 1
    c["ltri"][:] = np.triu(np.ones((P, P)), 1)
    c["iota"][:] = np.arange(64)
    c["thr"][:, 0:5] = np.arange(5) * BLOCK
    tok = np.arange(P)[:, None] + np.array([r0 for r0, _ in ROWS])
    c["pairs"][:] = np.stack([np.stack([tok, 2 * (k * NT + tok)], axis=-1) for k in range(2)], axis=1).reshape(P, 12)
    return onehot, c


def kernel(**inputs):
    import concourse.bacc as _bacc
    from concourse.bass_utils import run_bass_kernel_spmd as _run

    a = {k: np.asarray(v) for k, v in inputs.items()}
    onehot, c = constants()
    x = np.concatenate([a["x_prompt"].reshape(NPROMPT, D), a["x_sample"].reshape(NSAMPLE, D)])
    mem = a["mem_prompt"].reshape(NMEM, D)

    def columns(t):
        return np.ascontiguousarray(t.reshape(-1, KT, P).transpose(2, 1, 0))

    def chunks(w):
        return w.reshape(QTR, K4, P, COLS).transpose(0, 2, 1, 3).reshape(QTR, P, K4 * COLS)

    w_in, w_kv, w_out = a["w_in"][0], a["w_mem_kv"][0], a["w_out"][0]
    starts = [1024, 1536, 2048, 2560, 4096, 3072, 3584, 0, 512]
    w_proj = np.stack([chunks(w_kv[:, 0:512]), chunks(w_kv[:, 512:1024])] + [chunks(w_in[:, s:s + 512]) for s in starts])
    w_o = np.stack([chunks(w_out[:, n * 512:(n + 1) * 512]) for n in range(4)])

    def reached(cache):
        late = cache[:, PAST - KEYS_A:]
        early = cache[:, 0:PAST - KEYS_A].reshape(NBATCH, 96, 16, H, DH)[:, :, 0:8].reshape(NBATCH, KEYS_B, H, DH)
        return np.concatenate([late, early], axis=1)

    k = reached(a["cache_win_k"][0]).reshape(NBATCH, KEYS, HP, 128).transpose(0, 3, 2, 1)
    kc = np.concatenate([k[..., s:e].reshape(NBATCH, P, -1) for s, e in ((0, 512), (512, 1024), (1024, 1280))], axis=2)
    v = reached(a["cache_win_v"][0]).reshape(NBATCH, VT, P, H * DH).transpose(0, 2, 1, 3)
    vc = np.ascontiguousarray(v).reshape(NBATCH, P, VT * 1024)
    mkc = a["cache_mem_k"][0].reshape(2, 4, NMEM, G, DG).transpose(4, 0, 1, 3, 2).reshape(P, 2, 16, NMEM)
    mvc = a["cache_mem_v"][0].reshape(2, 4, 2, P, G * DG).transpose(3, 0, 1, 2, 4)

    c["gmix"][:] = a["g_mix"][0].reshape(KT, P).T
    c["gmem"][:] = a["g_mem"][0].reshape(KT, P).T
    c["bs"][:] = a["b_s"][0].T
    c["bss"][0:NSAMPLE] = np.tile(a["b_s"][0][:, 0:NQ].T, (NBATCH, 1))
    wr = np.concatenate([a["w_router_group"][0]] + [a["w_router_expert"][0, g] for g in range(NGRP)], axis=1)
    c["wr"][:] = wr.reshape(KT, P, 36).transpose(1, 0, 2).reshape(P, -1)
    wst = np.zeros((P, G, P), np.float32)
    wsbd = np.zeros((P, G, NSAMPLE), np.float32)
    for t in range(P):
        wst[0:t + 1, :, t] = a["w_s"][0][:, t, 0:t + 1].T
    for b in range(NBATCH):
        wsbd[b * NQ:(b + 1) * NQ, :, b * NQ:(b + 1) * NQ] = wst[0:NQ, :, 0:NQ]
    c["wst"][:] = wst.reshape(P, -1)
    c["wsbd"][:] = wsbd.reshape(P, -1)
    gv = np.concatenate([a["g_qb"][0], a["g_kb"][0], a["g_qm"][0], a["g_km"][0], a["g_av"][0].reshape(-1)])
    relb = np.concatenate([a["rel_bias"], np.ones((1, H), np.float32)])
    w_gu = np.stack([a["w_gate"][0], a["w_up"][0]], axis=1).reshape(NEXP, 2, KT, P, FF).transpose(0, 3, 1, 2, 4)
    w_dn = a["w_down"][0].reshape(NEXP, 2, P, D).transpose(0, 2, 1, 3)

    ins = {
        "x_rows": x, "mem_rows": mem, "x_t": columns(x), "mem_t": columns(mem), "w_proj": w_proj, "w_o": w_o,
        "kc": kc, "vc": vc, "mkc": mkc, "mvc": mvc, "cst_d": np.concatenate([c[n] for n in CST], axis=1),
        "gv_d": gv, "gffn_d": a["g_ffn"][0], "relb_d": relb, "onehot_d": onehot, "w_gu": w_gu, "w_dn": w_dn,
        "empty_d": np.tile(np.array([[0, 4 * NT]], np.uint32), (NTAB * BLOCK, 1)),
    }
    outs = {"o_y": (NT, D), "o_k": (NT, 1024), "o_v": (NT, 1024), "o_va": (192, 512), "o_mk": (NMEM, 512), "o_mv": (NMEM, 512)}
    scratch = {"bias_d": ((H, TABLE), F32), "n2_d": ((NT, D), F32), "tab_d": ((NTAB * BLOCK, 2), U32), "y_d": ((4 * NT, D // 2), F32)}

    nc = _bacc.Bacc("TRN2", target_bir_lowering=False, num_devices=1)
    arrays, args = {}, []
    for name, v in ins.items():
        arrays[name] = np.ascontiguousarray(v)
        args.append(nc.dram_tensor(name, arrays[name].shape, mybir.dt.from_np(arrays[name].dtype), kind="ExternalInput").ap())
    for name, shape in outs.items():
        args.append(nc.dram_tensor(name, shape, F32, kind="ExternalOutput").ap())
    for name, (shape, dt) in scratch.items():
        args.append(nc.dram_tensor(name, shape, dt, kind="Internal").ap())
    hybrid_step(nc, *args)
    r = _run(nc, [arrays], core_ids=[0]).results[0]

    y, k, v, va = r["o_y"], r["o_k"], r["o_v"], r["o_va"]
    return (y[0:256].reshape(1, 256, D), y[256:].reshape(NBATCH, NQ, D),
            k[0:256].reshape(1, 1, 256, H, DH), v[0:256].reshape(1, 1, 256, H, DH),
            va[0:128].reshape(1, 1, 128, G, DG), r["o_mk"].reshape(1, 1, NMEM, G, DG), r["o_mv"].reshape(1, 1, NMEM, G, DG),
            k[256:].reshape(1, NBATCH, NQ, H, DH), v[256:].reshape(1, NBATCH, NQ, H, DH),
            va[128:].reshape(1, NBATCH, NQ, G, DG))
```

```python
import math
from contextlib import ExitStack

import numpy as np

import concourse.bass as bass
from concourse import mybir

F32 = mybir.dt.float32
U32 = mybir.dt.uint32
I32 = mybir.dt.int32
ALU = mybir.AluOpType
ACT = mybir.ActivationFunctionType
X = mybir.AxisListType.X
ds = bass.ds

P = 128
D = 2048
KT = D // P
NPROMPT, NBATCH, NQ = 256, 8, 8
NSAMPLE = NBATCH * NQ
NT = NPROMPT + NSAMPLE
ROWS = [(0, 128), (128, 128), (256, 64)]
H, DH = 16, 64
HP = H // 2
G, DG = 4, 128
NMEM = 256
PAST = 2048
EPS = 1e-6
NEG = -1e30
COLS = 512
QTR = 4
K4 = KT // QTR
NCHUNK = 9
C_Q, C_K, C_QM, C_V, C_U, C_VA = 0, 2, 4, 5, 7, 8
KEYS_A, KEYS_B = 512, 768
KEYS = KEYS_A + KEYS_B
VT = KEYS // P
NKEY = KEYS + NSAMPLE
DIST0 = PAST + NQ - 1
TABLE = 2560
NEXP, NGRP, EPG, FF = 32, 4, 8, 256
BLOCK = 64
NBLK = (2 * NT - NEXP) // BLOCK + NEXP + 1
NBLK += NBLK % 2
NTAB = NBLK + 2
S_WIN = DH ** -0.5
S_MEM = DG ** -0.5

CST = {}
_at = 0
for _n, _w in (("ident", 128), ("flip", 128), ("ones", 128), ("ltri", 128), ("iota", 64), ("thr", 8), ("pairs", 12),
               ("gmix", 16), ("gmem", 16), ("bs", 4), ("bss", 4), ("wr", KT * 36), ("wst", 4 * 128), ("wsbd", 4 * 64),
               ("wmask", 256), ("wsel", 32), ("mmask", 512), ("msel", 32)):
    CST[_n] = (_at, _w)
    _at += _w
NCST = _at
GV = {"qb": (0, 64), "kb": (64, 64), "qm": (128, 128), "km": (256, 128), "av": (384, 512)}


class Steps:

    def __init__(self, eng, sem):
        self.eng, self.sem, self.base, self.n = eng, sem, 0, 0

    def __call__(self, ins):
        self.n += 1
        ins.then_inc(self.sem, 1)
        self.eng.wait_ge(self.sem, self.base + self.n)


def hybrid_step(nc, x_rows, mem_rows, x_t, mem_t, w_proj, w_o, kc, vc, mkc, mvc, cst_d, gv_d, gffn_d,
                relb_d, onehot_d, w_gu, w_dn, empty_d, o_y, o_k, o_v, o_va, o_mk, o_mv,
                bias_d, n2_d, tab_d, y_d):
    with ExitStack() as ctx:
        def sb(name, shape, dt=F32):
            return ctx.enter_context(nc.sbuf_tensor(name, shape, dt))

        def sem(name):
            return ctx.enter_context(nc.semaphore(name))

        cst = sb("cst", [P, NCST])
        gv = sb("gv", [P, 896])
        stat = sb("stat", [P, 256])
        nhalf = sb("nhalf", [P, 48])
        idx = sb("idx", [P, 24], U32)
        ARENA = 49152
        arena = sb("arena", [P, ARENA])
        ps = ctx.enter_context(nc.psum_tensor("ps", [P, 8, 512], F32))

        def c(name, rows=P):
            a, w = CST[name]
            return cst[0:rows, a:a + w]

        def area(at, *dims):
            n = int(np.prod(dims))
            ap = arena[:, at:at + n]
            if len(dims) == 1:
                return ap
            names = "abcdef"[:len(dims)]
            return ap.rearrange(f"p ({' '.join(names)}) -> p {' '.join(names)}",
                                **{k: v for k, v in zip(names, dims)})

        ident = c("ident")
        wr = c("wr").rearrange("p (k n) -> p k n", k=KT)
        wst = c("wst").rearrange("p (g n) -> p g n", g=G)
        wsbd = c("wsbd").rearrange("p (g n) -> p g n", g=G)
        A_W, A_XT = 0, 8192
        A_Z = A_XT + KT * NT
        A_BP = A_Z + NCHUNK * 3 * COLS
        A_KV = A_BP + H * 256
        A_QT = A_KV + 2048
        A_KT = A_QT + HP * NT
        A_QMT = A_KT + HP * NT
        A_MKT = A_QMT + G * NT
        A_Y = A_MKT + G * NMEM
        A_BS = A_Y + KT * NT
        A_END = A_BS + 2176
        assert A_END <= ARENA, A_END
        wring = area(A_W, QTR, K4, COLS)
        xT = area(A_XT, KT, NT)
        z = area(A_Z, NCHUNK, 3, COLS)
        bias_p = area(A_BP, H, 256)
        mk = area(A_KV, 2, COLS)
        mv = area(A_KV + 1024, 2, COLS)
        qT = area(A_QT, HP, NT)
        kT = area(A_KT, HP, NT)
        qmT = area(A_QMT, G, NT)
        mkT = area(A_MKT, G, NMEM)
        memT = area(A_Y, KT, NMEM)
        yT = area(A_Y, KT, NT)
        bias_s = area(A_BS, 2168)
        xst = area(A_QT, 2, D)
        bias_r = area(A_Z + C_V * 3 * COLS, H, 256)
        onehot = area(A_QT + 2 * D, TABLE)[0:33, :]
        relb = area(A_QT + 2 * D + TABLE, H)[0:33, :]
        table = area(A_BP, TABLE)[0:H, :]
        sc_p = [area(A_BS, 512), area(A_BS + 512, 512), mk[:, 0, :]]
        pt_p = area(A_BS + 1024, 2, 512)
        qmpad = area(A_END, 4 * 160)
        p_m = area(A_END + 640, 2, 256)
        pt_m = area(A_Y, 2, 2, P)
        y_m = area(A_Y + 512, COLS)
        kbuf = area(0, HP * KEYS)
        kA = area(0, HP, 512)
        kB1 = area(4096, HP, 512)
        kB2 = area(8192, HP, 256)
        vbuf = area(HP * KEYS, VT, 1024)
        assert 2 * HP * KEYS <= A_Z + C_V * 3 * COLS
        mkb = area(0, 2, 16, NMEM)
        mvb = area(10240, 2, 4, 2, COLS)
        A_RB = A_Z + C_U * 3 * COLS
        sc_s = area(A_RB, NKEY)
        pt_s = area(A_RB + 1344, 11, P)
        qpad = area(A_RB + 1344 + 1408, HP * 144)
        y_s = area(A_RB + 3904, 256)
        assert 3904 + 256 <= 2 * 3 * COLS + 4096
        A_H = A_RB + 512
        hres = area(A_H, 3, D)
        n2 = area(10240, 3, D)
        n2T = area(16384, KT, NT)
        gff = area(21504, D)
        wgu = area(0, 2, 2, KT, FF)
        wdn = area(16384, 2, 2, D)
        assert 24576 <= A_H and A_H + 3 * D <= A_KV
        A_E = A_H + 3 * D
        xg = area(A_E, 2, D)
        xgT = area(A_E + 2 * D, KT, BLOCK)
        E0 = A_E + 2 * D + KT * BLOCK
        gu_sb = area(E0, FF)
        sg = area(E0 + 256, 2, BLOCK)
        actT = area(E0 + 384, 2, BLOCK)
        y_sb = area(E0 + 512, 2, 1024)
        eblk_i = area(E0 + 2560, NBLK).bitcast(I32)
        cnt_i = area(E0 + 2624, 8).bitcast(I32)
        idx_all = area(E0 + 2640, 2 * NTAB).bitcast(U32).rearrange("p (n f) -> p n f", f=2)
        R0 = E0 + 2730
        g8 = area(R0, 3, 8)
        el = area(R0 + 24, 3, 32)
        mx = area(R0 + 120, 3, 8)
        mi = area(R0 + 144, 3, 8).bitcast(U32)
        grp = area(R0 + 168, 3, 1)
        goh = area(R0 + 171, 3, 4)
        prod = area(R0 + 183, 3, 4, 8)
        esel = area(R0 + 279, 3, 8)
        top = area(R0 + 303, 3, 8)
        ti = area(R0 + 327, 3, 8).bitcast(U32)
        tif = area(R0 + 351, 3, 2)
        eid = area(R0 + 357, 3, 2)
        moh = area(R0 + 363, 2, 3, 32)
        asum = area(R0 + 555, 3, 32)
        cmp5 = area(R0 + 651, 32, 5)
        nb = area(R0 + 811, 32)
        zer = area(R0 + 843, 32)
        incl = area(R0 + 875, 32)
        base = area(R0 + 907, 32)
        ge4 = area(R0 + 939, 2, 3, 4)
        rankf = area(R0 + 963, 2, 3)
        basef = area(R0 + 969, 2, 3)
        fullf = area(R0 + 975, 2, 3)
        pick = area(R0 + 1035, 3, 32)
        slotf = area(R0 + 1131, 2, 3)
        dd = area(R0 + 1137, 3, 1)
        w1p = area(R0 + 1140, 3, 1)
        wk = area(R0 + 1143, 2, 3, 1)
        cmpb = area(R0 + 1149, NBLK, 32)
        ebf = area(R0 + 1149 + NBLK * 32, NBLK)
        cntf = area(R0 + 1149 + NBLK * 33, 8)
        assert R0 + 1149 + NBLK * 33 + 8 <= ARENA
        yg = area(0, 2, 3, D)
        slot_u = idx[:, 0:6].rearrange("p (k t) -> p k t", k=2)
        pair_u = idx[:, 8:20].rearrange("p (k t f) -> p k t f", k=2, t=3)
        row_cur = [idx[0:BLOCK, 20 + s:21 + s] for s in range(2)]
        dst_cur = [idx[:, 22 + s:23 + s] for s in range(2)]

        s_cst, s_gv, s_relb = sem("s_cst"), sem("s_gv"), sem("s_relb")
        s_xst = [sem(f"s_xst{i}") for i in range(2)]
        s_xt, s_memt = sem("s_xt"), sem("s_memt")
        w_loaded = [sem(f"w_loaded{i}") for i in range(QTR)]
        w_used, gemm_done, z_ready = sem("w_used"), sem("gemm_done"), sem("z_ready")
        dv, ac, po = sem("dv"), sem("ac"), sem("po")
        pe_seen, pool_seen = sem("pe_seen"), sem("pool_seen")
        flip_mm, flip_used = sem("flip_mm"), sem("flip_used")
        dset, xt_scaled, sumsq, ms_ready, rs_ready = sem("dset"), sem("xt_scaled"), sem("sumsq"), sem("ms_ready"), sem("rs_ready")
        tab_mm, tab_cp, tab_out, bp_loaded, bs_loaded = sem("tab_mm"), sem("tab_cp"), sem("tab_out"), sem("bp_loaded"), sem("bs_loaded")
        normed, gelu_done, tr_done, tr_used = sem("normed"), sem("gelu_done"), sem("tr_done"), sem("tr_used")
        st_mem, st_k, st_v, st_va, st_y = (sem(n) for n in ("st_mem", "st_k", "st_v", "st_va", "st_y"))
        sc_read, sy_free, y_free, srec, route_d, route_e = (sem(n) for n in (
            "sc_read", "sy_free", "y_free", "srec", "route_d", "route_e"))
        sc_mm, mx_ready, exp_done, p_ready, pt_mm, pt_ready, pv_mm, y_used = (sem(n) for n in (
            "sc_mm", "mx_ready", "exp_done", "p_ready", "pt_mm", "pt_ready", "pv_mm", "y_used"))
        gate_mm, gated, gate_tr, gate_y = sem("gate_mm"), sem("gated"), sem("gate_tr"), sem("gate_y")
        pad_ready, mem_loaded, msc_mm, mmx, mexp, mpt_mm, mpt_ready, mpv_mm, m_masked, mfold_mm, my_ready = (sem(n) for n in (
            "pad_ready", "mem_loaded", "msc_mm", "mmx", "mexp", "mpt_mm", "mpt_ready", "mpv_mm", "m_masked", "mfold_mm", "my_ready"))
        k_loaded = [sem(f"k_loaded{i}") for i in range(3)]
        v_loaded, qpad_ready, s_mm, s_used, smx, sexp, spt_mm, spt_ready, spv_mm, s_masked, fold_mm, y_copied = (sem(n) for n in (
            "v_loaded", "qpad_ready", "s_mm", "s_used", "smx", "sexp", "spt_mm", "spt_ready", "spv_mm", "s_masked", "fold_mm", "y_copied"))
        wo_loaded = [sem(f"wo_loaded{i}") for i in range(QTR)]
        wo_used, wo_done, x_again, h_ready = sem("wo_used"), sem("wo_done"), sem("x_again"), sem("h_ready")
        n2_ready, n2_tr, n2T_ready, logits, routed, n2_stored, tab_zero, slots_out, idx_in = (sem(n) for n in (
            "n2_ready", "n2_tr", "n2T_ready", "logits", "routed", "n2_stored", "tab_zero", "slots_out", "idx_in"))
        onehots, ranks = sem("onehots"), sem("ranks")
        gu_loaded = [sem(f"gu_loaded{i}") for i in range(2)]
        dn_loaded = [sem(f"dn_loaded{i}") for i in range(2)]
        gathered = [sem(f"gathered{s}") for s in range(2)]
        xg_tr, xgT_ready, gu_mm, gu_copied, at_mm, silu_done, act_ready, dn_mm, y_ready = (sem(n) for n in (
            "xg_tr", "xgT_ready", "gu_mm", "gu_copied", "at_mm", "silu_done", "act_ready", "dn_mm", "y_ready"))
        y_stored = [sem(f"y_stored{s}") for s in range(2)]
        back = [sem(f"back{t}") for t in range(3)]
        final, moe_dv, idx_cp = sem("final"), sem("moe_dv"), sem("idx_cp")

        NORM_X, NORM_MEM = 0, 3
        st_rs = stat[:, 8:16]
        st_n = stat[:, 16:64]
        st_nr = stat[:, 64:112]
        st_m = stat[:, 112:124]
        st_l = stat[:, 124:136]
        st_r = stat[:, 136:148]
        st_h = stat[:, 148:151]
        st_hr = stat[:, 152:155]

        block = ctx.enter_context(nc.Block())

        @block.sync
        def _(sp):
            sp.dma_start(cst[:, :], cst_d).then_inc(s_cst, 16)
            sp.dma_start(memT, mem_t).then_inc(s_memt, 16)
            for q in range(QTR):
                sp.dma_start(wring[:, q], w_proj[0, q]).then_inc(w_loaded[q], 16)
            for n in range(2):
                sp.dma_start(xst[:, n], mem_rows[n * P:(n + 1) * P, :]).then_inc(s_xst[n], 16)
            sp.dma_start(xT, x_t).then_inc(s_xt, 16)
            sp.dma_start(gv[:, :], gv_d.partition_broadcast(P)).then_inc(s_gv, 16)
            for n, (r0, m) in enumerate(ROWS):
                sp.wait_ge(sumsq, n + 1)
                sp.dma_start(xst[0:m, n % 2], x_rows[r0:r0 + m, :]).then_inc(s_xst[n % 2], 16)
            sp.wait_ge(tab_out, 16)
            sp.dma_start(bias_r, bass.AP(tensor=bias_d.tensor, offset=DIST0 - 255, ap=[[1, P], [TABLE, H], [1, 256]])
                         ).then_inc(bp_loaded, 16)

            def next_chunk(ch, before):
                for q in range(QTR):
                    if q < QTR - 1:
                        sp.wait_ge(w_used, (ch - 1) * (QTR - 1) + q + 1)
                    else:
                        sp.wait_ge(gemm_done, before)
                    sp.dma_start(wring[:, q], w_proj[ds(ch, 1), q]).then_inc(w_loaded[q], 16)
            next_chunk(1, 2)
            with sp.Fori(2, NCHUNK + 2) as ch:
                next_chunk(ch, ch * 3 - 2)
            sp.wait_ge(gemm_done, 4 + 3 * NCHUNK)
            sp.dma_start(mkb, mkc).then_inc(mem_loaded, 16)
            sp.wait_ge(tr_done, 24)
            sp.wait_ge(st_k, 48)
            sp.dma_start(mvb, mvc).then_inc(mem_loaded, 16)
            sp.wait_ge(msc_mm, 2)
            sp.wait_ge(mpv_mm, 2)
            for n, (kp, a, b) in enumerate(((kA, 0, 4096), (kB1, 4096, 8192), (kB2, 8192, 10240))):
                sp.dma_start(kp, kc[0, :, a:b]).then_inc(k_loaded[n], 16)
            sp.dma_start(vbuf, vc[0]).then_inc(v_loaded, 16)
            sp.wait_ge(pv_mm, 20)
            sp.wait_ge(dset, 2)
            for q in range(NQ):
                sp.dma_start(bias_s[q:P:NQ, 0:PAST], bias_d[:, DIST0 - PAST - q:DIST0 - q]).then_inc(bs_loaded, 16)
                sp.dma_start(bias_s[q:P:NQ, PAST + 56:PAST + 64], bias_d[:, DIST0 - q:DIST0 - q + NQ]).then_inc(bs_loaded, 16)
            with sp.Fori(1, NBATCH) as b:
                for n, (kp, a, e) in enumerate(((kA, 0, 4096), (kB1, 4096, 8192), (kB2, 8192, 10240))):
                    sp.wait_ge(s_mm, (b - 1) * 3 + n + 1)
                    sp.dma_start(kp, kc[ds(b, 1), :, a:e]).then_inc(k_loaded[n], 16)
                sp.wait_ge(spv_mm, b)
                sp.dma_start(vbuf, vc[ds(b, 1)]).then_inc(v_loaded, 16)
            sp.wait_ge(s_mm, 3 * NBATCH)
            for q in range(QTR):
                sp.dma_start(wring[:, q], w_o[0, q]).then_inc(wo_loaded[q], 16)
            sp.wait_ge(fold_mm, NBATCH)
            sp.wait_ge(st_v, 48)
            for n, (r0, m) in enumerate(ROWS):
                sp.dma_start(hres[0:m, n], x_rows[r0:r0 + m, :]).then_inc(x_again, 16)
            with sp.Fori(1, 4) as ch:
                for q in range(QTR):
                    if q < QTR - 1:
                        sp.wait_ge(wo_used, (ch - 1) * (QTR - 1) + q + 1)
                    else:
                        sp.wait_ge(wo_done, ch * 3)
                    sp.dma_start(wring[:, q], w_o[ds(ch, 1), q]).then_inc(wo_loaded[q], 16)
            sp.dma_start(gff, gffn_d.partition_broadcast(P)).then_inc(x_again, 16)
            for n, (r0, m) in enumerate(ROWS):
                sp.wait_ge(n2_ready, n + 1)
                sp.dma_start(n2_d[r0:r0 + m, :], n2[0:m, n]).then_inc(n2_stored, 16)
            sp.wait_ge(routed, 1)
            sp.wait_ge(n2_stored, 48)
            pairs = sp.value_load(cnt_i[0:1, 0:1], min_val=1, max_val=NBLK // 2)
            for s in range(2):
                e = sp.value_load(eblk_i[0:1, s:s + 1], min_val=0, max_val=NEXP - 1)
                sp.dma_start(wgu[:, s], w_gu[ds(e, 1)]).then_inc(gu_loaded[s], 16)
                sp.dma_start(wdn[:, s], w_dn[ds(e, 1)]).then_inc(dn_loaded[s], 16)
            with sp.Fori(1, pairs) as i:
                for s in range(2):
                    e = sp.value_load(eblk_i[0:1, ds(i * 2 + s, 1)], min_val=0, max_val=NEXP - 1)
                    sp.wait_ge(gu_mm, i * 2 + (s - 1))
                    sp.dma_start(wgu[:, s], w_gu[ds(e, 1)]).then_inc(gu_loaded[s], 16)
                    sp.wait_ge(dn_mm, i * 2 + (s - 1))
                    sp.dma_start(wdn[:, s], w_dn[ds(e, 1)]).then_inc(dn_loaded[s], 16)

        @block.tensor
        def _(pe):
            mm, tr = nc.tensor.matmul, nc.tensor.transpose
            pe.wait_ge(s_relb, 32)
            for n in range(TABLE // 512):
                if n >= 2:
                    pe.wait_ge(tab_cp, n - 1)
                mm(ps[0:H, 6 + n % 2, :], relb[:, :], onehot[:, n * 512:(n + 1) * 512], start=True, stop=True).then_inc(tab_mm, 1)

            def chunk(bank, src, rows, load_value):
                for q in range(QTR):
                    pe.wait_ge(w_loaded[q], load_value)
                    for t, (r0, m) in enumerate(rows):
                        for k in range(K4):
                            kt = q * K4 + k
                            last = mm(ps[0:m, bank + t, :], src[:, kt, r0:r0 + m], wring[:, q, k, :],
                                      start=kt == 0, stop=kt == KT - 1)
                        if q == QTR - 1:
                            last.then_inc(gemm_done, 1)
                    if q < QTR - 1:
                        last.then_inc(w_used, 1)

            pe.wait_ge(xt_scaled, 1)
            for ch in range(2):
                chunk(3 * ch, memT, ROWS[:2], 16 * (ch + 1))
            pe.wait_ge(bp_loaded, 16)
            pe.wait_ge(tab_cp, TABLE // 512)
            for n in range(H // 2):
                if n >= 2:
                    pe.wait_ge(flip_used, n - 1)
                mm(ps[:, 6 + n % 2, :], c("flip"), bias_r[:, 2 * n:2 * n + 2, :], start=True, stop=True).then_inc(flip_mm, 1)
            pe.wait_ge(xt_scaled, 2)
            pe.wait_ge(z_ready, 4)
            with pe.Fori(0, NCHUNK // 2) as i:
                for s in range(2):
                    pe.wait_ge(z_ready, i * 6 + (4 + 3 * (s - 1)))
                    chunk(3 * s, xT, ROWS, i * 32 + 16 * (s + 3))
            pe.wait_ge(z_ready, 4 + 3 * (NCHUNK - 2))
            chunk(0, xT, ROWS, 16 * (NCHUNK + 2))

            def turn(n, src, rows):
                if n >= 2:
                    pe.wait_ge(tr_used, n - 1)
                for t, (r0, m) in enumerate(rows):
                    last = tr(ps[:, 6 + n % 2, r0:r0 + m], src(t)[0:m, :], ident[0:m, 0:m])
                last.then_inc(tr_done, 1)
            pe.wait_ge(flip_used, H // 2)
            n = 0
            pe.wait_ge(normed, 1)
            for g in range(G):
                turn(n, lambda t: mk[:, t, g * DG:(g + 1) * DG], ROWS[:2])
                n += 1
            pe.wait_ge(normed, 4)
            for ch, pairs in ((C_Q, HP), (C_K, HP), (C_QM, G)):
                for hp in range(pairs):
                    turn(n, lambda t: z[:, ch + hp // 4, t, (hp % 4) * P:(hp % 4 + 1) * P], ROWS)
                    n += 1
            pe.wait_ge(tr_used, n)
            pe.wait_ge(z_ready, 4 + 3 * NCHUNK)

            def scores(h):
                if h >= 2:
                    pe.wait_ge(sc_read, h - 1)
                b = h % 2
                if h < H:
                    r = slice(64 * (h % 2), 64 * (h % 2) + 64)
                    mm(ps[:, b, 0:128], qT[r, h // 2, 0:128], kT[r, h // 2, 0:128], start=True, stop=True)
                    mm(ps[:, b, 128:384], qT[r, h // 2, 128:256], kT[r, h // 2, 0:256], start=True, stop=True).then_inc(sc_mm, 1)
                else:
                    g = h - H
                    mm(ps[:, b, 0:256], qmT[:, g, 0:128], mkT[:, g, :], start=True, stop=True)
                    mm(ps[:, b, 256:512], qmT[:, g, 128:256], mkT[:, g, :], start=True, stop=True).then_inc(sc_mm, 1)

            def turn_p(h):
                b = 2 + h % 2
                pe.wait_ge(p_ready, h + 1)
                if h >= 2:
                    pe.wait_ge(pt_ready, h - 1)
                p = sc_p[h % 3]
                if h < H:
                    tr(ps[:, b, 0:128], p[:, 0:128], ident)
                    tr(ps[:, b, 128:256], p[:, 128:256], ident)
                    tr(ps[:, b, 256:384], p[:, 256:384], ident).then_inc(pt_mm, 1)
                else:
                    tr(ps[:, b, 0:128], p[:, 0:128], ident)
                    tr(ps[:, b, 128:256], p[:, 256:384], ident)
                    tr(ps[:, b, 256:384], p[:, 128:256], ident)
                    tr(ps[:, b, 384:512], p[:, 384:512], ident).then_inc(pt_mm, 1)

            def values(h):
                pe.wait_ge(pt_ready, h + 1)
                pt = pt_p[:, h % 2]
                if h < H:
                    hp, r = h // 2, slice(64 * (h % 2), 64 * (h % 2) + 64)
                    b = 4 + hp % 2
                    if h % 2 == 0 and hp >= 2:
                        pe.wait_ge(y_used, hp - 1)
                    v = [z[:, C_V + h // 8, t, (h % 8) * DH:(h % 8 + 1) * DH] for t in range(2)]
                    mm(ps[r, b, 0:256], v[0], pt[:, 0:256], start=True, stop=False, skip_group_check=True)
                    mm(ps[r, b, 128:256], v[1], pt[:, 256:384], start=False, stop=True, skip_group_check=True).then_inc(pv_mm, 1)
                else:
                    g = h - H
                    b = 4 + g % 2
                    pe.wait_ge(y_used, HP + g - 1)
                    mm(ps[:, b, 0:256], mv[:, 0, g * DG:(g + 1) * DG], pt[:, 0:256], start=True, stop=False)
                    mm(ps[:, b, 0:256], mv[:, 1, g * DG:(g + 1) * DG], pt[:, 256:512], start=False, stop=True).then_inc(pv_mm, 1)

            def gate():
                pe.wait_ge(normed, 5)
                pe.wait_ge(my_ready, 2)
                for g in range(G):
                    cols = slice(g * DG, (g + 1) * DG)
                    for t in range(2):
                        mm(ps[:, 6, t * 128:(t + 1) * 128], wst[:, g, :], z[:, C_VA, t, cols], start=True, stop=True)
                    mm(ps[0:64, 6, 256:384], wsbd[0:64, g, :], z[0:64, C_VA, 2, cols], start=True, stop=True).then_inc(gate_mm, 1)
                    pe.wait_ge(gated, g + 1)
                    if g:
                        pe.wait_ge(gate_y, g)
                    for t, (r0, m) in enumerate(ROWS):
                        last = tr(ps[:, 7, r0:r0 + m], z[0:m, C_U, t, g * DG:(g + 1) * DG], ident[0:m, 0:m])
                    last.then_inc(gate_tr, 1)

            def memory_scores(r):
                pe.wait_ge(pad_ready, r + 1)
                if r == 0:
                    pe.wait_ge(mem_loaded, 32)
                else:
                    pe.wait_ge(mexp, r)
                for h in range(G):
                    for b in range(4):
                        last = mm(ps[32 * b:32 * b + 32, 6, 256 * r:256 * r + 256], qmpad[:, b * 160 + h * 32:b * 160 + h * 32 + 32],
                                  mkb[:, r, 4 * b + h, :], start=h == 0, stop=h == 3)
                last.then_inc(msc_mm, 1)

            def memory_turn(r):
                pe.wait_ge(mexp, r + 1)
                if r:
                    pe.wait_ge(mpt_ready, r)
                for t in range(2):
                    last = tr(ps[:, 7, r * 256 + t * 128:r * 256 + (t + 1) * 128], p_m[:, r, t * 128:(t + 1) * 128], ident)
                last.then_inc(mpt_mm, 1)

            def memory_values(r):
                pe.wait_ge(mpt_ready, r + 1)
                pe.wait_ge(m_masked, r) if r else pe.wait_ge(mexp, 2)
                for t in range(2):
                    for b in range(4):
                        last = mm(ps[32 * b:32 * b + 32, 6, :], pt_m[:, r, t, 32 * b:32 * b + 32], mvb[:, r, b, t, :],
                                  start=t == 0, stop=t == 1)
                last.then_inc(mpv_mm, 1)

            def memory_fold(r):
                pe.wait_ge(m_masked, r + 1)
                pe.wait_ge(my_ready, r) if r else pe.wait_ge(mpt_ready, 2)
                for h in range(G):
                    last = mm(ps[:, 7, 32 * h:32 * h + 32], y_m[:, h * 128:(h + 1) * 128], c("msel"), start=True, stop=True)
                last.then_inc(mfold_mm, 1)

            between = {9: lambda: memory_scores(0), 10: lambda: memory_turn(0), 11: lambda: memory_scores(1),
                       12: lambda: memory_turn(1), 13: lambda: memory_values(0), 14: lambda: memory_fold(0),
                       15: lambda: memory_values(1), 16: lambda: memory_fold(1), 18: gate}
            for i in range(20 + 3):
                if i < 20:
                    scores(i)
                if i in between:
                    between[i]()
                if 2 <= i <= 21:
                    turn_p(i - 2)
                if i >= 3:
                    values(i - 3)
            pe.wait_ge(y_used, HP + G)
            pe.wait_ge(gate_y, G)

            def qk(b):
                pe.wait_ge(qpad_ready, b + 1)
                for n, (kp, w) in enumerate(((kA, 512), (kB1, 512), (kB2, 256))):
                    pe.wait_ge(k_loaded[n], b * 16 + 16)
                    if type(b) is not int:
                        pe.wait_ge(s_used, (b - 1) * 3 + n + 1)
                    for half in range(2):
                        for g in range(4):
                            hp = 2 * g + half
                            last = mm(ps[32 * g:32 * g + 32, n, 0:w], qpad[:, hp * 128 + 32 * g:hp * 128 + 32 * g + 32],
                                      kp[:, hp, :], start=half == 0, stop=half == 1)
                    if n == 2:
                        for half in range(2):
                            for g in range(4):
                                hp = 2 * g + half
                                last = mm(ps[32 * g:32 * g + 32, n, w:w + NSAMPLE],
                                          qpad[:, hp * 128 + 32 * g:hp * 128 + 32 * g + 32],
                                          kT[:, hp, NPROMPT:NT], start=half == 0, stop=half == 1)
                    last.then_inc(s_mm, 1)

            def turn_s(b):
                pe.wait_ge(sexp, b + 1)
                if type(b) is not int:
                    pe.wait_ge(spt_ready, b * 3)
                for t in range(11):
                    w = 128 if t < VT else NSAMPLE
                    last = tr(ps[0:w, 3 + t // 4, (t % 4) * 128:(t % 4) * 128 + 128], sc_s[:, t * 128:t * 128 + w], ident)
                    if t in (3, 7, 10):
                        last.then_inc(spt_mm, 1)

            def pv(turned, loaded, free):
                pe.wait_ge(spt_ready, turned)
                pe.wait_ge(v_loaded, loaded)
                pe.wait_ge(s_masked, free)
                for t in range(VT + 1):
                    for g in range(4):
                        if t < VT:
                            v, w = vbuf[:, t, g * 256:(g + 1) * 256], P
                        else:
                            v, w = z[0:NSAMPLE, C_V + g // 2, 2, (g % 2) * 256:(g % 2 + 1) * 256], NSAMPLE
                        last = mm(ps[32 * g:32 * g + 32, 6, 0:256], pt_s[0:w, t, 32 * g:32 * g + 32], v, start=t == 0, stop=t == VT)
                last.then_inc(spv_mm, 1)

            def fold(masked):
                pe.wait_ge(s_masked, masked)
                for j in range(2):
                    last = mm(ps[:, 7, 32 * j:32 * j + 32], y_s[:, j * 128:(j + 1) * 128], c("wsel"), start=True, stop=True)
                last.then_inc(fold_mm, 1)

            qk(0)
            turn_s(0)
            with pe.Fori(1, NBATCH) as b:
                pv(b * 3, b * 16, b)
                qk(b)
                fold(b + 1)
                turn_s(b)
            pv(3 * NBATCH, 16 * NBATCH, NBATCH)
            fold(NBATCH + 1)
            pe.wait_ge(y_copied, NBATCH)

            def out_chunk(bank, load_value):
                for q in range(QTR):
                    pe.wait_ge(wo_loaded[q], load_value)
                    for t, (r0, m) in enumerate(ROWS):
                        for k in range(K4):
                            kt = q * K4 + k
                            last = mm(ps[0:m, bank + t, :], yT[:, kt, r0:r0 + m], wring[:, q, k, :],
                                      start=kt == 0, stop=kt == KT - 1)
                        if q == QTR - 1:
                            last.then_inc(wo_done, 1)
                    if q < QTR - 1:
                        last.then_inc(wo_used, 1)
            out_chunk(0, 16)
            out_chunk(3, 32)
            pe.wait_ge(h_ready, 3)
            out_chunk(0, 48)
            pe.wait_ge(h_ready, 6)
            out_chunk(3, 64)

            pe.wait_ge(h_ready, 12)
            for t, (r0, m) in enumerate(ROWS):
                pe.wait_ge(n2_ready, t + 1)
                for k4 in range(4):
                    j = t * 4 + k4
                    if j >= 2:
                        pe.wait_ge(n2T_ready, j - 1)
                    for k in range(4):
                        kt = k4 * 4 + k
                        last = tr(ps[:, j % 2, k * 128:k * 128 + m], n2[0:m, t, kt * 128:(kt + 1) * 128], ident[0:m, 0:m])
                    last.then_inc(n2_tr, 1)
            pe.wait_ge(n2T_ready, 12)
            for t, (r0, m) in enumerate(ROWS):
                for kt in range(KT):
                    last = mm(ps[0:m, 2, t * 36:(t + 1) * 36], n2T[:, kt, r0:r0 + m], wr[:, kt, :], start=kt == 0, stop=kt == KT - 1)
            last.then_inc(logits, 1)
            pe.wait_ge(onehots, 1)
            for t in range(3):
                mm(ps[:, 3, t * 32:(t + 1) * 32], c("ltri"), asum[:, t, :], start=True, stop=t == 0)
                for u in range(t):
                    mm(ps[:, 3, t * 32:(t + 1) * 32], c("ones"), asum[:, u, :], start=False, stop=u == t - 1)
            for t in range(3):
                last = mm(ps[:, 3, 96:128], c("ones"), asum[:, t, :], start=t == 0, stop=t == 2)
            last.then_inc(ranks, 1)

            def turn_x(s, value):
                pe.wait_ge(gathered[s], value)
                pe.sem_inc(pe_seen, 1)
                for kt in range(KT):
                    last = tr(ps[:, 1 + kt // 8, (kt % 8) * 64:(kt % 8) * 64 + 64], xg[0:BLOCK, s, kt * 128:(kt + 1) * 128],
                              ident[0:BLOCK, 0:BLOCK])
                last.then_inc(xg_tr, 1)

            pe.wait_ge(routed, 1)
            pairs = pe.value_load(cnt_i[0:1, 0:1], min_val=1, max_val=NBLK // 2)
            turn_x(0, 16)
            with pe.Fori(0, pairs) as i:
                for s in range(2):
                    pe.wait_ge(xgT_ready, i * 4 + 2 * (s + 1))
                    pe.wait_ge(gu_loaded[s], i * 16 + 16)
                    for kt in range(KT):
                        for u in range(2):
                            last = mm(ps[64 * u:64 * u + 64, 0, 0:FF], xgT[:, kt, :], wgu[:, s, u, kt, :],
                                      start=kt == 0, stop=kt == KT - 1)
                    last.then_inc(gu_mm, 1)
                    turn_x(1 - s, i * 16 + 16 * (s + 1))
                    pe.wait_ge(gu_copied, i * 2 + s + 1)
                    for j in range(2):
                        last = tr(ps[:, 3, j * 128:(j + 1) * 128], gu_sb[:, j * 128:(j + 1) * 128], ident)
                    last.then_inc(at_mm, 1)
                    pe.wait_ge(act_ready, i * 2 + s + 1)
                    pe.wait_ge(dn_loaded[s], i * 16 + 16)
                    for j in range(2):
                        for b in range(2):
                            for half in range(2):
                                n = 2 * half + b
                                last = mm(ps[64 * half:64 * half + 64, 4 + 2 * s + b, :], actT[:, j, :],
                                          wdn[:, s, j, n * 512:(n + 1) * 512], start=j == 0, stop=j == 1)
                    last.then_inc(dn_mm, 1)

        @block.scalar
        def _(act):
            copy = nc.scalar.copy
            tiles = [(P, NORM_MEM), (P, NORM_MEM + 1)] + [(m, NORM_X + t) for t, (_, m) in enumerate(ROWS)]
            act.wait_ge(dset, 1)
            for n, (m, col) in enumerate(tiles):
                act.wait_ge(s_xst[n % 2], 16 * (n // 2 + 1))
                nc.scalar.activation(xst[0:m, n % 2], xst[0:m, n % 2], ACT.Square, accum_out=stat[0:m, col:col + 1]).then_inc(sumsq, 1)
            act.wait_ge(rs_ready, 1)
            for ch in range(2):
                for t in range(2):
                    act.wait_ge(gemm_done, ch * 2 + t + 1)
                    nc.scalar.activation((mk, mv)[ch][:, t], ps[:, 3 * ch + t, :], ACT.Copy,
                                         scale=st_rs[:, NORM_MEM + t:NORM_MEM + t + 1]).then_inc(z_ready, 1)

            def out(ch, s, done):
                for t, (_, m) in enumerate(ROWS):
                    act.wait_ge(gemm_done, done + t + 1)
                    nc.scalar.activation(z[0:m, ds(ch, 1), t, :], ps[0:m, 3 * s + t, :], ACT.Copy,
                                         scale=st_rs[0:m, NORM_X + t:NORM_X + t + 1]).then_inc(z_ready, 1)
            with act.Fori(0, NCHUNK // 2) as i:
                for s in range(2):
                    out(i * 2 + s, s, i * 6 + (4 + 3 * s))
            out(NCHUNK - 1, 0, 4 + 3 * (NCHUNK - 1))
            act.wait_ge(z_ready, 4 + 3 * NCHUNK)
            act.wait_ge(po, 2)
            nc.scalar.activation(z[:, C_U:C_VA + 1], z[:, C_U:C_VA + 1], ACT.Gelu).then_inc(gelu_done, 1)
            act.wait_ge(tab_cp, TABLE // 512)
            dst = [(mkT[:, g, :], NMEM) for g in range(G)] + [(qT[:, n, :], NT) for n in range(HP)] \
                + [(kT[:, n, :], NT) for n in range(HP)] + [(qmT[:, g, :], NT) for g in range(G)]
            for n, (d, w) in enumerate(dst):
                act.wait_ge(tr_done, n + 1)
                copy(d, ps[:, 6 + n % 2, 0:w]).then_inc(tr_used, 1)

            def memory_exp(r):
                act.wait_ge(mmx, r + 1)
                nc.scalar.activation(p_m[:, r], ps[:, 6, 256 * r:256 * r + 256], ACT.Exp, bias=st_m[:, 6 + r:7 + r], scale=S_MEM,
                                     accum_out=st_l[:, 6 + r:7 + r]).then_inc(mexp, 1)

            def memory_copy(r):
                act.wait_ge(mpt_mm, r + 1)
                copy(pt_m[:, r], ps[:, 7, 256 * r:256 * r + 256].rearrange("p (t n) -> p t n", t=2)).then_inc(mpt_ready, 1)

            def gate_out():
                for g in range(G):
                    act.wait_ge(gate_tr, g + 1)
                    copy(yT[:, g, :], ps[:, 7, 0:NT]).then_inc(gate_y, 1)

            between = {9: lambda: memory_exp(0), 10: lambda: memory_copy(0), 11: lambda: memory_exp(1),
                       12: lambda: memory_copy(1), 18: gate_out}
            for i in range(22):
                if i < 20:
                    act.wait_ge(mx_ready, i + 1)
                    b, w0, w = i % 3, *((128, 384) if i < H else (256, 512))
                    m = st_m[:, 2 * b:2 * b + 2]
                    l = st_l[:, 2 * b:2 * b + 2]
                    nc.scalar.activation(sc_p[b][:, 0:w0], sc_p[b][:, 0:w0], ACT.Exp, bias=m[:, 0:1], accum_out=l[:, 0:1])
                    nc.scalar.activation(sc_p[b][:, w0:w], sc_p[b][:, w0:w], ACT.Exp, bias=m[:, 1:2],
                                         accum_out=l[:, 1:2]).then_inc(exp_done, 1)
                if i in between:
                    between[i]()
                if i >= 2:
                    h = i - 2
                    w = 384 if h < H else 512
                    act.wait_ge(pt_mm, h + 1)
                    if h >= 2:
                        act.wait_ge(pv_mm, h - 1)
                    copy(pt_p[:, h % 2, 0:w], ps[:, 2 + h % 2, 0:w]).then_inc(pt_ready, 1)
            with act.Fori(0, NBATCH) as b:
                act.wait_ge(smx, b + 1)
                nc.scalar.activation(sc_s, sc_s, ACT.Exp, bias=st_m[:, 10:11], accum_out=st_l[:, 10:11]).then_inc(sexp, 1)
                for n in range(3):
                    act.wait_ge(spt_mm, b * 3 + n + 1)
                    if n < 2:
                        copy(pt_s[:, 4 * n:4 * n + 4], ps[:, 3 + n, :].rearrange("p (t n) -> p t n", t=4)).then_inc(spt_ready, 1)
                    else:
                        copy(pt_s[:, 8:10], ps[:, 5, 0:256].rearrange("p (t n) -> p t n", t=2))
                        copy(pt_s[0:64, 10], ps[0:64, 5, 256:384]).then_inc(spt_ready, 1)
            act.wait_ge(spv_mm, NBATCH)
            for t, (_, m) in enumerate(ROWS):
                act.wait_ge(h_ready, 10 + t)
                nc.scalar.activation(n2[0:m, t], hres[0:m, t], ACT.Square, accum_out=st_h[0:m, t:t + 1]).then_inc(sumsq, 1)
            for j in range(12):
                t, k4 = j // 4, j % 4
                r0, m = ROWS[t]
                act.wait_ge(n2_tr, j + 1)
                copy(n2T[:, 4 * k4:4 * k4 + 4, r0:r0 + m],
                     ps[:, j % 2, :].rearrange("p (k n) -> p k n", k=4)[:, :, 0:m]).then_inc(n2T_ready, 1)
            act.wait_ge(route_d, 1)
            nc.scalar.activation(dd, dd, ACT.Exp).then_inc(route_e, 1)

            act.wait_ge(routed, 1)
            pairs = act.value_load(cnt_i[0:1, 0:1], min_val=1, max_val=NBLK // 2)
            act.wait_ge(xg_tr, 1)
            copy(xgT[:, 8:16], ps[:, 2, :].rearrange("p (k n) -> p k n", k=8)).then_inc(xgT_ready, 1)
            with act.Fori(0, pairs) as i:
                for s in range(2):
                    act.wait_ge(xg_tr, i * 2 + s + 2)
                    copy(xgT[:, 8:16], ps[:, 2, :].rearrange("p (k n) -> p k n", k=8)).then_inc(xgT_ready, 1)
                    act.wait_ge(at_mm, i * 2 + s + 1)
                    nc.scalar.activation(sg, ps[:, 3, 0:256].rearrange("p (j n) -> p j n", j=2)[:, :, 0:BLOCK],
                                         ACT.Silu).then_inc(silu_done, 1)
                    act.wait_ge(dn_mm, i * 2 + s + 1)
                    act.wait_ge(y_free, i * 2 + s + 1)
                    copy(y_sb[:, s, 512:1024], ps[:, 5 + 2 * s, :]).then_inc(y_ready, 1)

        @block.vector
        def _(dve):
            link = Steps(dve, dv)
            V = nc.vector
            V.memset(stat[:, :], 1.0).then_inc(dset, 1)
            dve.wait_ge(s_cst, 16)
            dve.wait_ge(s_memt, 16)
            V.tensor_tensor(memT, memT, c("gmem").unsqueeze(2).to_broadcast([P, KT, NMEM]), ALU.mult).then_inc(xt_scaled, 1)
            for n in range(TABLE // 512):
                dve.wait_ge(tab_mm, n + 1)
                V.tensor_copy(table[:, n * 512:(n + 1) * 512], ps[0:H, 6 + n % 2, :]).then_inc(tab_cp, 1)
            dve.wait_ge(s_xt, 16)
            V.tensor_tensor(xT, xT, c("gmix").unsqueeze(2).to_broadcast([P, KT, NT]), ALU.mult).then_inc(xt_scaled, 1)
            dve.wait_ge(sumsq, 5)
            V.tensor_scalar(stat[:, 0:5], stat[:, 0:5], 1.0 / D, EPS, ALU.mult, ALU.add).then_inc(ms_ready, 1)
            for n in range(H // 2):
                dve.wait_ge(flip_mm, n + 1)
                V.tensor_copy(bias_p[:, 2 * n:2 * n + 2, :], ps[:, 6 + n % 2, :].rearrange("p (h n) -> p h n", h=2)).then_inc(flip_used, 1)

            state = {"n": 1}

            def norm(src, groups, e, gain, scratch, need):
                dve.wait_ge(z_ready, need)
                link(V.tensor_tensor(scratch, src, src, ALU.mult))
                link(V.tensor_reduce(st_n[:, 0:groups], scratch.rearrange("p n (h e) -> p (n h) e", e=e), X, ALU.add))
                V.tensor_scalar(st_n[:, 0:groups], st_n[:, 0:groups], 1.0 / e, EPS, ALU.mult, ALU.add).then_inc(ms_ready, 1)
                state["n"] += 1
                dve.wait_ge(rs_ready, state["n"])
                n = src.shape[1]
                for k in range(n):
                    v = src[:, k].rearrange("p (h e) -> p h e", e=e)
                    hh = COLS // e
                    rb = st_nr[:, k * hh:(k + 1) * hh].unsqueeze(2).to_broadcast([P, hh, e])
                    last = V.tensor_tensor(v, v, rb, ALU.mult)
                link(last)
                for k in range(n):
                    v = src[:, k].rearrange("p (h e) -> p h e", e=e)
                    hh = COLS // e
                    if gain[1] == COLS:
                        gb = gv[:, gain[0]:gain[0] + gain[1]].rearrange("p (h e) -> p h e", e=e)
                    else:
                        gb = gv[:, gain[0]:gain[0] + gain[1]].unsqueeze(1).to_broadcast([P, hh, e])
                    last = V.tensor_tensor(v, v, gb, ALU.mult)
                last.then_inc(normed, 1)

            def flat(ap):
                return ap.rearrange("p a t e -> p (a t) e")

            dve.wait_ge(s_gv, 16)
            dve.wait_ge(po, 2)
            dve.wait_ge(gemm_done, 4)
            norm(mk, 8, DG, GV["km"], area(A_Y, 2, COLS), 4)
            norm(flat(z[:, C_Q:C_Q + 2]), 48, DH, GV["qb"], area(A_Y, 6, COLS), 4 + 3 * 2)
            norm(flat(z[:, C_K:C_K + 2]), 48, DH, GV["kb"], area(A_Y, 6, COLS), 4 + 3 * 4)
            norm(flat(z[:, C_QM:C_QM + 1]), 12, DG, GV["qm"], area(A_Y, 3, COLS), 4 + 3 * 5)
            dve.wait_ge(gelu_done, 1)
            norm(flat(z[:, C_VA:C_VA + 1]), 12, DG, GV["av"], area(A_Y, 3, COLS), 4 + 3 * 9)

            def memory_pad(r):
                if r:
                    dve.wait_ge(msc_mm, r)
                V.tensor_copy(qmpad.rearrange("p (b h s) -> p b h s", b=4, h=4)[:, :, :, 0:8],
                              qmT[:, :, NPROMPT + 32 * r:NPROMPT + 32 * r + 32].rearrange("p h (b q) -> p b h q", b=4)
                              ).then_inc(pad_ready, 1)

            def memory_max(r):
                dve.wait_ge(msc_mm, r + 1)
                link(V.tensor_reduce(st_m[:, 8 + r:9 + r], ps[:, 6, 256 * r:256 * r + 256], X, ALU.max))
                V.tensor_scalar(st_m[:, 6 + r:7 + r], st_m[:, 8 + r:9 + r], -S_MEM, None, ALU.mult).then_inc(mmx, 1)

            def memory_mask(r):
                dve.wait_ge(mexp, r + 1)
                link(V.reciprocal(st_r[:, 6 + r:7 + r], st_l[:, 6 + r:7 + r]))
                dve.wait_ge(mpv_mm, r + 1)
                V.scalar_tensor_tensor(y_m, ps[:, 6, :], st_r[:, 6 + r:7 + r], c("mmask"), ALU.mult, ALU.mult).then_inc(m_masked, 1)

            def memory_out(r):
                dve.wait_ge(mfold_mm, r + 1)
                V.tensor_copy(yT[:, 12:16, NPROMPT + 32 * r:NPROMPT + 32 * r + 32],
                              ps[:, 7, 0:128].rearrange("p (h n) -> p h n", h=4)).then_inc(my_ready, 1)

            def gate():
                for g in range(G):
                    cols = slice(g * DG, (g + 1) * DG)
                    dve.wait_ge(gate_mm, g + 1)
                    V.scalar_tensor_tensor(z[:, C_U, 0:2, cols], ps[:, 6, 0:256].rearrange("p (t n) -> p t n", t=2),
                                           c("bs")[:, g:g + 1], z[:, C_U, 0:2, cols], ALU.add, ALU.mult)
                    V.scalar_tensor_tensor(z[0:64, C_U, 2, cols], ps[0:64, 6, 256:384],
                                           c("bss", 64)[:, g:g + 1], z[0:64, C_U, 2, cols], ALU.add, ALU.mult).then_inc(gated, 1)

            link(V.memset(qmpad, 0.0))
            between = {8: lambda: memory_pad(0), 9: lambda: (memory_max(0), memory_pad(1)), 11: lambda: memory_max(1),
                       13: lambda: memory_mask(0), 14: lambda: memory_out(0), 15: lambda: memory_mask(1), 16: lambda: memory_out(1), 18: gate}
            for i in range(24):
                if i < 20:
                    b = i % 3
                    dve.wait_ge(sc_mm, i + 1)
                    if i == 2:
                        dve.wait_ge(st_mem, 32)
                    w0, w = (128, 384) if i < H else (256, 512)
                    if i < H:
                        V.scalar_tensor_tensor(sc_p[b][:, 0:128], ps[:, i % 2, 0:128], S_WIN, bias_p[:, i, 128:256], ALU.mult, ALU.add)
                        last = V.scalar_tensor_tensor(sc_p[b][:, 128:384], ps[:, i % 2, 128:384], S_WIN, bias_p[:, i, :], ALU.mult, ALU.add)
                    else:
                        last = V.tensor_scalar(sc_p[b][:, :], ps[:, i % 2, :], S_MEM, None, ALU.mult)
                    last.then_inc(sc_read, 1)
                    dve.wait_ge(sc_read, i + 1)
                    V.tensor_reduce(st_m[:, 2 * b:2 * b + 1], sc_p[b][:, 0:w0], X, ALU.max, negate=True)
                    V.tensor_reduce(st_m[:, 2 * b + 1:2 * b + 2], sc_p[b][:, w0:w], X, ALU.max, negate=True).then_inc(mx_ready, 1)
                if i in between:
                    between[i]()
                if 1 <= i <= 20:
                    h = i - 1
                    b = h % 3
                    w0, w = (128, 384) if h < H else (256, 512)
                    dve.wait_ge(exp_done, h + 1)
                    link(V.reciprocal(st_r[:, 2 * b:2 * b + 2], st_l[:, 2 * b:2 * b + 2]))
                    V.tensor_scalar(sc_p[b][:, 0:w0], sc_p[b][:, 0:w0], st_r[:, 2 * b:2 * b + 1], None, ALU.mult)
                    V.tensor_scalar(sc_p[b][:, w0:w], sc_p[b][:, w0:w], st_r[:, 2 * b + 1:2 * b + 2], None, ALU.mult).then_inc(p_ready, 1)
                if i >= 4:
                    h = i - 4
                    dve.wait_ge(pv_mm, h + 1)
                    if h < H and h % 2 == 1:
                        V.tensor_copy(yT[:, 4 + h // 2, 0:256], ps[:, 4 + (h // 2) % 2, 0:256]).then_inc(y_used, 1)
                    if h >= H:
                        V.tensor_copy(yT[:, 12 + h - H, 0:256], ps[:, 4 + (h - H) % 2, 0:256]).then_inc(y_used, 1)
            V.memset(bias_s[:, PAST:PAST + 120], NEG).then_inc(dset, 1)
            dve.wait_ge(gate_tr, G)
            dve.wait_ge(st_va, 32)
            link(V.memset(qpad, 0.0))
            dve.wait_ge(bs_loaded, 16 * 16)

            def pad_q(b):
                for j in range(2):
                    r = slice(64 * j, 64 * j + 64)
                    last = V.tensor_copy(qpad.rearrange("p (h s) -> p h s", s=144)[r, :, 8 * j:8 * j + 8],
                                         qT[r, :, ds(b * 8 + NPROMPT, 8)])
                last.then_inc(qpad_ready, 1)

            def mask(b):
                V.scalar_tensor_tensor(y_s, ps[:, 6, 0:256], st_r[:, 10:11], c("wmask"), ALU.mult, ALU.mult).then_inc(s_masked, 1)

            def y_out(b):
                V.tensor_copy(yT[:, 4:12, ds(b * 8 + NPROMPT, 8)].rearrange("p (g j) q -> p j g q", j=2),
                              ps[:, 7, 0:64].rearrange("p (j g q) -> p j g q", j=2, g=4)).then_inc(y_copied, 1)

            bB = bias_s[:, 0:1536].rearrange("p (m s) -> p m s", s=16)[:, :, 0:8]

            def soften(b):
                dve.wait_ge(s_mm, b * 3 + 1)
                V.scalar_tensor_tensor(sc_s[:, 0:512], ps[:, 0, :], S_WIN, bias_s[:, 1536:2048], ALU.mult, ALU.add).then_inc(s_used, 1)
                dve.wait_ge(s_mm, b * 3 + 2)
                V.scalar_tensor_tensor(sc_s[:, 512:1024].rearrange("p (m s) -> p m s", s=8), ps[:, 1, :].rearrange("p (m s) -> p m s", s=8),
                                       S_WIN, bB[:, 0:64], ALU.mult, ALU.add).then_inc(s_used, 1)
                dve.wait_ge(s_mm, b * 3 + 3)
                V.scalar_tensor_tensor(sc_s[:, 1024:1280].rearrange("p (m s) -> p m s", s=8), ps[:, 2, 0:256].rearrange("p (m s) -> p m s", s=8),
                                       S_WIN, bB[:, 64:96], ALU.mult, ALU.add)
                V.scalar_tensor_tensor(sc_s[:, 1280:1344], ps[:, 2, 256:320], S_WIN, bias_s[:, ds(b * -8 + (PAST + 56), NSAMPLE)],
                                       ALU.mult, ALU.add).then_inc(s_used, 1)
                dve.wait_ge(s_used, b * 3 + 3)
                V.tensor_reduce(st_m[:, 10:11], sc_s, X, ALU.max, negate=True).then_inc(smx, 1)
                dve.wait_ge(sexp, b + 1)
                V.reciprocal(st_r[:, 10:11], st_l[:, 10:11]).then_inc(srec, 1)

            dve.sem_inc(s_masked, 1)
            pad_q(0)
            soften(0)
            with dve.Fori(1, NBATCH) as b:
                dve.wait_ge(s_mm, b * 3)
                pad_q(b)
                dve.wait_ge(srec, b)
                dve.wait_ge(spv_mm, b)
                mask(b - 1)
                soften(b)
                dve.wait_ge(fold_mm, b)
                y_out(b - 1)
            dve.wait_ge(srec, NBATCH)
            dve.wait_ge(spv_mm, NBATCH)
            mask(NBATCH - 1)
            dve.wait_ge(fold_mm, NBATCH)
            y_out(NBATCH - 1)
            dve.wait_ge(x_again, 48)
            V.memset(st_h, 1.0)
            for ch in range(4):
                for t, (_, m) in enumerate(ROWS):
                    dve.wait_ge(wo_done, 3 * ch + t + 1)
                    hh = hres[0:m, t, ch * 512:(ch + 1) * 512]
                    V.tensor_tensor(hh, ps[0:m, 3 * (ch % 2) + t, :], hh, ALU.add).then_inc(h_ready, 1)
            dve.wait_ge(sumsq, 8)
            V.tensor_scalar(st_h, st_h, 1.0 / D, EPS, ALU.mult, ALU.add).then_inc(ms_ready, 1)
            state["n"] += 1
            dve.wait_ge(rs_ready, state["n"])
            dve.wait_ge(x_again, 64)
            for t, (_, m) in enumerate(ROWS):
                V.scalar_tensor_tensor(n2[0:m, t], hres[0:m, t], st_hr[0:m, t:t + 1], gff[0:m, :], ALU.mult, ALU.mult).then_inc(n2_ready, 1)

            link(V.memset(area(R0, 120), -3e38))
            dve.wait_ge(logits, 1)
            lg = ps[:, 2, 0:108].rearrange("p (t n) -> p t n", t=3)
            for t, m in ((slice(0, 2), P), (slice(2, 3), 64)):
                V.tensor_copy(g8[0:m, t, 0:4], lg[0:m, t, 0:4])
                last = V.tensor_copy(el[0:m, t, :], lg[0:m, t, 4:36])
            link(last)
            for t in range(3):
                link(V.max(mx[:, t, :], g8[:, t, :]))
                link(V.max_index(mi[:, t, :], mx[:, t, :], g8[:, t, :]))
            link(V.tensor_copy(grp, mi[:, :, 0:1]))
            iota = c("iota")
            link(V.tensor_tensor(goh, iota[:, 0:4].unsqueeze(1).to_broadcast([P, 3, 4]), grp.to_broadcast([P, 3, 4]), ALU.is_equal))
            link(V.tensor_tensor(prod, el.rearrange("p t (g e) -> p t g e", g=4), goh.unsqueeze(3).to_broadcast([P, 3, 4, 8]), ALU.mult))
            link(V.tensor_reduce(esel, prod.rearrange("p t g e -> p t e g"), X, ALU.add))
            for t in range(3):
                link(V.max(top[:, t, :], esel[:, t, :]))
                link(V.max_index(ti[:, t, :], top[:, t, :], esel[:, t, :]))
            link(V.tensor_copy(tif, ti[:, :, 0:2]))
            link(V.scalar_tensor_tensor(eid, grp.to_broadcast([P, 3, 2]), float(EPG), tif, ALU.mult, ALU.add))
            for k in range(2):
                link(V.tensor_tensor(moh[:, k], iota[:, 0:32].unsqueeze(1).to_broadcast([P, 3, 32]),
                                     eid[:, :, k:k + 1].to_broadcast([P, 3, 32]), ALU.is_equal))
            link(V.memset(moh[64:128, :, 2, :], 0.0))
            V.tensor_tensor(asum, moh[:, 0], moh[:, 1], ALU.add).then_inc(onehots, 1)
            V.tensor_tensor(dd, top[:, :, 1:2], top[:, :, 0:1], ALU.subtract).then_inc(route_d, 1)
            dve.wait_ge(route_e, 1)
            link(V.tensor_scalar(w1p, dd, 1.0, None, ALU.add))
            link(V.reciprocal(wk[:, 0], w1p))
            link(V.tensor_tensor(wk[:, 1], dd, wk[:, 0], ALU.mult))
            dve.wait_ge(ranks, 1)
            link(V.tensor_copy(nb, ps[:, 3, 96:128]))
            link(V.tensor_tensor(cmp5, nb.unsqueeze(2).to_broadcast([P, 32, 5]),
                                 c("thr")[:, 0:5].unsqueeze(1).to_broadcast([P, 32, 5]), ALU.is_gt))
            link(V.tensor_reduce(nb, cmp5, X, ALU.add))
            link(V.memset(zer, 0.0))
            link(V.tensor_tensor_scan(incl, nb, zer, 0.0, ALU.add, ALU.add))
            link(V.tensor_tensor(base, incl, nb, ALU.subtract))
            for k in range(2):
                link(V.tensor_tensor(pick, moh[:, k], ps[:, 3, 0:96].rearrange("p (t e) -> p t e", t=3), ALU.mult))
                link(V.tensor_reduce(rankf[:, k], pick, X, ALU.add))
                link(V.tensor_tensor(pick, moh[:, k], base.unsqueeze(1).to_broadcast([P, 3, 32]), ALU.mult))
                link(V.tensor_reduce(basef[:, k], pick, X, ALU.add))
            link(V.tensor_tensor(ge4, rankf.unsqueeze(3).to_broadcast([P, 2, 3, 4]),
                                 c("thr")[:, 1:5].unsqueeze(1).unsqueeze(1).to_broadcast([P, 2, 3, 4]), ALU.is_ge))
            link(V.tensor_reduce(fullf, ge4, X, ALU.add))
            link(V.scalar_tensor_tensor(slotf, rankf, float(NTAB), basef, ALU.mult, ALU.add))
            link(V.scalar_tensor_tensor(slotf, fullf, float(1 - BLOCK * NTAB), slotf, ALU.mult, ALU.add))
            link(V.tensor_copy(slot_u, slotf))
            link(V.tensor_copy(pair_u, c("pairs").rearrange("p (k t f) -> p k t f", k=2, t=3)))
            link(V.tensor_tensor(cmpb, incl.unsqueeze(1).to_broadcast([P, NBLK, 32]),
                                 iota[:, 0:NBLK].unsqueeze(2).to_broadcast([P, NBLK, 32]), ALU.is_le))
            link(V.tensor_reduce(ebf, cmpb, X, ALU.add))
            link(V.tensor_scalar(ebf, ebf, float(NEXP - 1), None, ALU.min))
            link(V.tensor_copy(eblk_i, ebf))
            link(V.tensor_scalar(cntf[:, 0:1], incl[:, 31:32], 0.5, 0.25, ALU.mult, ALU.add))
            V.tensor_copy(cnt_i[:, 0:1], cntf[:, 0:1]).then_inc(routed, 1)
            dve.wait_ge(routed, 1)

            pairs = dve.value_load(cnt_i[0:1, 0:1], min_val=1, max_val=NBLK // 2)
            dve.wait_ge(xg_tr, 1)
            V.tensor_copy(xgT[:, 0:8], ps[:, 1, :].rearrange("p (k n) -> p k n", k=8)).then_inc(xgT_ready, 1)
            with dve.Fori(0, pairs) as i:
                for s in range(2):
                    dve.wait_ge(gu_mm, i * 2 + s + 1)
                    V.tensor_copy(gu_sb, ps[:, 0, 0:FF]).then_inc(gu_copied, 1)
                    dve.wait_ge(xg_tr, i * 2 + s + 2)
                    V.tensor_copy(xgT[:, 0:8], ps[:, 1, :].rearrange("p (k n) -> p k n", k=8)).then_inc(xgT_ready, 1)
                    dve.wait_ge(silu_done, i * 2 + s + 1)
                    V.tensor_tensor(actT, sg, ps[:, 3, 0:256].rearrange("p (j n) -> p j n", j=2)[:, :, BLOCK:2 * BLOCK],
                                    ALU.mult).then_inc(act_ready, 1)
                    dve.wait_ge(dn_mm, i * 2 + s + 1)
                    dve.wait_ge(y_free, i * 2 + s + 1)
                    V.tensor_copy(y_sb[:, s, 0:512], ps[:, 4 + 2 * s, :]).then_inc(y_ready, 1)
            for t, (_, m) in enumerate(ROWS):
                dve.wait_ge(back[t], 32)
                for k in range(2):
                    last = V.scalar_tensor_tensor(hres[0:m, t], yg[0:m, k, t], wk[0:m, k, t], hres[0:m, t], ALU.mult, ALU.add)
                    if k == 0:
                        last.then_inc(moe_dv, 1)
                        dve.wait_ge(moe_dv, t + 1)
                last.then_inc(final, 1)

        @block.gpsimd
        def _(pool):
            g = nc.gpsimd
            pool.dma_start(relb[:, :], relb_d).then_inc(s_relb, 16)
            pool.dma_start(onehot[:, :], onehot_d).then_inc(s_relb, 16)
            g.memset(nhalf[:, :], -0.5).then_inc(po, 1)
            pool.dma_start(tab_d, empty_d).then_inc(tab_zero, 16)
            pool.wait_ge(tab_cp, TABLE // 512)
            pool.dma_start(bias_d, table[:, :]).then_inc(tab_out, 16)
            def rsqrt(n, out, in_):
                pool.wait_ge(ms_ready, n)
                g.tensor_tensor(out, in_, nhalf[:, 0:in_.shape[1]], ALU.pow).then_inc(rs_ready, 1)
            pool.wait_ge(po, 1)
            rsqrt(1, st_rs[:, 0:5], stat[:, 0:5])
            pool.wait_ge(rs_ready, 1)
            pool.wait_ge(flip_mm, H // 2)
            g.memset(z[64:128, :, 2, :], 0.0).then_inc(po, 1)
            pool.wait_ge(z_ready, 4)
            pool.dma_start(o_mv.rearrange("(t p) n -> p t n", p=P), mv).then_inc(st_mem, 16)
            rsqrt(2, st_nr[:, 0:8], st_n[:, 0:8])
            pool.wait_ge(normed, 1)
            pool.dma_start(o_mk.rearrange("(t p) n -> p t n", p=P), mk).then_inc(st_mem, 16)
            rsqrt(3, st_nr[:, 0:48], st_n[:, 0:48])
            rsqrt(4, st_nr[:, 0:48], st_n[:, 0:48])
            pool.wait_ge(normed, 3)

            for a in range(2):
                pool.dma_start(o_k[0:256, a * 512:(a + 1) * 512].rearrange("(t p) n -> p t n", p=P), z[:, C_K + a, 0:2, :]).then_inc(st_k, 16)
            pool.dma_start(o_k[256:320, :].rearrange("p (a n) -> p a n", a=2), z[0:64, C_K:C_K + 2, 2, :]).then_inc(st_k, 16)
            rsqrt(5, st_nr[:, 0:12], st_n[:, 0:12])
            pool.wait_ge(z_ready, 4 + 3 * 7)
            for a in range(2):
                pool.dma_start(o_v[0:256, a * 512:(a + 1) * 512].rearrange("(t p) n -> p t n", p=P), z[:, C_V + a, 0:2, :]).then_inc(st_v, 16)
            pool.dma_start(o_v[256:320, :].rearrange("p (a n) -> p a n", a=2), z[0:64, C_V:C_V + 2, 2, :]).then_inc(st_v, 16)
            rsqrt(6, st_nr[:, 0:12], st_n[:, 0:12])
            pool.wait_ge(normed, 5)
            pool.dma_start(o_va[0:128, :], z[:, C_VA, 1, :]).then_inc(st_va, 16)
            pool.dma_start(o_va[128:192, :], z[0:64, C_VA, 2, :]).then_inc(st_va, 16)
            rsqrt(7, st_hr[:, 0:3], st_h[:, 0:3])
            pool.wait_ge(routed, 1)
            pool.wait_ge(tab_zero, 16)
            for k in range(2):
                for t, (_, m) in enumerate(ROWS):
                    pool.indirect_dma_start(tab_d, bass.IndirectOffsetOnAxis(ap=slot_u[0:m, k, t:t + 1], axis=0),
                                            pair_u[0:m, k, t, :], None).then_inc(slots_out, 16)
            pool.wait_ge(slots_out, 16 * 6)
            pool.wait_ge(n2_stored, 48)
            pool.wait_ge(st_mem, 32)
            pool.wait_ge(st_k, 48)
            pool.wait_ge(st_v, 48)
            pool.wait_ge(st_va, 32)
            for half in range(2):
                pool.dma_start(idx_all[64 * half:64 * half + 64], tab_d.rearrange("(p n) f -> p n f", p=BLOCK)).then_inc(idx_in, 16)
            pool.wait_ge(idx_in, 32)
            for s in range(2):
                g.tensor_copy(row_cur[s], idx_all[0:BLOCK, s, 0:1]).then_inc(idx_cp, 1)
            g.tensor_scalar(idx_all[64:128, :, 1], idx_all[64:128, :, 1], 1.0, None, ALU.add).then_inc(idx_cp, 1)
            pool.wait_ge(idx_cp, 3)
            for s in range(2):
                pool.indirect_dma_start(xg[0:BLOCK, s, :], None, n2_d, bass.IndirectOffsetOnAxis(ap=row_cur[s], axis=0)).then_inc(gathered[s], 16)
            pairs = pool.value_load(cnt_i[0:1, 0:1], min_val=1, max_val=NBLK // 2)
            g.sem_inc(y_free, 1)
            with pool.Fori(0, pairs) as i:
                for s in range(2):
                    pool.wait_ge(xg_tr, i * 2 + s + 1)
                    pool.wait_ge(gathered[s], i * 16 + 16)
                    g.tensor_copy(row_cur[s], idx_all[0:BLOCK, ds(i * 2 + s + 2, 1), 0]).then_inc(idx_cp, 1)
                    g.tensor_copy(dst_cur[s], idx_all[:, ds(i * 2 + s, 1), 1]).then_inc(idx_cp, 1)
                    pool.wait_ge(idx_cp, i * 4 + (2 * s + 5))
                    g.sem_inc(pool_seen, 1)
                    pool.indirect_dma_start(xg[0:BLOCK, s, :], None, n2_d, bass.IndirectOffsetOnAxis(ap=row_cur[s], axis=0)).then_inc(gathered[s], 16)
                    pool.wait_ge(y_ready, i * 4 + 2 * (s + 1))
                    g.sem_inc(pool_seen, 1)
                    pool.indirect_dma_start(y_d, bass.IndirectOffsetOnAxis(ap=dst_cur[s], axis=0), y_sb[:, s, :], None,
                                            bounds_check=4 * NT - 1, oob_is_err=False).then_inc(y_stored[s], 16)
                    pool.wait_ge(y_stored[1 - s], i * 16 + 16 * s)
                    g.sem_inc(y_free, 1)
            for s in range(2):
                pool.wait_ge(y_stored[s], pairs * 16)
                pool.wait_ge(gathered[s], pairs * 16 + 16)
            pool.wait_ge(dn_mm, pairs * 2)
            g.sem_inc(pool_seen, 1)
            for t, (r0, m) in enumerate(ROWS):
                for k in range(2):
                    pool.dma_start(yg[0:m, k, t, :].rearrange("p (a n) -> p a n", a=2),
                                   y_d[2 * (k * NT + r0):2 * (k * NT + r0 + m), :].rearrange("(p a) n -> p a n", a=2)).then_inc(back[t], 16)
            for t, (r0, m) in enumerate(ROWS):
                pool.wait_ge(final, t + 1)
                pool.dma_start(o_y[r0:r0 + m, :], hres[0:m, t]).then_inc(st_y, 16)
            pool.wait_ge(st_y, 48)


def distance_bucket(dist):
    d = np.maximum(dist, 0)
    exact = 16
    df = np.maximum(d, 1).astype(np.float32)
    large = exact + (np.log(df / np.float32(exact)) / np.float32(math.log(2048 / exact)) * np.float32(16)).astype(np.int32)
    return np.where(d < exact, d, np.minimum(large, 31))


def constants():
    dist = DIST0 - np.arange(TABLE)
    count = sum(((dist >= 0) & (dist <= w) & (dist % dl == 0)).astype(int) for w, dl in ((128, 1), (512, 4), (2048, 16)))
    onehot = np.zeros((33, TABLE), np.float32)
    onehot[distance_bucket(dist), np.arange(TABLE)] = 1
    onehot[32] = np.where(count > 0, np.log(np.maximum(count, 1)), NEG)
    c = {n: np.zeros((P, w), np.float32) for n, (_, w) in CST.items()}
    c["ident"][:] = np.eye(P)
    c["flip"][:] = np.eye(P)[::-1]
    c["ones"][:] = 1
    c["ltri"][:] = np.triu(np.ones((P, P)), 1)
    c["iota"][:] = np.arange(64)
    h, q = np.divmod(np.arange(P), NQ)
    c["wmask"][:] = (h % 4)[:, None] == np.arange(256) // DH
    c["wsel"][:] = h[:, None] // 4 * NQ + q[:, None] == np.arange(32)
    b, h = h // G, h % G
    c["mmask"][:] = h[:, None] == np.arange(512) // DG
    c["msel"][:] = b[:, None] * NQ + q[:, None] == np.arange(32)
    c["thr"][:, 0:5] = np.arange(5) * BLOCK
    tok = np.arange(P)[:, None] + np.array([r0 for r0, _ in ROWS])
    c["pairs"][:] = np.stack([np.stack([tok, 2 * (k * NT + tok)], axis=-1) for k in range(2)], axis=1).reshape(P, 12)
    return onehot, c


def kernel(**inputs):
    import concourse.bacc as _bacc
    from concourse.bass_utils import run_bass_kernel_spmd as _run

    a = {k: np.asarray(v) for k, v in inputs.items()}
    onehot, c = constants()
    x = np.concatenate([a["x_prompt"].reshape(NPROMPT, D), a["x_sample"].reshape(NSAMPLE, D)])
    mem = a["mem_prompt"].reshape(NMEM, D)

    def columns(t):
        return np.ascontiguousarray(t.reshape(-1, KT, P).transpose(2, 1, 0))

    def chunks(w):
        return w.reshape(QTR, K4, P, COLS).transpose(0, 2, 1, 3).reshape(QTR, P, K4 * COLS)

    w_in, w_kv, w_out = a["w_in"][0], a["w_mem_kv"][0], a["w_out"][0]
    starts = [1024, 1536, 2048, 2560, 4096, 3072, 3584, 0, 512]
    w_proj = np.stack([chunks(w_kv[:, 0:512]), chunks(w_kv[:, 512:1024])] + [chunks(w_in[:, s:s + 512]) for s in starts])
    w_o = np.stack([chunks(w_out[:, n * 512:(n + 1) * 512]) for n in range(4)])

    def reached(cache):
        late = cache[:, PAST - KEYS_A:]
        early = cache[:, 0:PAST - KEYS_A].reshape(NBATCH, 96, 16, H, DH)[:, :, 0:8].reshape(NBATCH, KEYS_B, H, DH)
        return np.concatenate([late, early], axis=1)

    k = reached(a["cache_win_k"][0]).reshape(NBATCH, KEYS, HP, 128).transpose(0, 3, 2, 1)
    kc = np.concatenate([k[..., s:e].reshape(NBATCH, P, -1) for s, e in ((0, 512), (512, 1024), (1024, 1280))], axis=2)
    v = reached(a["cache_win_v"][0]).reshape(NBATCH, VT, P, H * DH).transpose(0, 2, 1, 3)
    vc = np.ascontiguousarray(v).reshape(NBATCH, P, VT * 1024)
    mkc = a["cache_mem_k"][0].reshape(2, 4, NMEM, G, DG).transpose(4, 0, 1, 3, 2).reshape(P, 2, 16, NMEM)
    mvc = a["cache_mem_v"][0].reshape(2, 4, 2, P, G * DG).transpose(3, 0, 1, 2, 4)

    c["gmix"][:] = a["g_mix"][0].reshape(KT, P).T
    c["gmem"][:] = a["g_mem"][0].reshape(KT, P).T
    c["bs"][:] = a["b_s"][0].T
    c["bss"][0:NSAMPLE] = np.tile(a["b_s"][0][:, 0:NQ].T, (NBATCH, 1))
    wr = np.concatenate([a["w_router_group"][0]] + [a["w_router_expert"][0, g] for g in range(NGRP)], axis=1)
    c["wr"][:] = wr.reshape(KT, P, 36).transpose(1, 0, 2).reshape(P, -1)
    wst = np.zeros((P, G, P), np.float32)
    wsbd = np.zeros((P, G, NSAMPLE), np.float32)
    for t in range(P):
        wst[0:t + 1, :, t] = a["w_s"][0][:, t, 0:t + 1].T
    for b in range(NBATCH):
        wsbd[b * NQ:(b + 1) * NQ, :, b * NQ:(b + 1) * NQ] = wst[0:NQ, :, 0:NQ]
    c["wst"][:] = wst.reshape(P, -1)
    c["wsbd"][:] = wsbd.reshape(P, -1)
    gv = np.concatenate([a["g_qb"][0], a["g_kb"][0], a["g_qm"][0], a["g_km"][0], a["g_av"][0].reshape(-1)])
    relb = np.concatenate([a["rel_bias"], np.ones((1, H), np.float32)])
    w_gu = np.stack([a["w_gate"][0], a["w_up"][0]], axis=1).reshape(NEXP, 2, KT, P, FF).transpose(0, 3, 1, 2, 4)
    w_dn = a["w_down"][0].reshape(NEXP, 2, P, D).transpose(0, 2, 1, 3)

    ins = {
        "x_rows": x, "mem_rows": mem, "x_t": columns(x), "mem_t": columns(mem), "w_proj": w_proj, "w_o": w_o,
        "kc": kc, "vc": vc, "mkc": mkc, "mvc": mvc, "cst_d": np.concatenate([c[n] for n in CST], axis=1),
        "gv_d": gv, "gffn_d": a["g_ffn"][0], "relb_d": relb, "onehot_d": onehot, "w_gu": w_gu, "w_dn": w_dn,
        "empty_d": np.tile(np.array([[0, 4 * NT]], np.uint32), (NTAB * BLOCK, 1)),
    }
    outs = {"o_y": (NT, D), "o_k": (NT, 1024), "o_v": (NT, 1024), "o_va": (192, 512), "o_mk": (NMEM, 512), "o_mv": (NMEM, 512)}
    scratch = {"bias_d": ((H, TABLE), F32), "n2_d": ((NT, D), F32), "tab_d": ((NTAB * BLOCK, 2), U32), "y_d": ((4 * NT, D // 2), F32)}

    nc = _bacc.Bacc("TRN2", target_bir_lowering=False, num_devices=1)
    arrays, args = {}, []
    for name, v in ins.items():
        arrays[name] = np.ascontiguousarray(v)
        args.append(nc.dram_tensor(name, arrays[name].shape, mybir.dt.from_np(arrays[name].dtype), kind="ExternalInput").ap())
    for name, shape in outs.items():
        args.append(nc.dram_tensor(name, shape, F32, kind="ExternalOutput").ap())
    for name, (shape, dt) in scratch.items():
        args.append(nc.dram_tensor(name, shape, dt, kind="Internal").ap())
    hybrid_step(nc, *args)
    r = _run(nc, [arrays], core_ids=[0]).results[0]

    y, k, v, va = r["o_y"], r["o_k"], r["o_v"], r["o_va"]
    return (y[0:256].reshape(1, 256, D), y[256:].reshape(NBATCH, NQ, D),
            k[0:256].reshape(1, 1, 256, H, DH), v[0:256].reshape(1, 1, 256, H, DH),
            va[0:128].reshape(1, 1, 128, G, DG), r["o_mk"].reshape(1, 1, NMEM, G, DG), r["o_mv"].reshape(1, 1, NMEM, G, DG),
            k[256:].reshape(1, NBATCH, NQ, H, DH), v[256:].reshape(1, NBATCH, NQ, H, DH),
            va[128:].reshape(1, NBATCH, NQ, G, DG))
```

```python
import math
from contextlib import ExitStack

import numpy as np

import concourse.bass as bass
from concourse import mybir

F32 = mybir.dt.float32
U32 = mybir.dt.uint32
I32 = mybir.dt.int32
ALU = mybir.AluOpType
ACT = mybir.ActivationFunctionType
X = mybir.AxisListType.X
ds = bass.ds

P = 128
D = 2048
KT = D // P
NPROMPT, NBATCH, NQ = 256, 8, 8
NSAMPLE = NBATCH * NQ
NT = NPROMPT + NSAMPLE
ROWS = [(0, 128), (128, 128), (256, 64)]
H, DH = 16, 64
HP = H // 2
G, DG = 4, 128
NMEM = 256
PAST = 2048
EPS = 1e-6
NEG = -1e30
COLS = 512
QTR = 4
K4 = KT // QTR
NCHUNK = 9
C_Q, C_K, C_QM, C_V, C_U, C_VA = 0, 2, 4, 5, 7, 8
KEYS_A, KEYS_B = 512, 768
KEYS = KEYS_A + KEYS_B
VT = KEYS // P
NKEY = KEYS + NSAMPLE
DIST0 = PAST + NQ - 1
TABLE = 2560
NEXP, NGRP, EPG, FF = 32, 4, 8, 256
BLOCK = 64
UNROLL = 2
NMORE = (2 * NT - 2) // BLOCK + 1
NMORE += -NMORE % UNROLL
NBLK = NEXP + NMORE
NTAB = NBLK + 2
S_WIN = DH ** -0.5
S_MEM = DG ** -0.5

CST = {}
_at = 0
for _n, _w in (("ident", 128), ("flip", 128), ("ones", 128), ("ltri", 128), ("iota", 64), ("thr", 8), ("pairs", 12),
               ("gmix", 16), ("gmem", 16), ("bs", 4), ("bss", 4), ("wr", KT * 36), ("wst", 4 * 128), ("wsbd", 4 * 64),
               ("wmask", 256), ("wsel", 32), ("mmask", 512), ("msel", 32)):
    CST[_n] = (_at, _w)
    _at += _w
NCST = _at
GV = {"qb": (0, 64), "kb": (64, 64), "qm": (128, 128), "km": (256, 128), "av": (384, 512)}


class Steps:

    def __init__(self, eng, sem):
        self.eng, self.sem, self.base, self.n = eng, sem, 0, 0

    def __call__(self, ins):
        self.n += 1
        ins.then_inc(self.sem, 1)
        self.eng.wait_ge(self.sem, self.base + self.n)


def hybrid_step(nc, x_rows, mem_rows, x_t, mem_t, w_proj, w_o, kc, vc, mkc, mvc, cst_d, gv_d, gffn_d,
                relb_d, onehot_d, w_gu, w_dn, empty_d, o_y, o_k, o_v, o_va, o_mk, o_mv,
                bias_d, bias_q_d, n2_d, tab_d, y_d):
    with ExitStack() as ctx:
        def sb(name, shape, dt=F32):
            return ctx.enter_context(nc.sbuf_tensor(name, shape, dt))

        def sem(name):
            return ctx.enter_context(nc.semaphore(name))

        cst = sb("cst", [P, NCST])
        gv = sb("gv", [P, 896])
        stat = sb("stat", [P, 256])
        nhalf = sb("nhalf", [P, 48])
        idx = sb("idx", [P, 24], U32)
        ARENA = 49152
        arena = sb("arena", [P, ARENA])
        ps = ctx.enter_context(nc.psum_tensor("ps", [P, 8, 512], F32))

        def c(name, rows=P):
            a, w = CST[name]
            return cst[0:rows, a:a + w]

        def area(at, *dims):
            n = int(np.prod(dims))
            ap = arena[:, at:at + n]
            if len(dims) == 1:
                return ap
            names = "abcdef"[:len(dims)]
            return ap.rearrange(f"p ({' '.join(names)}) -> p {' '.join(names)}",
                                **{k: v for k, v in zip(names, dims)})

        ident = c("ident")
        wr = c("wr").rearrange("p (k n) -> p k n", k=KT)
        wst = c("wst").rearrange("p (g n) -> p g n", g=G)
        wsbd = c("wsbd").rearrange("p (g n) -> p g n", g=G)
        W_RING = KT * COLS
        A_W, A_XT = 0, W_RING
        A_Z = A_XT + KT * NT
        A_BP = A_Z + NCHUNK * 3 * COLS
        A_KV = A_BP + H * 256
        A_QT = A_KV + 2048
        A_KT = A_QT + HP * NT
        A_QMT = A_KT + HP * NT
        A_MKT = A_QMT + G * NT
        A_Y = A_MKT + G * NMEM
        A_BS = A_Y + KT * NT
        A_END = A_BS + 2176
        assert A_END <= ARENA, A_END
        wring = area(A_W, QTR, K4, COLS)
        xT = area(A_XT, KT, NT)
        z = area(A_Z, NCHUNK, 3, COLS)
        bias_p = area(A_BP, H, 256)
        mk = area(A_KV, 2, COLS)
        mv = area(A_KV + 1024, 2, COLS)
        qT = area(A_QT, HP, NT)
        kT = area(A_KT, HP, NT)
        qmT = area(A_QMT, G, NT)
        mkT = area(A_MKT, G, NMEM)
        memT = area(A_Y, KT, NMEM)
        yT = area(A_Y, KT, NT)
        bias_s = area(A_BS, 2168)
        xst = area(A_QT, 2, D)
        bias_r = area(A_Z + C_V * 3 * COLS, H, 256)
        onehot = area(A_QT + 2 * D, TABLE)[0:33, :]
        relb = area(A_QT + 2 * D + TABLE, H)[0:33, :]
        table = area(A_BP, TABLE)[0:H, :]
        sc_p = [area(A_BS, 512), area(A_BS + 512, 512), mk[:, 0, :]]
        pt_p = area(A_BS + 1024, 2, 512)
        qmpad = area(A_END, 4 * 160)
        p_m = area(A_END + 640, 2, 256)
        pt_m = area(A_Y, 2, 2, P)
        y_m = area(A_Y + 512, COLS)
        kA = area(0, HP, 512)
        kB1 = area(4096, HP, 512)
        kB2 = area(8192, HP, 256)
        vbuf = area(HP * KEYS, VT, 1024)
        assert 2 * HP * KEYS <= A_Z + C_V * 3 * COLS
        mkb = area(0, 2, 16, NMEM)
        mvb = area(10240, 2, 4, 2, COLS)
        A_RB = A_Z + C_U * 3 * COLS
        sc_s = area(A_RB, NKEY)
        pt_s = area(A_RB + 1344, 11, P)
        qpad = area(A_RB + 1344 + 1408, HP * 144)
        y_s = area(A_RB + 3904, 256)
        assert 3904 + 256 <= 2 * 3 * COLS + 4096
        EW = 2 * KT * FF + 2 * D
        A_EW = [W_RING + EW * s for s in range(UNROLL)]
        wgu = [area(at, 2, KT, FF) for at in A_EW]
        wdn = [area(at + 2 * KT * FF, 2, D) for at in A_EW]
        A_H = W_RING + UNROLL * EW
        hres = area(A_H, 3, D)
        assert A_H + 3 * D <= A_Y
        n2 = area(A_EW[1], 3, D)
        n2T = area(A_EW[1] + 3 * D, KT, NT)
        assert 3 * D <= 2 * KT * FF and 3 * D + KT * NT <= EW
        squares = area(A_H + 3 * D, COLS)
        lgT = area(A_H + 3 * D + COLS, NT)[0:36, :]
        assert A_H + 3 * D + COLS + NT <= A_Y
        gff = area(A_BS, D)
        xg = area(A_Y, 2, D)
        xgT = area(A_Y + 2 * D, KT, BLOCK)
        assert A_Y + 2 * D + KT * BLOCK <= A_BS
        gu_sb = area(0, FF)
        sg = area(256, 2, BLOCK)
        actT = area(384, 2, BLOCK)
        y_sb = area(512, 2, 1024)
        A_I = A_BS + D
        eblk_i = area(A_I, NBLK).bitcast(I32)
        cnt_i = area(A_I + 64, 8).bitcast(I32)
        idx_all = area(A_I + 72, 2 * NTAB).bitcast(U32).rearrange("p (n f) -> p n f", f=2)
        assert A_I + 72 + 2 * NTAB <= ARENA
        R0 = 3 * D
        g8 = area(R0, 3, 8)
        el = area(R0 + 24, 3, 32)
        mx = area(R0 + 120, 3, 8)
        mi = area(R0 + 144, 3, 8).bitcast(U32)
        grp = area(R0 + 168, 3, 1)
        goh = area(R0 + 171, 3, 4)
        prod = area(R0 + 183, 3, 4, 8)
        esel = area(R0 + 279, 3, 8)
        top = area(R0 + 303, 3, 8)
        ti = area(R0 + 327, 3, 8).bitcast(U32)
        tif = area(R0 + 351, 3, 2)
        eid = area(R0 + 357, 3, 2)
        moh = area(R0 + 363, 2, 3, 32)
        asum = area(R0 + 555, 3, 32)
        cmp4 = area(R0 + 651, 32, 4)
        nb = area(R0 + 811, 32)
        zer = area(R0 + 843, 32)
        incl = area(R0 + 875, 32)
        base = area(R0 + 907, 32)
        ge4 = area(R0 + 939, 2, 3, 4)
        rankf = area(R0 + 963, 2, 3)
        basef = area(R0 + 969, 2, 3)
        fullf = area(R0 + 975, 2, 3)
        pick = area(R0 + 1035, 3, 32)
        slotf = area(R0 + 1131, 2, 3)
        dd = area(R0 + 1137, 3, 1)
        w1p = area(R0 + 1140, 3, 1)
        wk = area(R0 + 1143, 2, 3, 1)
        cmpb = area(R0 + 1149, NMORE, 32)
        ebf = area(R0 + 1149 + NMORE * 32, NMORE)
        cntf = area(R0 + 1149 + NMORE * 33, 8)
        assert R0 + 1149 + NMORE * 33 + 8 <= W_RING
        yg = area(A_EW[0], 2, 3, D)
        slot_u = idx[:, 0:6].rearrange("p (k t) -> p k t", k=2)
        pair_u = idx[:, 8:20].rearrange("p (k t f) -> p k t f", k=2, t=3)
        row_cur = [idx[0:BLOCK, 20 + s:21 + s] for s in range(2)]
        dst_cur = [idx[:, 22 + s:23 + s] for s in range(2)]

        s_cst, s_gv, s_relb = sem("s_cst"), sem("s_gv"), sem("s_relb")
        s_xst = [sem(f"s_xst{i}") for i in range(2)]
        s_xt, s_memt = sem("s_xt"), sem("s_memt")
        w_loaded = [sem(f"w_loaded{i}") for i in range(QTR)]
        w_used, gemm_done, z_ready = sem("w_used"), sem("gemm_done"), sem("z_ready")
        dv, po = sem("dv"), sem("po")
        pe_seen, pool_seen = sem("pe_seen"), sem("pool_seen")
        flip_mm, flip_used = sem("flip_mm"), sem("flip_used")
        dset, mem_scaled, xt_scaled, sumsq, ms_ready, rs_ready = sem("dset"), sem("mem_scaled"), sem("xt_scaled"), sem("sumsq"), sem("ms_ready"), sem("rs_ready")
        tab_mm, tab_cp, tab_out, rows_out, bp_loaded, bs_loaded = sem("tab_mm"), sem("tab_cp"), sem("tab_out"), sem("rows_out"), sem("bp_loaded"), sem("bs_loaded")
        normed, gelu_done, tr_done, tr_used = sem("normed"), sem("gelu_done"), sem("tr_done"), sem("tr_used")
        st_mem, st_k, st_v, st_va, y_stored_out = (sem(n) for n in ("st_mem", "st_k", "st_v", "st_va", "y_stored_out"))
        sc_read, y_free, srec, route_d, route_e = (sem(n) for n in (
            "sc_read", "y_free", "srec", "route_d", "route_e"))
        sc_mm, mx_ready, exp_done, p_ready, pt_mm, pt_ready, pv_mm, y_used = (sem(n) for n in (
            "sc_mm", "mx_ready", "exp_done", "p_ready", "pt_mm", "pt_ready", "pv_mm", "y_used"))
        gate_mm, gated, gate_tr, gate_y = sem("gate_mm"), sem("gated"), sem("gate_tr"), sem("gate_y")
        pad_ready, mkb_loaded, mvb_loaded, msc_mm, mmx, mexp, mpt_mm, mpt_ready, mpv_mm, m_masked, mfold_mm, my_ready = (sem(n) for n in (
            "pad_ready", "mkb_loaded", "mvb_loaded", "msc_mm", "mmx", "mexp", "mpt_mm", "mpt_ready", "mpv_mm", "m_masked", "mfold_mm", "my_ready"))
        k_loaded = [sem(f"k_loaded{i}") for i in range(3)]
        v_loaded, qpad_ready, s_mm, s_used, smx, sexp, spt_mm, spt_ready, spv_mm, s_masked, fold_mm, y_copied = (sem(n) for n in (
            "v_loaded", "qpad_ready", "s_mm", "s_used", "smx", "sexp", "spt_mm", "spt_ready", "spv_mm", "s_masked", "fold_mm", "y_copied"))
        wo_loaded = [sem(f"wo_loaded{i}") for i in range(QTR)]
        wo_used, wo_done, x_again, h_ready = sem("wo_used"), sem("wo_done"), sem("x_again"), sem("h_ready")
        n2_ready, n2_tr, n2T_ready, logits, routed, n2_stored, tab_zero, slots_out, idx_in = (sem(n) for n in (
            "n2_ready", "n2_tr", "n2T_ready", "logits", "routed", "n2_stored", "tab_zero", "slots_out", "idx_in"))
        g_ready, lgT_mm, lgT_ready, onehots, ranks, slots_ready = (sem(n) for n in (
            "g_ready", "lgT_mm", "lgT_ready", "onehots", "ranks", "slots_ready"))
        gu_loaded = [sem(f"gu_loaded{i}") for i in range(UNROLL)]
        dn_loaded = [sem(f"dn_loaded{i}") for i in range(UNROLL)]
        gathered = [sem(f"gathered{s}") for s in range(2)]
        xg_tr, xgT_ready, gu_mm, gu_copied, at_mm, silu_done, act_ready, dn_mm, y_ready = (sem(n) for n in (
            "xg_tr", "xgT_ready", "gu_mm", "gu_copied", "at_mm", "silu_done", "act_ready", "dn_mm", "y_ready"))
        y_stored = [sem(f"y_stored{s}") for s in range(2)]
        back = [[sem(f"back{t}_{k}") for k in range(2)] for t in range(3)]
        final, moe_dv, idx_cp = sem("final"), sem("moe_dv"), sem("idx_cp")

        NORM_X, NORM_MEM = 0, 3
        st_rs = stat[:, 8:16]
        st_n = stat[:, 16:64]
        st_nr = stat[:, 64:112]
        st_m = stat[:, 112:124]
        st_l = stat[:, 124:136]
        st_r = stat[:, 136:148]
        st_hq = stat[:, 160:172]
        st_h = stat[:, 148:151]
        st_hr = stat[:, 152:155]

        block = ctx.enter_context(nc.Block())

        @block.sync
        def _(sp):
            sp.dma_start(cst[:, :], cst_d).then_inc(s_cst, 16)
            sp.dma_start(memT, mem_t).then_inc(s_memt, 16)
            for q in range(QTR):
                sp.dma_start(wring[:, q], w_proj[0, q]).then_inc(w_loaded[q], 16)
            for n in range(2):
                sp.dma_start(xst[:, n], mem_rows[n * P:(n + 1) * P, :]).then_inc(s_xst[n], 16)
            for n, (r0, m) in enumerate(ROWS):
                sp.wait_ge(sumsq, n + 1)
                sp.dma_start(xst[0:m, n % 2], x_rows[r0:r0 + m, :]).then_inc(s_xst[n % 2], 16)
                if m < P:
                    sp.dma_start(xst[m:2 * m, n % 2], x_rows[r0:r0 + m, :]).then_inc(s_xst[n % 2], 16)
            def next_chunk(ch, before):
                for q in range(QTR):
                    if q < QTR - 1:
                        sp.wait_ge(w_used, (ch - 1) * (QTR - 1) + q + 1)
                    else:
                        sp.wait_ge(gemm_done, before)
                    sp.dma_start(wring[:, q], w_proj[ds(ch, 1), q]).then_inc(w_loaded[q], 16)
            next_chunk(1, 2)
            sp.dma_start(xT, x_t).then_inc(s_xt, 16)
            sp.dma_start(gv[:, :], gv_d.partition_broadcast(P)).then_inc(s_gv, 16)
            sp.wait_ge(tab_out, 16)
            sp.dma_start(bias_r, bass.AP(tensor=bias_d.tensor, offset=DIST0 - 255, ap=[[1, P], [TABLE, H], [1, 256]])
                         ).then_inc(bp_loaded, 16)
            with sp.Fori(2, NCHUNK + 2) as ch:
                next_chunk(ch, ch * 3 - 2)
            sp.wait_ge(gemm_done, 4 + 3 * NCHUNK)
            sp.dma_start(mkb, mkc).then_inc(mkb_loaded, 16)
            sp.wait_ge(tr_done, 24)
            sp.wait_ge(st_k, 48)
            sp.dma_start(mvb, mvc).then_inc(mvb_loaded, 16)
            sp.wait_ge(msc_mm, 2)
            for n, (kp, a, b) in enumerate(((kA, 0, 4096), (kB1, 4096, 8192), (kB2, 8192, 10240))):
                sp.dma_start(kp, kc[0, :, a:b]).then_inc(k_loaded[n], 16)
            sp.wait_ge(mpv_mm, 2)
            sp.dma_start(vbuf, vc[0]).then_inc(v_loaded, 16)
            with sp.Fori(1, NBATCH) as b:
                for n, (kp, a, e) in enumerate(((kA, 0, 4096), (kB1, 4096, 8192), (kB2, 8192, 10240))):
                    sp.wait_ge(s_mm, (b - 1) * 3 + n + 1)
                    sp.dma_start(kp, kc[ds(b, 1), :, a:e]).then_inc(k_loaded[n], 16)
                sp.wait_ge(spv_mm, b)
                sp.dma_start(vbuf, vc[ds(b, 1)]).then_inc(v_loaded, 16)
            sp.wait_ge(s_mm, 3 * NBATCH)
            for q in range(QTR):
                sp.dma_start(wring[:, q], w_o[0, q]).then_inc(wo_loaded[q], 16)
            sp.wait_ge(fold_mm, NBATCH)
            sp.wait_ge(st_v, 48)
            for n, (r0, m) in enumerate(ROWS):
                sp.dma_start(hres[0:m, n], x_rows[r0:r0 + m, :]).then_inc(x_again, 16)
            sp.dma_start(gff, gffn_d.partition_broadcast(P)).then_inc(x_again, 16)
            for ch in range(1, 4):
                for q in range(QTR):
                    if q < QTR - 1:
                        sp.wait_ge(wo_used, (ch - 1) * (QTR - 1) + q + 1)
                    else:
                        sp.wait_ge(wo_done, ch * 3)
                    sp.dma_start(wring[:, q], w_o[ch, q]).then_inc(wo_loaded[q], 16)
                    if q == 0 and ch == 1:
                        sp.dma_start(wgu[0], w_gu[0]).then_inc(gu_loaded[0], 16)
                    if q == 2 and ch == 1:
                        sp.dma_start(wdn[0], w_dn[0]).then_inc(dn_loaded[0], 16)
            sp.wait_ge(logits, 1)
            sp.dma_start(wdn[1], w_dn[1]).then_inc(dn_loaded[1], 16)
            for n, (r0, m) in enumerate(ROWS):
                sp.wait_ge(n2_ready, n + 1)
                sp.dma_start(n2_d[r0:r0 + m, :], n2[0:m, n]).then_inc(n2_stored, 16)
            for r in range(2):
                sp.wait_ge(gathered[r], 16)
            sp.wait_ge(n2_stored, 48)
            sp.dma_start(wgu[1], w_gu[1]).then_inc(gu_loaded[1], 16)
            sp.wait_ge(routed, 1)
            steps = sp.value_load(cnt_i[0:1, 0:1], min_val=NEXP // UNROLL, max_val=NBLK // UNROLL)
            with sp.Fori(1, steps) as i:
                for s in range(UNROLL):
                    e = sp.value_load(eblk_i[0:1, ds(i * UNROLL + s, 1)], min_val=0, max_val=NEXP - 1)
                    sp.wait_ge(gu_mm, i * UNROLL + (s + 1 - UNROLL))
                    sp.dma_start(wgu[s], w_gu[ds(e, 1)]).then_inc(gu_loaded[s], 16)
                    sp.wait_ge(dn_mm, i * UNROLL + (s + 1 - UNROLL))
                    sp.dma_start(wdn[s], w_dn[ds(e, 1)]).then_inc(dn_loaded[s], 16)

        @block.tensor
        def _(pe):
            mm, tr = nc.tensor.matmul, nc.tensor.transpose
            def tile_product(bank, t, m, src, q):
                for k in range(K4):
                    kt = q * K4 + k
                    if m == P:
                        last = mm(ps[:, bank + t, :], src(kt), wring[:, q, k, :], start=kt == 0, stop=kt == KT - 1)
                    else:
                        for j in range(2):
                            last = mm(ps[64 * j:64 * j + 64, bank + t, 0:256], src(kt), wring[:, q, k, 256 * j:256 * j + 256],
                                      start=kt == 0, stop=kt == KT - 1)
                return last

            def chunk(bank, src, rows, load_value, scaled=None):
                for q in range(QTR):
                    pe.wait_ge(w_loaded[q], load_value)
                    if scaled is not None:
                        pe.wait_ge(scaled, q + 1)
                    for t, (r0, m) in enumerate(rows):
                        last = tile_product(bank, t, m, lambda kt: src[:, kt, r0:r0 + m], q)
                        if q == QTR - 1:
                            last.then_inc(gemm_done, 1)
                    if q < QTR - 1:
                        last.then_inc(w_used, 1)

            chunk(0, memT, ROWS[:2], 16, mem_scaled)
            pe.wait_ge(s_relb, 32)
            for n in range(TABLE // 512):
                if n >= 2:
                    pe.wait_ge(tab_cp, n - 1)
                mm(ps[0:H, 6 + n % 2, :], relb[:, :], onehot[:, n * 512:(n + 1) * 512], start=True, stop=True).then_inc(tab_mm, 1)
            chunk(3, memT, ROWS[:2], 32)
            pe.wait_ge(bp_loaded, 16)
            pe.wait_ge(tab_cp, TABLE // 512)
            for n in range(H // 2):
                if n >= 2:
                    pe.wait_ge(flip_used, n - 1)
                mm(ps[:, 6 + n % 2, :], c("flip"), bias_r[:, 2 * n:2 * n + 2, :], start=True, stop=True).then_inc(flip_mm, 1)
            pe.wait_ge(xt_scaled, 1)
            pe.wait_ge(z_ready, 4)
            with pe.Fori(0, NCHUNK // 2) as i:
                for s in range(2):
                    pe.wait_ge(z_ready, i * 6 + (4 + 3 * (s - 1)))
                    chunk(3 * s, xT, ROWS, i * 32 + 16 * (s + 3))
            pe.wait_ge(z_ready, 4 + 3 * (NCHUNK - 2))
            chunk(0, xT, ROWS, 16 * (NCHUNK + 2))

            def turn(n, src, rows):
                if n >= 4:
                    pe.wait_ge(tr_used, n - 3)
                for t, (r0, m) in enumerate(rows):
                    last = tr(ps[:, 4 + n % 4, r0:r0 + m], src(t)[0:m, :], ident[0:m, 0:m])
                last.then_inc(tr_done, 1)
            pe.wait_ge(flip_used, H // 2)
            pe.wait_ge(z_ready, 4 + 3 * (NCHUNK - 1))
            n = 0
            pe.wait_ge(normed, 1)
            for g in range(G):
                turn(n, lambda t: mk[:, t, g * DG:(g + 1) * DG], ROWS[:2])
                n += 1
            pe.wait_ge(normed, 4)
            for ch, pairs in ((C_Q, HP), (C_K, HP), (C_QM, G)):
                for hp in range(pairs):
                    turn(n, lambda t: z[:, ch + hp // 4, t, (hp % 4) * P:(hp % 4 + 1) * P], ROWS)
                    n += 1
            pe.wait_ge(tr_used, n)
            pe.wait_ge(z_ready, 4 + 3 * NCHUNK)

            def scores(h):
                if h >= 2:
                    pe.wait_ge(sc_read, h - 1)
                b = h % 2
                if h < H:
                    r = slice(64 * (h % 2), 64 * (h % 2) + 64)
                    mm(ps[:, b, 0:128], qT[r, h // 2, 0:128], kT[r, h // 2, 0:128], start=True, stop=True)
                    mm(ps[:, b, 128:384], qT[r, h // 2, 128:256], kT[r, h // 2, 0:256], start=True, stop=True).then_inc(sc_mm, 1)
                else:
                    g = h - H
                    mm(ps[:, b, 0:256], qmT[:, g, 0:128], mkT[:, g, :], start=True, stop=True)
                    mm(ps[:, b, 256:512], qmT[:, g, 128:256], mkT[:, g, :], start=True, stop=True).then_inc(sc_mm, 1)

            def turn_p(h):
                b = 2 + h % 2
                pe.wait_ge(p_ready, h + 1)
                if h >= 2:
                    pe.wait_ge(pt_ready, h - 1)
                p = sc_p[h % 3]
                if h < H:
                    tr(ps[:, b, 0:128], p[:, 0:128], ident)
                    tr(ps[:, b, 128:256], p[:, 128:256], ident)
                    tr(ps[:, b, 256:384], p[:, 256:384], ident).then_inc(pt_mm, 1)
                else:
                    tr(ps[:, b, 0:128], p[:, 0:128], ident)
                    tr(ps[:, b, 128:256], p[:, 256:384], ident)
                    tr(ps[:, b, 256:384], p[:, 128:256], ident)
                    tr(ps[:, b, 384:512], p[:, 384:512], ident).then_inc(pt_mm, 1)

            def values(h):
                pe.wait_ge(pt_ready, h + 1)
                pt = pt_p[:, h % 2]
                if h < H:
                    hp, r = h // 2, slice(64 * (h % 2), 64 * (h % 2) + 64)
                    b = 4 + hp % 2
                    if h % 2 == 0 and hp >= 2:
                        pe.wait_ge(y_used, hp - 1)
                    v = [z[:, C_V + h // 8, t, (h % 8) * DH:(h % 8 + 1) * DH] for t in range(2)]
                    mm(ps[r, b, 0:256], v[0], pt[:, 0:256], start=True, stop=False, skip_group_check=True)
                    mm(ps[r, b, 128:256], v[1], pt[:, 256:384], start=False, stop=True, skip_group_check=True).then_inc(pv_mm, 1)
                else:
                    g = h - H
                    b = 4 + g % 2
                    pe.wait_ge(y_used, HP + g - 1)
                    mm(ps[:, b, 0:256], mv[:, 0, g * DG:(g + 1) * DG], pt[:, 0:256], start=True, stop=False)
                    mm(ps[:, b, 0:256], mv[:, 1, g * DG:(g + 1) * DG], pt[:, 256:512], start=False, stop=True).then_inc(pv_mm, 1)

            def gate_products(g):
                if g == 0:
                    pe.wait_ge(normed, 5)
                    pe.wait_ge(m_masked, 2)
                else:
                    pe.wait_ge(gated, g)
                cols = slice(g * DG, (g + 1) * DG)
                for t in range(2):
                    mm(ps[:, 6, t * 128:(t + 1) * 128], wst[:, g, :], z[:, C_VA, t, cols], start=True, stop=True)
                mm(ps[0:64, 6, 256:384], wsbd[0:64, g, :], z[0:64, C_VA, 2, cols], start=True, stop=True).then_inc(gate_mm, 1)

            def gate_turn(g):
                pe.wait_ge(gated, g + 1)
                pe.wait_ge(gate_y, g) if g else pe.wait_ge(my_ready, 2)
                for t, (r0, m) in enumerate(ROWS):
                    last = tr(ps[:, 7, r0:r0 + m], z[0:m, C_U, t, g * DG:(g + 1) * DG], ident[0:m, 0:m])
                last.then_inc(gate_tr, 1)

            def memory_scores(r):
                pe.wait_ge(pad_ready, r + 1)
                if r == 0:
                    pe.wait_ge(mkb_loaded, 16)
                else:
                    pe.wait_ge(mexp, r)
                for h in range(G):
                    for b in range(4):
                        last = mm(ps[32 * b:32 * b + 32, 6, 256 * r:256 * r + 256], qmpad[:, b * 160 + h * 32:b * 160 + h * 32 + 32],
                                  mkb[:, r, 4 * b + h, :], start=h == 0, stop=h == 3)
                last.then_inc(msc_mm, 1)

            def memory_turn(r):
                pe.wait_ge(mexp, r + 1)
                if r:
                    pe.wait_ge(mpt_ready, r)
                for t in range(2):
                    last = tr(ps[:, 7, r * 256 + t * 128:r * 256 + (t + 1) * 128], p_m[:, r, t * 128:(t + 1) * 128], ident)
                last.then_inc(mpt_mm, 1)

            def memory_values(r):
                pe.wait_ge(mpt_ready, r + 1)
                pe.wait_ge(mvb_loaded, 16)
                pe.wait_ge(m_masked, r) if r else pe.wait_ge(mexp, 2)
                for t in range(2):
                    for b in range(4):
                        last = mm(ps[32 * b:32 * b + 32, 6, :], pt_m[:, r, t, 32 * b:32 * b + 32], mvb[:, r, b, t, :],
                                  start=t == 0, stop=t == 1)
                last.then_inc(mpv_mm, 1)

            def memory_fold(r):
                pe.wait_ge(m_masked, r + 1)
                pe.wait_ge(my_ready, r) if r else pe.wait_ge(mpt_ready, 2)
                for h in range(G):
                    last = mm(ps[:, 7, 32 * h:32 * h + 32], y_m[:, h * 128:(h + 1) * 128], c("msel"), start=True, stop=True)
                last.then_inc(mfold_mm, 1)

            between = {4: lambda: memory_scores(0), 5: lambda: memory_turn(0), 6: lambda: memory_scores(1),
                       7: lambda: memory_turn(1), 8: lambda: memory_values(0), 9: lambda: memory_fold(0),
                       10: lambda: memory_values(1), 11: lambda: memory_fold(1), 12: lambda: gate_products(0),
                       13: lambda: (gate_turn(0), gate_products(1)), 14: lambda: (gate_turn(1), gate_products(2)),
                       15: lambda: (gate_turn(2), gate_products(3)), 16: lambda: gate_turn(3)}
            for i in range(20 + 3):
                if i < 20:
                    scores(i)
                if i in between:
                    between[i]()
                if 2 <= i <= 21:
                    turn_p(i - 2)
                if i >= 3:
                    values(i - 3)
            pe.wait_ge(y_used, HP + G)
            pe.wait_ge(gate_y, G)

            def qk(b):
                pe.wait_ge(qpad_ready, b + 1)
                for n, (kp, w) in enumerate(((kA, 512), (kB1, 512), (kB2, 256))):
                    pe.wait_ge(k_loaded[n], b * 16 + 16)
                    if type(b) is not int:
                        pe.wait_ge(s_used, (b - 1) * 3 + n + 1)
                    for half in range(2):
                        for g in range(4):
                            hp = 2 * g + half
                            last = mm(ps[32 * g:32 * g + 32, n, 0:w], qpad[:, hp * 128 + 32 * g:hp * 128 + 32 * g + 32],
                                      kp[:, hp, :], start=half == 0, stop=half == 1)
                    if n == 2:
                        for half in range(2):
                            for g in range(4):
                                hp = 2 * g + half
                                last = mm(ps[32 * g:32 * g + 32, n, w:w + NSAMPLE],
                                          qpad[:, hp * 128 + 32 * g:hp * 128 + 32 * g + 32],
                                          kT[:, hp, NPROMPT:NT], start=half == 0, stop=half == 1)
                    last.then_inc(s_mm, 1)

            def turn_s(b):
                pe.wait_ge(sexp, b + 1)
                if type(b) is not int:
                    pe.wait_ge(spt_ready, b * 3)
                for t in range(11):
                    w = 128 if t < VT else NSAMPLE
                    last = tr(ps[0:w, 3 + t // 4, (t % 4) * 128:(t % 4) * 128 + 128], sc_s[:, t * 128:t * 128 + w], ident)
                    if t in (3, 7, 10):
                        last.then_inc(spt_mm, 1)

            def pv(turned, loaded, free):
                pe.wait_ge(spt_ready, turned)
                pe.wait_ge(v_loaded, loaded)
                pe.wait_ge(s_masked, free)
                for t in range(VT + 1):
                    for g in range(4):
                        if t < VT:
                            v, w = vbuf[:, t, g * 256:(g + 1) * 256], P
                        else:
                            v, w = z[0:NSAMPLE, C_V + g // 2, 2, (g % 2) * 256:(g % 2 + 1) * 256], NSAMPLE
                        last = mm(ps[32 * g:32 * g + 32, 6, 0:256], pt_s[0:w, t, 32 * g:32 * g + 32], v, start=t == 0, stop=t == VT)
                last.then_inc(spv_mm, 1)

            def fold(masked):
                pe.wait_ge(s_masked, masked)
                for j in range(2):
                    last = mm(ps[:, 7, 32 * j:32 * j + 32], y_s[:, j * 128:(j + 1) * 128], c("wsel"), start=True, stop=True)
                last.then_inc(fold_mm, 1)

            qk(0)
            turn_s(0)
            with pe.Fori(1, NBATCH) as b:
                pv(b * 3, b * 16, b)
                qk(b)
                fold(b + 1)
                turn_s(b)
            pv(3 * NBATCH, 16 * NBATCH, NBATCH)
            fold(NBATCH + 1)
            pe.wait_ge(y_copied, NBATCH)

            def turn_n2(ch):
                for t, (r0, m) in enumerate(ROWS):
                    pe.wait_ge(g_ready, 3 * ch + t + 1)
                    for k in range(4):
                        kt = 4 * ch + k
                        last = tr(ps[:, 3 * (ch % 2) + t, k * 128:k * 128 + m], n2[0:m, t, kt * 128:(kt + 1) * 128], ident[0:m, 0:m])
                    last.then_inc(n2_tr, 1)

            def route_sums(ch):
                pe.wait_ge(n2T_ready, 3 * ch + 3)
                for k in range(4):
                    kt = 4 * ch + k
                    last = mm(ps[0:36, 7, 0:NT], wr[:, kt, :], n2T[:, kt, :], start=kt == 0, stop=kt == KT - 1)
                return last

            def out_chunk(ch):
                for q in range(QTR):
                    pe.wait_ge(wo_loaded[q], 16 * (ch + 1))
                    for t, (r0, m) in enumerate(ROWS):
                        last = tile_product(3 * (ch % 2), t, m, lambda kt: yT[:, kt, r0:r0 + m], q)
                        if q == QTR - 1:
                            last.then_inc(wo_done, 1)
                    if q < QTR - 1:
                        last.then_inc(wo_used, 1)
                    if ch and q == 1:
                        turn_n2(ch - 1)
                    if ch and q == 2:
                        route_sums(ch - 1)
            for ch in range(4):
                out_chunk(ch)
            turn_n2(3)
            route_sums(3).then_inc(lgT_mm, 1)
            pe.wait_ge(lgT_ready, 1)
            for t, (r0, m) in enumerate(ROWS):
                last = tr(ps[0:m, 6, t * 36:(t + 1) * 36], lgT[:, r0:r0 + m], ident[0:36, 0:36])
            last.then_inc(logits, 1)
            pe.wait_ge(onehots, 1)
            for t in range(3):
                mm(ps[:, 3, t * 32:(t + 1) * 32], c("ltri"), asum[:, t, :], start=True, stop=t == 0)
                for u in range(t):
                    mm(ps[:, 3, t * 32:(t + 1) * 32], c("ones"), asum[:, u, :], start=False, stop=u == t - 1)
            for t in range(3):
                last = mm(ps[:, 3, 96:128], c("ones"), asum[:, t, :], start=t == 0, stop=t == 2)
            last.then_inc(ranks, 1)

            def turn_x(s, value):
                pe.wait_ge(gathered[s], value)
                pe.sem_inc(pe_seen, 1)
                for kt in range(KT):
                    last = tr(ps[:, 1 + kt // 8, (kt % 8) * 64:(kt % 8) * 64 + 64], xg[0:BLOCK, s, kt * 128:(kt + 1) * 128],
                              ident[0:BLOCK, 0:BLOCK])
                last.then_inc(xg_tr, 1)

            pe.wait_ge(routed, 1)
            steps = pe.value_load(cnt_i[0:1, 0:1], min_val=NEXP // UNROLL, max_val=NBLK // UNROLL)
            turn_x(0, 16)
            with pe.Fori(0, steps) as i:
                for s in range(UNROLL):
                    r = s % 2
                    pe.wait_ge(xgT_ready, i * (2 * UNROLL) + 2 * (s + 1))
                    pe.wait_ge(gu_loaded[s], i * 16 + 16)
                    for kt in range(KT):
                        for u in range(2):
                            last = mm(ps[64 * u:64 * u + 64, 0, 0:FF], xgT[:, kt, :], wgu[s][:, u, kt, :],
                                      start=kt == 0, stop=kt == KT - 1)
                    last.then_inc(gu_mm, 1)
                    turn_x(1 - r, i * (8 * UNROLL) + 16 * ((s + 1) // 2 + 1))
                    pe.wait_ge(gu_copied, i * UNROLL + s + 1)
                    for j in range(2):
                        last = tr(ps[:, 3, j * 128:(j + 1) * 128], gu_sb[:, j * 128:(j + 1) * 128], ident)
                    last.then_inc(at_mm, 1)
                    pe.wait_ge(act_ready, i * UNROLL + s + 1)
                    pe.wait_ge(dn_loaded[s], i * 16 + 16)
                    for j in range(2):
                        for b in range(2):
                            for half in range(2):
                                n = 2 * half + b
                                last = mm(ps[64 * half:64 * half + 64, 4 + 2 * r + b, :], actT[:, j, :],
                                          wdn[s][:, j, n * 512:(n + 1) * 512], start=j == 0, stop=j == 1)
                    last.then_inc(dn_mm, 1)

        @block.scalar
        def _(act):
            copy = nc.scalar.copy
            tiles = [(P, NORM_MEM), (P, NORM_MEM + 1)] + [(P, NORM_X + t) for t in range(len(ROWS))]
            act.wait_ge(dset, 1)
            for n, (m, col) in enumerate(tiles):
                act.wait_ge(s_xst[n % 2], 16 * (n // 2 + 1 + (n == 4)))
                nc.scalar.activation(xst[0:m, n % 2], xst[0:m, n % 2], ACT.Square, accum_out=stat[0:m, col:col + 1]).then_inc(sumsq, 1)
            act.wait_ge(rs_ready, 1)
            for ch in range(2):
                for t in range(2):
                    act.wait_ge(gemm_done, ch * 2 + t + 1)
                    nc.scalar.activation((mk, mv)[ch][:, t], ps[:, 3 * ch + t, :], ACT.Copy,
                                         scale=st_rs[:, NORM_MEM + t:NORM_MEM + t + 1]).then_inc(z_ready, 1)

            def out(ch, s, done):
                for t, (_, m) in enumerate(ROWS):
                    act.wait_ge(gemm_done, done + t + 1)
                    for j in range(P // m):
                        w = COLS * m // P
                        last = nc.scalar.activation(z[0:m, ds(ch, 1), t, w * j:w * j + w], ps[m * j:m * j + m, 3 * s + t, 0:w], ACT.Copy,
                                                    scale=st_rs[m * j:m * j + m, NORM_X + t:NORM_X + t + 1])
                    last.then_inc(z_ready, 1)
            with act.Fori(0, NCHUNK // 2) as i:
                for s in range(2):
                    out(i * 2 + s, s, i * 6 + (4 + 3 * s))
            out(NCHUNK - 1, 0, 4 + 3 * (NCHUNK - 1))
            act.wait_ge(z_ready, 4 + 3 * NCHUNK)
            act.wait_ge(po, 2)
            nc.scalar.activation(z[:, C_U:C_VA + 1], z[:, C_U:C_VA + 1], ACT.Gelu).then_inc(gelu_done, 1)
            act.wait_ge(tab_cp, TABLE // 512)
            dst = [(mkT[:, g, :], NMEM) for g in range(G)] + [(qT[:, n, :], NT) for n in range(HP)] \
                + [(kT[:, n, :], NT) for n in range(HP)] + [(qmT[:, g, :], NT) for g in range(G)]
            for n, (d, w) in enumerate(dst):
                act.wait_ge(tr_done, n + 1)
                copy(d, ps[:, 4 + n % 4, 0:w]).then_inc(tr_used, 1)

            def memory_exp(r):
                act.wait_ge(mmx, r + 1)
                nc.scalar.activation(p_m[:, r], ps[:, 6, 256 * r:256 * r + 256], ACT.Exp, bias=st_m[:, 6 + r:7 + r], scale=S_MEM,
                                     accum_out=st_l[:, 6 + r:7 + r]).then_inc(mexp, 1)

            def memory_copy(r):
                act.wait_ge(mpt_mm, r + 1)
                copy(pt_m[:, r], ps[:, 7, 256 * r:256 * r + 256].rearrange("p (t n) -> p t n", t=2)).then_inc(mpt_ready, 1)

            def gate_out(g):
                act.wait_ge(gate_tr, g + 1)
                copy(yT[:, g, :], ps[:, 7, 0:NT]).then_inc(gate_y, 1)

            between = {4: lambda: memory_exp(0), 5: lambda: memory_copy(0), 6: lambda: memory_exp(1),
                       7: lambda: memory_copy(1), 13: lambda: gate_out(0), 14: lambda: gate_out(1),
                       15: lambda: gate_out(2), 16: lambda: gate_out(3)}
            for i in range(22):
                if i < 20:
                    act.wait_ge(mx_ready, i + 1)
                    b, w0, w = i % 3, *((128, 384) if i < H else (256, 512))
                    m = st_m[:, 2 * b:2 * b + 2]
                    l = st_l[:, 2 * b:2 * b + 2]
                    nc.scalar.activation(sc_p[b][:, 0:w0], sc_p[b][:, 0:w0], ACT.Exp, bias=m[:, 0:1], accum_out=l[:, 0:1])
                    nc.scalar.activation(sc_p[b][:, w0:w], sc_p[b][:, w0:w], ACT.Exp, bias=m[:, 1:2],
                                         accum_out=l[:, 1:2]).then_inc(exp_done, 1)
                if i in between:
                    between[i]()
                if i >= 2:
                    h = i - 2
                    w = 384 if h < H else 512
                    act.wait_ge(pt_mm, h + 1)
                    if h >= 2:
                        act.wait_ge(pv_mm, h - 1)
                    copy(pt_p[:, h % 2, 0:w], ps[:, 2 + h % 2, 0:w]).then_inc(pt_ready, 1)
            act.wait_ge(pv_mm, 20)
            act.wait_ge(dset, 2)
            act.wait_ge(rows_out, 16 * NQ)
            act.dma_start(bias_s[:, 0:PAST], bias_q_d[:, 0:PAST]).then_inc(bs_loaded, 16)
            act.dma_start(bias_s[:, PAST + 56:PAST + 64], bias_q_d[:, PAST:PAST + NQ]).then_inc(bs_loaded, 16)
            with act.Fori(0, NBATCH) as b:
                act.wait_ge(smx, b + 1)
                nc.scalar.activation(sc_s, sc_s, ACT.Exp, bias=st_m[:, 10:11], accum_out=st_l[:, 10:11]).then_inc(sexp, 1)
                for n in range(3):
                    act.wait_ge(spt_mm, b * 3 + n + 1)
                    if n < 2:
                        copy(pt_s[:, 4 * n:4 * n + 4], ps[:, 3 + n, :].rearrange("p (t n) -> p t n", t=4)).then_inc(spt_ready, 1)
                    else:
                        copy(pt_s[:, 8:10], ps[:, 5, 0:256].rearrange("p (t n) -> p t n", t=2))
                        copy(pt_s[0:64, 10], ps[0:64, 5, 256:384]).then_inc(spt_ready, 1)
            for ch in range(4):
                for t, (_, m) in enumerate(ROWS):
                    act.wait_ge(h_ready, 3 * ch + t + 1)
                    act.wait_ge(sumsq, 5 + 3 * ch + t)
                    nc.scalar.activation(squares[0:m, :], hres[0:m, t, ch * COLS:(ch + 1) * COLS], ACT.Square,
                                         accum_out=st_hq[0:m, 3 * ch + t:3 * ch + t + 1]).then_inc(sumsq, 1)
                for t, (r0, m) in enumerate(ROWS):
                    act.wait_ge(n2_tr, 3 * ch + t + 1)
                    copy(n2T[:, 4 * ch:4 * ch + 4, r0:r0 + m],
                         ps[:, 3 * (ch % 2) + t, :].rearrange("p (k n) -> p k n", k=4)[:, :, 0:m]).then_inc(n2T_ready, 1)
            act.wait_ge(lgT_mm, 1)
            copy(lgT, ps[0:36, 7, 0:NT]).then_inc(lgT_ready, 1)
            act.wait_ge(rs_ready, 7)
            for t, (_, m) in enumerate(ROWS):
                nc.scalar.activation(n2[0:m, t], n2[0:m, t], ACT.Copy, scale=st_hr[0:m, t:t + 1]).then_inc(n2_ready, 1)
            act.wait_ge(route_d, 1)
            nc.scalar.activation(dd, dd, ACT.Exp).then_inc(route_e, 1)

            act.wait_ge(routed, 1)
            steps = act.value_load(cnt_i[0:1, 0:1], min_val=NEXP // UNROLL, max_val=NBLK // UNROLL)
            act.wait_ge(xg_tr, 1)
            copy(xgT[:, 8:16], ps[:, 2, :].rearrange("p (k n) -> p k n", k=8)).then_inc(xgT_ready, 1)
            with act.Fori(0, steps) as i:
                for s in range(UNROLL):
                    act.wait_ge(xg_tr, i * UNROLL + s + 2)
                    copy(xgT[:, 8:16], ps[:, 2, :].rearrange("p (k n) -> p k n", k=8)).then_inc(xgT_ready, 1)
                    act.wait_ge(at_mm, i * UNROLL + s + 1)
                    nc.scalar.activation(sg, ps[:, 3, 0:256].rearrange("p (j n) -> p j n", j=2)[:, :, 0:BLOCK],
                                         ACT.Silu).then_inc(silu_done, 1)
                    act.wait_ge(dn_mm, i * UNROLL + s + 1)
                    act.wait_ge(y_free, i * UNROLL + s + 1)
                    copy(y_sb[:, s % 2, 512:1024], ps[:, 5 + 2 * (s % 2), :]).then_inc(y_ready, 1)

        @block.vector
        def _(dve):
            link = Steps(dve, dv)
            V = nc.vector
            V.memset(stat[:, :], 1.0).then_inc(dset, 1)
            dve.wait_ge(s_cst, 16)
            dve.wait_ge(s_memt, 16)
            for q in range(QTR):
                part = memT[:, q * K4:(q + 1) * K4]
                V.tensor_tensor(part, part, c("gmem")[:, q * K4:(q + 1) * K4].unsqueeze(2).to_broadcast([P, K4, NMEM]),
                                ALU.mult).then_inc(mem_scaled, 1)
            dve.wait_ge(sumsq, 5)
            V.tensor_scalar(stat[:, 0:5], stat[:, 0:5], 1.0 / D, EPS, ALU.mult, ALU.add).then_inc(ms_ready, 1)
            for n in range(TABLE // 512):
                dve.wait_ge(tab_mm, n + 1)
                V.tensor_copy(table[:, n * 512:(n + 1) * 512], ps[0:H, 6 + n % 2, :]).then_inc(tab_cp, 1)
            dve.wait_ge(s_xt, 16)
            V.tensor_tensor(xT, xT, c("gmix").unsqueeze(2).to_broadcast([P, KT, NT]), ALU.mult).then_inc(xt_scaled, 1)
            dve.wait_ge(rows_out, 16 * NQ)
            for n in range(H // 2):
                dve.wait_ge(flip_mm, n + 1)
                V.tensor_copy(bias_p[:, 2 * n:2 * n + 2, :], ps[:, 6 + n % 2, :].rearrange("p (h n) -> p h n", h=2)).then_inc(flip_used, 1)

            state = {"n": 1}

            def norm(src, groups, e, gain, scratch, need):
                dve.wait_ge(z_ready, need)
                link(V.tensor_tensor(scratch, src, src, ALU.mult))
                link(V.tensor_reduce(st_n[:, 0:groups], scratch.rearrange("p n (h e) -> p (n h) e", e=e), X, ALU.add))
                V.tensor_scalar(st_n[:, 0:groups], st_n[:, 0:groups], 1.0 / e, EPS, ALU.mult, ALU.add).then_inc(ms_ready, 1)
                state["n"] += 1
                dve.wait_ge(rs_ready, state["n"])
                n = src.shape[1]
                for k in range(n):
                    v = src[:, k].rearrange("p (h e) -> p h e", e=e)
                    hh = COLS // e
                    rb = st_nr[:, k * hh:(k + 1) * hh].unsqueeze(2).to_broadcast([P, hh, e])
                    last = V.tensor_tensor(v, v, rb, ALU.mult)
                link(last)
                for k in range(n):
                    v = src[:, k].rearrange("p (h e) -> p h e", e=e)
                    hh = COLS // e
                    if gain[1] == COLS:
                        gb = gv[:, gain[0]:gain[0] + gain[1]].rearrange("p (h e) -> p h e", e=e)
                    else:
                        gb = gv[:, gain[0]:gain[0] + gain[1]].unsqueeze(1).to_broadcast([P, hh, e])
                    last = V.tensor_tensor(v, v, gb, ALU.mult)
                last.then_inc(normed, 1)

            def flat(ap):
                return ap.rearrange("p a t e -> p (a t) e")

            dve.wait_ge(s_gv, 16)
            dve.wait_ge(po, 2)
            dve.wait_ge(gemm_done, 4)
            norm(mk, 8, DG, GV["km"], area(A_Y, 2, COLS), 4)
            norm(flat(z[:, C_Q:C_Q + 2]), 48, DH, GV["qb"], area(A_Y, 6, COLS), 4 + 3 * 2)
            norm(flat(z[:, C_K:C_K + 2]), 48, DH, GV["kb"], area(A_Y, 6, COLS), 4 + 3 * 4)
            norm(flat(z[:, C_QM:C_QM + 1]), 12, DG, GV["qm"], area(A_Y, 3, COLS), 4 + 3 * 5)
            dve.wait_ge(gelu_done, 1)
            norm(flat(z[:, C_VA:C_VA + 1]), 12, DG, GV["av"], area(A_Y, 3, COLS), 4 + 3 * 9)

            def memory_pad(r):
                if r:
                    dve.wait_ge(msc_mm, r)
                V.tensor_copy(qmpad.rearrange("p (b h s) -> p b h s", b=4, h=4)[:, :, :, 0:8],
                              qmT[:, :, NPROMPT + 32 * r:NPROMPT + 32 * r + 32].rearrange("p h (b q) -> p b h q", b=4)
                              ).then_inc(pad_ready, 1)

            def memory_max(r):
                dve.wait_ge(msc_mm, r + 1)
                link(V.tensor_reduce(st_m[:, 8 + r:9 + r], ps[:, 6, 256 * r:256 * r + 256], X, ALU.max))
                V.tensor_scalar(st_m[:, 6 + r:7 + r], st_m[:, 8 + r:9 + r], -S_MEM, None, ALU.mult).then_inc(mmx, 1)

            def memory_mask(r):
                dve.wait_ge(mexp, r + 1)
                link(V.reciprocal(st_r[:, 6 + r:7 + r], st_l[:, 6 + r:7 + r]))
                dve.wait_ge(mpv_mm, r + 1)
                V.scalar_tensor_tensor(y_m, ps[:, 6, :], st_r[:, 6 + r:7 + r], c("mmask"), ALU.mult, ALU.mult).then_inc(m_masked, 1)

            def memory_out(r):
                dve.wait_ge(mfold_mm, r + 1)
                V.tensor_copy(yT[:, 12:16, NPROMPT + 32 * r:NPROMPT + 32 * r + 32],
                              ps[:, 7, 0:128].rearrange("p (h n) -> p h n", h=4)).then_inc(my_ready, 1)

            def gate(g):
                cols = slice(g * DG, (g + 1) * DG)
                dve.wait_ge(gate_mm, g + 1)
                V.scalar_tensor_tensor(z[:, C_U, 0:2, cols], ps[:, 6, 0:256].rearrange("p (t n) -> p t n", t=2),
                                       c("bs")[:, g:g + 1], z[:, C_U, 0:2, cols], ALU.add, ALU.mult)
                V.scalar_tensor_tensor(z[0:64, C_U, 2, cols], ps[0:64, 6, 256:384],
                                       c("bss", 64)[:, g:g + 1], z[0:64, C_U, 2, cols], ALU.add, ALU.mult).then_inc(gated, 1)

            link(V.memset(qmpad, 0.0))
            between = {3: lambda: memory_pad(0), 4: lambda: (memory_max(0), memory_pad(1)), 6: lambda: memory_max(1),
                       8: lambda: memory_mask(0), 9: lambda: memory_out(0), 10: lambda: memory_mask(1), 11: lambda: memory_out(1),
                       12: lambda: gate(0), 13: lambda: gate(1), 14: lambda: gate(2), 15: lambda: gate(3)}
            for i in range(24):
                if i < 20:
                    b = i % 3
                    dve.wait_ge(sc_mm, i + 1)
                    if i == 2:
                        dve.wait_ge(st_mem, 32)
                    w0, w = (128, 384) if i < H else (256, 512)
                    if i < H:
                        V.scalar_tensor_tensor(sc_p[b][:, 0:128], ps[:, i % 2, 0:128], S_WIN, bias_p[:, i, 128:256], ALU.mult, ALU.add)
                        last = V.scalar_tensor_tensor(sc_p[b][:, 128:384], ps[:, i % 2, 128:384], S_WIN, bias_p[:, i, :], ALU.mult, ALU.add)
                    else:
                        last = V.tensor_scalar(sc_p[b][:, :], ps[:, i % 2, :], S_MEM, None, ALU.mult)
                    last.then_inc(sc_read, 1)
                    dve.wait_ge(sc_read, i + 1)
                    V.tensor_reduce(st_m[:, 2 * b:2 * b + 1], sc_p[b][:, 0:w0], X, ALU.max, negate=True)
                    V.tensor_reduce(st_m[:, 2 * b + 1:2 * b + 2], sc_p[b][:, w0:w], X, ALU.max, negate=True).then_inc(mx_ready, 1)
                if i in between:
                    between[i]()
                if 1 <= i <= 20:
                    h = i - 1
                    b = h % 3
                    w0, w = (128, 384) if h < H else (256, 512)
                    dve.wait_ge(exp_done, h + 1)
                    link(V.reciprocal(st_r[:, 2 * b:2 * b + 2], st_l[:, 2 * b:2 * b + 2]))
                    V.tensor_scalar(sc_p[b][:, 0:w0], sc_p[b][:, 0:w0], st_r[:, 2 * b:2 * b + 1], None, ALU.mult)
                    V.tensor_scalar(sc_p[b][:, w0:w], sc_p[b][:, w0:w], st_r[:, 2 * b + 1:2 * b + 2], None, ALU.mult).then_inc(p_ready, 1)
                if i >= 4:
                    h = i - 4
                    dve.wait_ge(pv_mm, h + 1)
                    if h < H and h % 2 == 1:
                        V.tensor_copy(yT[:, 4 + h // 2, 0:256], ps[:, 4 + (h // 2) % 2, 0:256]).then_inc(y_used, 1)
                    if h >= H:
                        V.tensor_copy(yT[:, 12 + h - H, 0:256], ps[:, 4 + (h - H) % 2, 0:256]).then_inc(y_used, 1)
            V.memset(bias_s[:, PAST:PAST + 120], NEG).then_inc(dset, 1)
            dve.wait_ge(gate_tr, G)
            dve.wait_ge(st_va, 32)
            link(V.memset(qpad, 0.0))

            def pad_q(b):
                for j in range(2):
                    r = slice(64 * j, 64 * j + 64)
                    last = V.tensor_copy(qpad.rearrange("p (h s) -> p h s", s=144)[r, :, 8 * j:8 * j + 8],
                                         qT[r, :, ds(b * 8 + NPROMPT, 8)])
                last.then_inc(qpad_ready, 1)

            def mask(b):
                V.scalar_tensor_tensor(y_s, ps[:, 6, 0:256], st_r[:, 10:11], c("wmask"), ALU.mult, ALU.mult).then_inc(s_masked, 1)

            def y_out(b):
                V.tensor_copy(yT[:, 4:12, ds(b * 8 + NPROMPT, 8)].rearrange("p (g j) q -> p j g q", j=2),
                              ps[:, 7, 0:64].rearrange("p (j g q) -> p j g q", j=2, g=4)).then_inc(y_copied, 1)

            bB = bias_s[:, 0:1536].rearrange("p (m s) -> p m s", s=16)[:, :, 0:8]

            def soften(b):
                dve.wait_ge(s_mm, b * 3 + 1)
                V.scalar_tensor_tensor(sc_s[:, 0:512], ps[:, 0, :], S_WIN, bias_s[:, 1536:2048], ALU.mult, ALU.add).then_inc(s_used, 1)
                dve.wait_ge(s_mm, b * 3 + 2)
                V.scalar_tensor_tensor(sc_s[:, 512:1024].rearrange("p (m s) -> p m s", s=8), ps[:, 1, :].rearrange("p (m s) -> p m s", s=8),
                                       S_WIN, bB[:, 0:64], ALU.mult, ALU.add).then_inc(s_used, 1)
                dve.wait_ge(s_mm, b * 3 + 3)
                V.scalar_tensor_tensor(sc_s[:, 1024:1280].rearrange("p (m s) -> p m s", s=8), ps[:, 2, 0:256].rearrange("p (m s) -> p m s", s=8),
                                       S_WIN, bB[:, 64:96], ALU.mult, ALU.add)
                V.scalar_tensor_tensor(sc_s[:, 1280:1344], ps[:, 2, 256:320], S_WIN, bias_s[:, ds(b * -8 + (PAST + 56), NSAMPLE)],
                                       ALU.mult, ALU.add).then_inc(s_used, 1)
                dve.wait_ge(s_used, b * 3 + 3)
                V.tensor_reduce(st_m[:, 10:11], sc_s, X, ALU.max, negate=True).then_inc(smx, 1)
                dve.wait_ge(sexp, b + 1)
                V.reciprocal(st_r[:, 10:11], st_l[:, 10:11]).then_inc(srec, 1)

            dve.sem_inc(s_masked, 1)
            pad_q(0)
            dve.wait_ge(bs_loaded, 32)
            soften(0)
            with dve.Fori(1, NBATCH) as b:
                dve.wait_ge(s_mm, b * 3)
                pad_q(b)
                dve.wait_ge(srec, b)
                dve.wait_ge(spv_mm, b)
                mask(b - 1)
                soften(b)
                dve.wait_ge(fold_mm, b)
                y_out(b - 1)
            dve.wait_ge(srec, NBATCH)
            dve.wait_ge(spv_mm, NBATCH)
            mask(NBATCH - 1)
            dve.wait_ge(fold_mm, NBATCH)
            y_out(NBATCH - 1)
            dve.wait_ge(x_again, 64)
            for ch in range(4):
                for t, (_, m) in enumerate(ROWS):
                    dve.wait_ge(wo_done, 3 * ch + t + 1)
                    for j in range(P // m):
                        w = COLS * m // P
                        hh = hres[0:m, t, ch * 512 + w * j:ch * 512 + w * j + w]
                        last = V.tensor_tensor(hh, ps[m * j:m * j + m, 3 * (ch % 2) + t, 0:w], hh, ALU.add)
                    last.then_inc(h_ready, 1)
                for t, (_, m) in enumerate(ROWS):
                    dve.wait_ge(h_ready, 3 * ch + t + 1)
                    cols = slice(ch * COLS, (ch + 1) * COLS)
                    V.tensor_tensor(n2[0:m, t, cols], hres[0:m, t, cols], gff[0:m, cols], ALU.mult).then_inc(g_ready, 1)
            dve.wait_ge(sumsq, 5 + 12)
            link(V.tensor_reduce(st_h, st_hq.rearrange("p (c t) -> p t c", t=3), X, ALU.add))
            V.tensor_scalar(st_h, st_h, 1.0 / D, EPS, ALU.mult, ALU.add).then_inc(ms_ready, 1)
            state["n"] += 1

            iota = c("iota")
            link(V.memset(area(R0, 120), -3e38))
            link(V.memset(moh[64:128, :, 2, :], 0.0))
            link(V.memset(zer, 0.0))
            link(V.tensor_copy(pair_u, c("pairs").rearrange("p (k t f) -> p k t f", k=2, t=3)))
            link(V.tensor_copy(eblk_i[:, 0:NEXP], iota[:, 0:NEXP]))
            dve.wait_ge(rs_ready, state["n"])
            dve.wait_ge(logits, 1)
            for t, (_, m) in enumerate(ROWS):
                lg = ps[0:m, 6, t * 36:(t + 1) * 36]
                V.tensor_scalar(g8[0:m, t, 0:4], lg[:, 0:4], st_hr[0:m, t:t + 1], None, ALU.mult)
                last = V.tensor_scalar(el[0:m, t, :], lg[:, 4:36], st_hr[0:m, t:t + 1], None, ALU.mult)
            link(last)
            for t in range(3):
                link(V.max(mx[:, t, :], g8[:, t, :]))
                link(V.max_index(mi[:, t, :], mx[:, t, :], g8[:, t, :]))
            link(V.tensor_copy(grp, mi[:, :, 0:1]))
            link(V.tensor_tensor(goh, iota[:, 0:4].unsqueeze(1).to_broadcast([P, 3, 4]), grp.to_broadcast([P, 3, 4]), ALU.is_equal))
            link(V.tensor_tensor(prod, el.rearrange("p t (g e) -> p t g e", g=4), goh.unsqueeze(3).to_broadcast([P, 3, 4, 8]), ALU.mult))
            link(V.tensor_reduce(esel, prod.rearrange("p t g e -> p t e g"), X, ALU.add))
            for t in range(3):
                link(V.max(top[:, t, :], esel[:, t, :]))
                link(V.max_index(ti[:, t, :], top[:, t, :], esel[:, t, :]))
            link(V.tensor_copy(tif, ti[:, :, 0:2]))
            link(V.scalar_tensor_tensor(eid, grp.to_broadcast([P, 3, 2]), float(EPG), tif, ALU.mult, ALU.add))
            for k in range(2):
                for t, m in ((slice(0, 2), P), (slice(2, 3), 64)):
                    last = V.tensor_tensor(moh[0:m, k, t], iota[0:m, 0:32].unsqueeze(1).to_broadcast([m, t.stop - t.start, 32]),
                                           eid[0:m, t, k:k + 1].to_broadcast([m, t.stop - t.start, 32]), ALU.is_equal)
            link(last)
            V.tensor_tensor(asum, moh[:, 0], moh[:, 1], ALU.add).then_inc(onehots, 1)
            V.tensor_tensor(dd, top[:, :, 1:2], top[:, :, 0:1], ALU.subtract).then_inc(route_d, 1)
            dve.wait_ge(route_e, 1)
            link(V.tensor_scalar(w1p, dd, 1.0, None, ALU.add))
            link(V.reciprocal(wk[:, 0], w1p))
            link(V.tensor_tensor(wk[:, 1], dd, wk[:, 0], ALU.mult))
            dve.wait_ge(ranks, 1)
            link(V.tensor_copy(nb, ps[:, 3, 96:128]))
            link(V.tensor_tensor(cmp4, nb.unsqueeze(2).to_broadcast([P, 32, 4]),
                                 c("thr")[:, 0:4].unsqueeze(1).to_broadcast([P, 32, 4]), ALU.is_gt))
            link(V.tensor_reduce(nb, cmp4, X, ALU.add))
            link(V.tensor_tensor_scan(incl, nb, zer, 0.0, ALU.add, ALU.add))
            link(V.tensor_tensor(base, incl, nb, ALU.subtract))
            for k in range(2):
                link(V.tensor_tensor(pick, moh[:, k], ps[:, 3, 0:96].rearrange("p (t e) -> p t e", t=3), ALU.mult))
                link(V.tensor_reduce(rankf[:, k], pick, X, ALU.add))
                link(V.tensor_tensor(pick, moh[:, k], base.unsqueeze(1).to_broadcast([P, 3, 32]), ALU.mult))
                link(V.tensor_reduce(basef[:, k], pick, X, ALU.add))
            link(V.tensor_tensor(ge4, rankf.unsqueeze(3).to_broadcast([P, 2, 3, 4]),
                                 c("thr")[:, 0:4].unsqueeze(1).unsqueeze(1).to_broadcast([P, 2, 3, 4]), ALU.is_ge))
            link(V.tensor_reduce(fullf, ge4, X, ALU.add))
            own = eid.rearrange("p t k -> p k t")
            link(V.scalar_tensor_tensor(slotf, basef, float(NEXP - 1), fullf, ALU.add, ALU.add))
            link(V.tensor_tensor(slotf, slotf, own, ALU.subtract))
            link(V.tensor_tensor(slotf, slotf, ge4[:, :, :, 0], ALU.mult))
            link(V.tensor_tensor(slotf, slotf, own, ALU.add))
            link(V.scalar_tensor_tensor(slotf, rankf, float(NTAB), slotf, ALU.mult, ALU.add))
            link(V.scalar_tensor_tensor(slotf, fullf, float(-BLOCK * NTAB), slotf, ALU.mult, ALU.add))
            V.tensor_copy(slot_u, slotf).then_inc(slots_ready, 1)
            link(V.tensor_tensor(cmpb, incl.unsqueeze(1).to_broadcast([P, NMORE, 32]),
                                 iota[:, 0:NMORE].unsqueeze(2).to_broadcast([P, NMORE, 32]), ALU.is_le))
            link(V.tensor_reduce(ebf, cmpb, X, ALU.add))
            link(V.tensor_scalar(ebf, ebf, float(NEXP - 1), None, ALU.min))
            link(V.tensor_copy(eblk_i[:, NEXP:NBLK], ebf))
            link(V.tensor_scalar(cntf[:, 0:1], incl[:, 31:32], 1.0 / UNROLL, NEXP // UNROLL + 0.5 - 0.5 / UNROLL, ALU.mult, ALU.add))
            V.tensor_copy(cnt_i[:, 0:1], cntf[:, 0:1]).then_inc(routed, 1)
            dve.wait_ge(routed, 1)
            V.memset(xg[0:BLOCK], 0.0).then_inc(dset, 1)

            steps = dve.value_load(cnt_i[0:1, 0:1], min_val=NEXP // UNROLL, max_val=NBLK // UNROLL)
            dve.wait_ge(xg_tr, 1)
            V.tensor_copy(xgT[:, 0:8], ps[:, 1, :].rearrange("p (k n) -> p k n", k=8)).then_inc(xgT_ready, 1)
            with dve.Fori(0, steps) as i:
                for s in range(UNROLL):
                    dve.wait_ge(gu_mm, i * UNROLL + s + 1)
                    V.tensor_copy(gu_sb, ps[:, 0, 0:FF]).then_inc(gu_copied, 1)
                    dve.wait_ge(xg_tr, i * UNROLL + s + 2)
                    V.tensor_copy(xgT[:, 0:8], ps[:, 1, :].rearrange("p (k n) -> p k n", k=8)).then_inc(xgT_ready, 1)
                    dve.wait_ge(silu_done, i * UNROLL + s + 1)
                    V.tensor_tensor(actT, sg, ps[:, 3, 0:256].rearrange("p (j n) -> p j n", j=2)[:, :, BLOCK:2 * BLOCK],
                                    ALU.mult).then_inc(act_ready, 1)
                    dve.wait_ge(dn_mm, i * UNROLL + s + 1)
                    dve.wait_ge(y_free, i * UNROLL + s + 1)
                    V.tensor_copy(y_sb[:, s % 2, 0:512], ps[:, 4 + 2 * (s % 2), :]).then_inc(y_ready, 1)
            for t, (_, m) in enumerate(ROWS):
                for k in range(2):
                    dve.wait_ge(back[t][k], 16)
                    last = V.scalar_tensor_tensor(hres[0:m, t], yg[0:m, k, t], wk[0:m, k, t], hres[0:m, t], ALU.mult, ALU.add)
                    if k == 0:
                        last.then_inc(moe_dv, 1)
                        dve.wait_ge(moe_dv, t + 1)
                last.then_inc(final, 1)

        @block.gpsimd
        def _(pool):
            g = nc.gpsimd
            pool.dma_start(relb[:, :], relb_d).then_inc(s_relb, 16)
            pool.dma_start(onehot[:, :], onehot_d).then_inc(s_relb, 16)
            g.memset(nhalf[:, :], -0.5).then_inc(po, 1)
            pool.dma_start(tab_d, empty_d).then_inc(tab_zero, 16)
            pool.wait_ge(tab_cp, TABLE // 512)
            pool.dma_start(bias_d, table[:, :]).then_inc(tab_out, 16)
            for q in range(NQ):
                pool.dma_start(bias_q_d.rearrange("(h q) n -> h q n", q=NQ)[:, q, :],
                               table[:, DIST0 - PAST - q:DIST0 - q + NQ]).then_inc(rows_out, 16)
            def rsqrt(n, out, in_):
                pool.wait_ge(ms_ready, n)
                g.tensor_tensor(out, in_, nhalf[:, 0:in_.shape[1]], ALU.pow).then_inc(rs_ready, 1)
            pool.wait_ge(po, 1)
            rsqrt(1, st_rs[:, 0:5], stat[:, 0:5])
            pool.wait_ge(rs_ready, 1)
            pool.wait_ge(flip_mm, H // 2)
            g.memset(z[64:128, :, 2, :], 0.0).then_inc(po, 1)
            pool.wait_ge(z_ready, 4)
            pool.dma_start(o_mv.rearrange("(t p) n -> p t n", p=P), mv).then_inc(st_mem, 16)
            rsqrt(2, st_nr[:, 0:8], st_n[:, 0:8])
            pool.wait_ge(normed, 1)
            pool.dma_start(o_mk.rearrange("(t p) n -> p t n", p=P), mk).then_inc(st_mem, 16)
            rsqrt(3, st_nr[:, 0:48], st_n[:, 0:48])
            rsqrt(4, st_nr[:, 0:48], st_n[:, 0:48])
            pool.wait_ge(normed, 3)

            for a in range(2):
                pool.dma_start(o_k[0:256, a * 512:(a + 1) * 512].rearrange("(t p) n -> p t n", p=P), z[:, C_K + a, 0:2, :]).then_inc(st_k, 16)
            pool.dma_start(o_k[256:320, :].rearrange("p (a n) -> p a n", a=2), z[0:64, C_K:C_K + 2, 2, :]).then_inc(st_k, 16)
            rsqrt(5, st_nr[:, 0:12], st_n[:, 0:12])
            pool.wait_ge(z_ready, 4 + 3 * 7)
            for a in range(2):
                pool.dma_start(o_v[0:256, a * 512:(a + 1) * 512].rearrange("(t p) n -> p t n", p=P), z[:, C_V + a, 0:2, :]).then_inc(st_v, 16)
            pool.dma_start(o_v[256:320, :].rearrange("p (a n) -> p a n", a=2), z[0:64, C_V:C_V + 2, 2, :]).then_inc(st_v, 16)
            rsqrt(6, st_nr[:, 0:12], st_n[:, 0:12])
            pool.wait_ge(normed, 5)
            pool.dma_start(o_va[0:128, :], z[:, C_VA, 1, :]).then_inc(st_va, 16)
            pool.dma_start(o_va[128:192, :], z[0:64, C_VA, 2, :]).then_inc(st_va, 16)
            rsqrt(7, st_hr[:, 0:3], st_h[:, 0:3])
            pool.wait_ge(slots_ready, 1)
            pool.wait_ge(tab_zero, 16)
            for k in range(2):
                for t, (_, m) in enumerate(ROWS):
                    pool.indirect_dma_start(tab_d, bass.IndirectOffsetOnAxis(ap=slot_u[0:m, k, t:t + 1], axis=0),
                                            pair_u[0:m, k, t, :], None).then_inc(slots_out, 16)
            pool.wait_ge(slots_out, 16 * 6)
            pool.wait_ge(n2_stored, 48)
            pool.wait_ge(st_mem, 32)
            pool.wait_ge(st_k, 48)
            pool.wait_ge(st_v, 48)
            pool.wait_ge(st_va, 32)
            for half in range(2):
                pool.dma_start(idx_all[64 * half:64 * half + 64], tab_d.rearrange("(p n) f -> p n f", p=BLOCK)).then_inc(idx_in, 16)
            pool.wait_ge(idx_in, 32)
            for s in range(2):
                g.tensor_copy(row_cur[s], idx_all[0:BLOCK, s, 0:1]).then_inc(idx_cp, 1)
            g.tensor_scalar(idx_all[64:128, :, 1], idx_all[64:128, :, 1], 1.0, None, ALU.add).then_inc(idx_cp, 1)
            pool.wait_ge(idx_cp, 3)
            pool.wait_ge(dset, 3)
            for s in range(2):
                pool.indirect_dma_start(xg[0:BLOCK, s, :], None, n2_d, bass.IndirectOffsetOnAxis(ap=row_cur[s], axis=0),
                                        bounds_check=NT - 1, oob_is_err=False).then_inc(gathered[s], 16)
            pool.wait_ge(routed, 1)
            steps = pool.value_load(cnt_i[0:1, 0:1], min_val=NEXP // UNROLL, max_val=NBLK // UNROLL)
            g.sem_inc(y_free, 2)
            with pool.Fori(0, steps) as i:
                for s in range(UNROLL):
                    r = s % 2
                    pool.wait_ge(xg_tr, i * UNROLL + s + 1)
                    pool.wait_ge(gathered[r], i * (8 * UNROLL) + 16 * (s // 2 + 1))
                    g.tensor_copy(row_cur[r], idx_all[0:BLOCK, ds(i * UNROLL + s + 2, 1), 0]).then_inc(idx_cp, 1)
                    g.tensor_copy(dst_cur[r], idx_all[:, ds(i * UNROLL + s, 1), 1]).then_inc(idx_cp, 1)
                    pool.wait_ge(idx_cp, i * (2 * UNROLL) + (2 * s + 5))
                    g.sem_inc(pool_seen, 1)
                    pool.indirect_dma_start(xg[0:BLOCK, r, :], None, n2_d, bass.IndirectOffsetOnAxis(ap=row_cur[r], axis=0),
                                            bounds_check=NT - 1, oob_is_err=False).then_inc(gathered[r], 16)
                    pool.wait_ge(y_ready, i * (2 * UNROLL) + 2 * (s + 1))
                    g.sem_inc(pool_seen, 1)
                    pool.indirect_dma_start(y_d, bass.IndirectOffsetOnAxis(ap=dst_cur[r], axis=0), y_sb[:, r, :], None,
                                            bounds_check=4 * NT - 1, oob_is_err=False).then_inc(y_stored[r], 16)
                    pool.wait_ge(y_stored[r], i * (8 * UNROLL) + 16 * (s // 2 + 1))
                    g.sem_inc(y_free, 1)
            for r in range(2):
                pool.wait_ge(gathered[r], steps * (8 * UNROLL) + 16)
            pool.wait_ge(dn_mm, steps * UNROLL)
            g.sem_inc(pool_seen, 1)
            for t, (r0, m) in enumerate(ROWS):
                for k in range(2):
                    pool.dma_start(yg[0:m, k, t, :].rearrange("p (a n) -> p a n", a=2),
                                   y_d[2 * (k * NT + r0):2 * (k * NT + r0 + m), :].rearrange("(p a) n -> p a n", a=2)).then_inc(back[t][k], 16)
            for t, (r0, m) in enumerate(ROWS):
                pool.wait_ge(final, t + 1)
                pool.dma_start(o_y[r0:r0 + m, :], hres[0:m, t]).then_inc(y_stored_out, 16)
            pool.wait_ge(y_stored_out, 48)


def distance_bucket(dist):
    d = np.maximum(dist, 0)
    exact = 16
    df = np.maximum(d, 1).astype(np.float32)
    large = exact + (np.log(df / np.float32(exact)) / np.float32(math.log(2048 / exact)) * np.float32(16)).astype(np.int32)
    return np.where(d < exact, d, np.minimum(large, 31))


def constants():
    dist = DIST0 - np.arange(TABLE)
    count = sum(((dist >= 0) & (dist <= w) & (dist % dl == 0)).astype(int) for w, dl in ((128, 1), (512, 4), (2048, 16)))
    onehot = np.zeros((33, TABLE), np.float32)
    onehot[distance_bucket(dist), np.arange(TABLE)] = 1
    onehot[32] = np.where(count > 0, np.log(np.maximum(count, 1)), NEG)
    c = {n: np.zeros((P, w), np.float32) for n, (_, w) in CST.items()}
    c["ident"][:] = np.eye(P)
    c["flip"][:] = np.eye(P)[::-1]
    c["ones"][:] = 1
    c["ltri"][:] = np.triu(np.ones((P, P)), 1)
    c["iota"][:] = np.arange(64)
    h, q = np.divmod(np.arange(P), NQ)
    c["wmask"][:] = (h % 4)[:, None] == np.arange(256) // DH
    c["wsel"][:] = h[:, None] // 4 * NQ + q[:, None] == np.arange(32)
    b, h = h // G, h % G
    c["mmask"][:] = h[:, None] == np.arange(512) // DG
    c["msel"][:] = b[:, None] * NQ + q[:, None] == np.arange(32)
    c["thr"][:, 0:4] = np.arange(1, 5) * BLOCK
    tok = np.arange(P)[:, None] + np.array([r0 for r0, _ in ROWS])
    c["pairs"][:] = np.stack([np.stack([tok, 2 * (k * NT + tok)], axis=-1) for k in range(2)], axis=1).reshape(P, 12)
    return onehot, c


def kernel(**inputs):
    import concourse.bacc as _bacc
    from concourse.bass_utils import run_bass_kernel_spmd as _run

    a = {k: np.asarray(v) for k, v in inputs.items()}
    onehot, c = constants()
    x = np.concatenate([a["x_prompt"].reshape(NPROMPT, D), a["x_sample"].reshape(NSAMPLE, D)])
    mem = a["mem_prompt"].reshape(NMEM, D)

    def columns(t):
        return np.ascontiguousarray(t.reshape(-1, KT, P).transpose(2, 1, 0))

    def chunks(w):
        return w.reshape(QTR, K4, P, COLS).transpose(0, 2, 1, 3).reshape(QTR, P, K4 * COLS)

    w_in, w_kv, w_out = a["w_in"][0], a["w_mem_kv"][0], a["w_out"][0]
    starts = [1024, 1536, 2048, 2560, 4096, 3072, 3584, 0, 512]
    w_proj = np.stack([chunks(w_kv[:, 0:512]), chunks(w_kv[:, 512:1024])] + [chunks(w_in[:, s:s + 512]) for s in starts])
    w_o = np.stack([chunks(w_out[:, n * 512:(n + 1) * 512]) for n in range(4)])

    def reached(cache):
        late = cache[:, PAST - KEYS_A:]
        early = cache[:, 0:PAST - KEYS_A].reshape(NBATCH, 96, 16, H, DH)[:, :, 0:8].reshape(NBATCH, KEYS_B, H, DH)
        return np.concatenate([late, early], axis=1)

    k = reached(a["cache_win_k"][0]).reshape(NBATCH, KEYS, HP, 128).transpose(0, 3, 2, 1)
    kc = np.concatenate([k[..., s:e].reshape(NBATCH, P, -1) for s, e in ((0, 512), (512, 1024), (1024, 1280))], axis=2)
    v = reached(a["cache_win_v"][0]).reshape(NBATCH, VT, P, H * DH).transpose(0, 2, 1, 3)
    vc = np.ascontiguousarray(v).reshape(NBATCH, P, VT * 1024)
    mkc = a["cache_mem_k"][0].reshape(2, 4, NMEM, G, DG).transpose(4, 0, 1, 3, 2).reshape(P, 2, 16, NMEM)
    mvc = a["cache_mem_v"][0].reshape(2, 4, 2, P, G * DG).transpose(3, 0, 1, 2, 4)

    c["gmix"][:] = a["g_mix"][0].reshape(KT, P).T
    c["gmem"][:] = a["g_mem"][0].reshape(KT, P).T
    c["bs"][:] = a["b_s"][0].T
    c["bss"][0:NSAMPLE] = np.tile(a["b_s"][0][:, 0:NQ].T, (NBATCH, 1))
    wr = np.concatenate([a["w_router_group"][0]] + [a["w_router_expert"][0, g] for g in range(NGRP)], axis=1)
    c["wr"][:] = wr.reshape(KT, P, 36).transpose(1, 0, 2).reshape(P, -1)
    wst = np.zeros((P, G, P), np.float32)
    wsbd = np.zeros((P, G, NSAMPLE), np.float32)
    for t in range(P):
        wst[0:t + 1, :, t] = a["w_s"][0][:, t, 0:t + 1].T
    for b in range(NBATCH):
        wsbd[b * NQ:(b + 1) * NQ, :, b * NQ:(b + 1) * NQ] = wst[0:NQ, :, 0:NQ]
    c["wst"][:] = wst.reshape(P, -1)
    c["wsbd"][:] = wsbd.reshape(P, -1)
    gv = np.concatenate([a["g_qb"][0], a["g_kb"][0], a["g_qm"][0], a["g_km"][0], a["g_av"][0].reshape(-1)])
    relb = np.concatenate([a["rel_bias"], np.ones((1, H), np.float32)])
    w_gu = np.stack([a["w_gate"][0], a["w_up"][0]], axis=1).reshape(NEXP, 2, KT, P, FF).transpose(0, 3, 1, 2, 4)
    w_dn = a["w_down"][0].reshape(NEXP, 2, P, D).transpose(0, 2, 1, 3)

    ins = {
        "x_rows": x, "mem_rows": mem, "x_t": columns(x), "mem_t": columns(mem), "w_proj": w_proj, "w_o": w_o,
        "kc": kc, "vc": vc, "mkc": mkc, "mvc": mvc, "cst_d": np.concatenate([c[n] for n in CST], axis=1),
        "gv_d": gv, "gffn_d": a["g_ffn"][0], "relb_d": relb, "onehot_d": onehot, "w_gu": w_gu, "w_dn": w_dn,
        "empty_d": np.tile(np.array([[NT, 4 * NT]], np.uint32), (NTAB * BLOCK, 1)),
    }
    outs = {"o_y": (NT, D), "o_k": (NT, 1024), "o_v": (NT, 1024), "o_va": (192, 512), "o_mk": (NMEM, 512), "o_mv": (NMEM, 512)}
    scratch = {"bias_d": ((H, TABLE), F32), "bias_q_d": ((P, PAST + NQ), F32), "n2_d": ((NT, D), F32), "tab_d": ((NTAB * BLOCK, 2), U32), "y_d": ((4 * NT, D // 2), F32)}

    nc = _bacc.Bacc("TRN2", target_bir_lowering=False, num_devices=1)
    arrays, args = {}, []
    for name, v in ins.items():
        arrays[name] = np.ascontiguousarray(v)
        args.append(nc.dram_tensor(name, arrays[name].shape, mybir.dt.from_np(arrays[name].dtype), kind="ExternalInput").ap())
    for name, shape in outs.items():
        args.append(nc.dram_tensor(name, shape, F32, kind="ExternalOutput").ap())
    for name, (shape, dt) in scratch.items():
        args.append(nc.dram_tensor(name, shape, dt, kind="Internal").ap())
    hybrid_step(nc, *args)
    r = _run(nc, [arrays], core_ids=[0]).results[0]

    y, k, v, va = r["o_y"], r["o_k"], r["o_v"], r["o_va"]
    return (y[0:256].reshape(1, 256, D), y[256:].reshape(NBATCH, NQ, D),
            k[0:256].reshape(1, 1, 256, H, DH), v[0:256].reshape(1, 1, 256, H, DH),
            va[0:128].reshape(1, 1, 128, G, DG), r["o_mk"].reshape(1, 1, NMEM, G, DG), r["o_mv"].reshape(1, 1, NMEM, G, DG),
            k[256:].reshape(1, NBATCH, NQ, H, DH), v[256:].reshape(1, NBATCH, NQ, H, DH),
            va[128:].reshape(1, NBATCH, NQ, G, DG))
```
